# Optimizing a Trainium2 kernel written in Bass

```python
import math
import jax, jax.numpy as jnp
from jax import lax
import numpy as np

D_MODEL = 1024
BATCH = 1
SEQ = 256
DEPTH = 1

LRU_WIDTH = 1024
LRU_HEADS = 16
LRU_HEAD_DIM = LRU_WIDTH // LRU_HEADS
LRU_CONV = 4
LRU_C = 8.0
HYENA_WIDTH = 1024
HYENA_ORDER = 2
HYENA_CONV = 3
FILTER_EMB = 33
FILTER_BANDS = (FILTER_EMB - 1) // 2
FILTER_HIDDEN = 64
DECAY_FAST = 0.3
DECAY_SLOW = 1.5
DECAY_TARGET = 1e-2
N_BRANCHES = 2
IN_COLS = 2 * LRU_WIDTH + (HYENA_ORDER + 1) * HYENA_WIDTH + N_BRANCHES * D_MODEL
N_EXPERTS = 16
CAPACITY_FACTOR = 2
D_FF_EXPERT = 2 * D_MODEL
EPS = 1e-6


def rmsnorm(x, g):
    xf = x.astype(jnp.float32)
    y = xf * lax.rsqrt(jnp.mean(xf * xf, axis=-1, keepdims=True) + EPS)
    return (y * g.astype(jnp.float32)).astype(x.dtype)

def dwconv(x, w, b, pad):
    C = x.shape[-1]
    y = lax.conv_general_dilated(x, w[:, None, :].astype(x.dtype), window_strides=(1,), padding=[pad],
                                 dimension_numbers=("NWC", "WIO", "NWC"), feature_group_count=C)
    return y + b.astype(x.dtype)

def rg_lru(xa, w_r, b_r, w_i, b_i, lam, reverse):
    B, S, W = xa.shape
    xh = xa.reshape(B, S, LRU_HEADS, LRU_HEAD_DIM)
    r = jax.nn.sigmoid(jnp.einsum('bshi,hij->bshj', xh, w_r.astype(jnp.float32)).reshape(B, S, W) + b_r.astype(jnp.float32))
    i = jax.nn.sigmoid(jnp.einsum('bshi,hij->bshj', xh, w_i.astype(jnp.float32)).reshape(B, S, W) + b_i.astype(jnp.float32))
    log_a = -LRU_C * r * jax.nn.softplus(-lam.astype(jnp.float32))
    a = jnp.exp(log_a)
    mult = jnp.sqrt(jnp.maximum(1.0 - jnp.exp(2.0 * log_a), 0.0))
    pos = jnp.arange(S)[None, :, None]
    start = S - 1 if reverse else 0
    mult = jnp.where(pos == start, 1.0, mult)
    bx = mult * (i * xa)

    def combine(e1, e2):
        a1, b1 = e1
        a2, b2 = e2
        return a1 * a2, a2 * b1 + b2

    _, h = lax.associative_scan(combine, (a, bx), axis=1, reverse=reverse)
    return h

def hyena_filters(L, w1, b1, w2, b2, w3, freq):
    f32 = jnp.float32
    t = jnp.linspace(0.0, 1.0, L, dtype=f32)[:, None]
    w = (2.0 * math.pi / L) * jnp.arange(L, dtype=f32)[:, None]
    f = jnp.linspace(1e-4, FILTER_BANDS - 1, FILTER_BANDS, dtype=f32)[None, :]
    z = jnp.concatenate([t, jnp.cos(w * f), -jnp.sin(w * f)], axis=-1)
    freq = freq.astype(f32)
    h = jnp.sin(freq[0] * (z @ w1.astype(f32) + b1.astype(f32)))
    h = jnp.sin(freq[1] * (h @ w2.astype(f32) + b2.astype(f32)))
    h = (h @ w3.astype(f32)).reshape(L, HYENA_ORDER, 2, HYENA_WIDTH)
    min_decay = math.log(DECAY_TARGET) / DECAY_SLOW
    max_decay = math.log(DECAY_TARGET) / DECAY_FAST
    deltas = jnp.abs(jnp.linspace(min_decay, max_decay, HYENA_WIDTH, dtype=f32))
    decay = jnp.exp(-t * deltas[None, :])
    return h * decay[:, None, None, :]

def bidir_kernel(hf, hb):
    zero = jnp.zeros((1, hf.shape[1]), hf.dtype)
    return jnp.concatenate([hf, zero, hb[:0:-1]], axis=0)

def fftconv(u, k, bias):
    L = u.shape[1]
    U = jnp.fft.rfft(u, n=2 * L, axis=1)
    K = jnp.fft.rfft(k, axis=0)
    y = jnp.fft.irfft(U * K[None], n=2 * L, axis=1)[:, :L]
    return y + u * bias.astype(jnp.float32)

def first_inputs(seed: int = 0) -> dict:
    key = jax.random.key(seed)
    ks = jax.random.split(key, 32)
    f32 = jnp.float32
    nrm = lambda k, shape, s: (jax.random.normal(k, shape, f32) * s).astype(f32)
    Dp = DEPTH
    u = jax.random.uniform(ks[9], (Dp, 2, LRU_WIDTH), f32, 0.9, 0.999)
    a0 = u ** (1.0 / LRU_C)
    lam = jnp.log(a0) - jnp.log1p(-a0)
    return {
        "x": nrm(ks[0], (BATCH, SEQ, D_MODEL), 1.0),
        "g_mix": 1.0 + nrm(ks[1], (Dp, D_MODEL), 0.01),
        "w_in": nrm(ks[2], (Dp, D_MODEL, IN_COLS), D_MODEL ** -0.5),
        "conv_a_w": nrm(ks[3], (Dp, LRU_CONV, LRU_WIDTH), LRU_CONV ** -0.5),
        "conv_a_b": nrm(ks[4], (Dp, LRU_WIDTH), 0.01),
        "lru_w_r": nrm(ks[5], (Dp, 2, LRU_HEADS, LRU_HEAD_DIM, LRU_HEAD_DIM), LRU_HEAD_DIM ** -0.5),
        "lru_b_r": nrm(ks[6], (Dp, 2, LRU_WIDTH), 0.01),
        "lru_w_i": nrm(ks[7], (Dp, 2, LRU_HEADS, LRU_HEAD_DIM, LRU_HEAD_DIM), LRU_HEAD_DIM ** -0.5),
        "lru_b_i": nrm(ks[8], (Dp, 2, LRU_WIDTH), 0.01),
        "lru_lambda": lam,
        "w_a_out": nrm(ks[10], (Dp, LRU_WIDTH, D_MODEL), LRU_WIDTH ** -0.5),
        "conv_b_w": nrm(ks[11], (Dp, HYENA_CONV, (HYENA_ORDER + 1) * HYENA_WIDTH), HYENA_CONV ** -0.5),
        "conv_b_b": nrm(ks[12], (Dp, (HYENA_ORDER + 1) * HYENA_WIDTH), 0.01),
        "filt_w1": nrm(ks[13], (Dp, FILTER_EMB, FILTER_HIDDEN), FILTER_EMB ** -0.5),
        "filt_b1": nrm(ks[14], (Dp, FILTER_HIDDEN), 0.1),
        "filt_w2": nrm(ks[15], (Dp, FILTER_HIDDEN, FILTER_HIDDEN), FILTER_HIDDEN ** -0.5),
        "filt_b2": nrm(ks[16], (Dp, FILTER_HIDDEN), 0.1),
        "filt_w3": nrm(ks[17], (Dp, FILTER_HIDDEN, HYENA_ORDER * 2 * HYENA_WIDTH), 0.005),
        "filt_freq": 1.0 + nrm(ks[18], (Dp, 2, FILTER_HIDDEN), 0.01),
        "filt_bias": nrm(ks[19], (Dp, HYENA_ORDER, HYENA_WIDTH), 0.5),
        "w_b_out": nrm(ks[20], (Dp, HYENA_WIDTH, D_MODEL), HYENA_WIDTH ** -0.5),
        "w_o": nrm(ks[21], (Dp, D_MODEL, D_MODEL), D_MODEL ** -0.5),
        "g_ffn": 1.0 + nrm(ks[22], (Dp, D_MODEL), 0.01),
        "w_router": nrm(ks[23], (Dp, D_MODEL, N_EXPERTS), D_MODEL ** -0.5),
        "w_gate": nrm(ks[24], (Dp, N_EXPERTS, D_MODEL, D_FF_EXPERT), D_MODEL ** -0.5),
        "w_up": nrm(ks[25], (Dp, N_EXPERTS, D_MODEL, D_FF_EXPERT), D_MODEL ** -0.5),
        "w_down": nrm(ks[26], (Dp, N_EXPERTS, D_FF_EXPERT, D_MODEL), D_FF_EXPERT ** -0.5),
        "g_final": 1.0 + nrm(ks[27], (D_MODEL,), 0.01),
    }

def first_block(x, g_mix, w_in, conv_a_w, conv_a_b, lru_w_r, lru_b_r, lru_w_i, lru_b_i, lru_lambda, w_a_out,
              conv_b_w, conv_b_b, filt_w1, filt_b1, filt_w2, filt_b2, filt_w3, filt_freq, filt_bias, w_b_out,
              w_o, g_ffn, w_router, w_gate, w_up, w_down, g_final):
    f32 = jnp.float32
    dt = x.dtype
    B, S, D = x.shape
    bidx = jnp.arange(B)[:, None, None]
    cap = CAPACITY_FACTOR * S // N_EXPERTS
    for l in range(DEPTH):
        h = rmsnorm(x, g_mix[l])
        proj = h @ w_in[l]
        a_x, a_gate, hy, gates = jnp.split(
            proj, [LRU_WIDTH, 2 * LRU_WIDTH, 2 * LRU_WIDTH + (HYENA_ORDER + 1) * HYENA_WIDTH], axis=-1)

        xa = dwconv(a_x, conv_a_w[l], conv_a_b[l], (LRU_CONV // 2, LRU_CONV - 1 - LRU_CONV // 2)).astype(f32)
        h_a = (rg_lru(xa, lru_w_r[l, 0], lru_b_r[l, 0], lru_w_i[l, 0], lru_b_i[l, 0], lru_lambda[l, 0], False)
               + rg_lru(xa, lru_w_r[l, 1], lru_b_r[l, 1], lru_w_i[l, 1], lru_b_i[l, 1], lru_lambda[l, 1], True))
        y_a = (h_a * jax.nn.gelu(a_gate.astype(f32))).astype(dt) @ w_a_out[l]

        hy = dwconv(hy, conv_b_w[l], conv_b_b[l], (HYENA_CONV // 2, HYENA_CONV - 1 - HYENA_CONV // 2))
        v, x1, x2 = jnp.split(hy, HYENA_ORDER + 1, axis=-1)
        filt = hyena_filters(S, filt_w1[l], filt_b1[l], filt_w2[l], filt_b2[l], filt_w3[l], filt_freq[l])
        z = v.astype(f32)
        for n, gate in enumerate((x1, x2)):
            k = bidir_kernel(filt[:, n, 0], filt[:, n, 1])
            z = gate.astype(f32) * fftconv(z, k, filt_bias[l, n])
        y_b = z.astype(dt) @ w_b_out[l]

        g_a, g_b = jnp.split(jax.nn.sigmoid(gates.astype(f32)), N_BRANCHES, axis=-1)
        merged = (g_a * y_a.astype(f32) + g_b * y_b.astype(f32)).astype(dt)
        x = x + merged @ w_o[l]

        h = rmsnorm(x, g_ffn[l])
        aff = jax.nn.softmax((h @ w_router[l]).astype(f32), axis=-1)
        vals, idx = lax.top_k(jnp.swapaxes(aff, 1, 2), cap)
        xe = h[bidx, idx]
        gt = jnp.einsum('becd,edf->becf', xe, w_gate[l])
        up = jnp.einsum('becd,edf->becf', xe, w_up[l])
        ye = jnp.einsum('becf,efd->becd', jax.nn.silu(gt) * up, w_down[l])
        ye = ye * vals[..., None].astype(ye.dtype)
        x = x + jnp.zeros_like(x).at[bidx, idx].add(ye.astype(dt))
    return rmsnorm(x, g_final)


DEPTH_2 = 2

CHUNK = 64
N_MEM = 256
HEAD_DIM = 64
A_HEADS = 6
A_WIDTH = A_HEADS * HEAD_DIM
A_DECAY_LORA = 32
A_ICLR_LORA = 32
A_VRES_LORA = 32
A_GATE_LORA = 64
A_GN_EPS = 64e-5
A_PROJ = 3 * A_WIDTH + A_DECAY_LORA + A_ICLR_LORA + A_GATE_LORA
B_HEADS = 6
B_WIDTH = B_HEADS * HEAD_DIM
B_PREV_CHUNKS = 8
B_BAND = (B_PREV_CHUNKS + 1) * CHUNK
REL_MAX = 256
N_REL = CHUNK - 1 + REL_MAX + 1
C_GROUPS = 4
C_GROUP_DIM = 64
C_WIDTH = C_GROUPS * C_GROUP_DIM
POOL_WINDOWS = (2, 4, 8, 16)
MIX_WIDTH = A_WIDTH + B_WIDTH + C_WIDTH
IN_PROJ = A_PROJ + 3 * B_WIDTH + C_WIDTH
X_HEADS = 4
X_HEAD_DIM = D_MODEL // X_HEADS
D_FF = 2816
RMS_EPS = 1e-6
NEG_INF = -1e30


def rms_norm(x, g):
    xf = x.astype(jnp.float32)
    y = xf * lax.rsqrt(jnp.mean(xf * xf, axis=-1, keepdims=True) + RMS_EPS)
    return (y * g.astype(jnp.float32)).astype(x.dtype)

def swiglu(x, w_in, w_out):
    gate, up = jnp.split(x @ w_in, 2, axis=-1)
    return (jax.nn.silu(gate) * up) @ w_out

def token_shift(p):
    return jnp.pad(p, ((0, 0), (1, 0), (0, 0)))[:, :-1]

def rwkv7_mixer(p, v_first, mu, w0, w_up, a0, a_up, g_up, k_k, k_a, r_k, gn_g, gn_b, vres):
    B_, T, _ = p.shape
    f32 = jnp.float32
    p = p + mu * (token_shift(p) - p)
    r, k, v, wd, ad, gd = jnp.split(
        p, [A_WIDTH, 2 * A_WIDTH, 3 * A_WIDTH, 3 * A_WIDTH + A_DECAY_LORA,
            3 * A_WIDTH + A_DECAY_LORA + A_ICLR_LORA], axis=-1)
    w = -jax.nn.softplus(-(w0 + jnp.tanh(wd) @ w_up)) - 0.5
    decay = jnp.exp(-jnp.exp(w.astype(f32)))
    a = jax.nn.sigmoid(a0 + ad @ a_up)
    g = jax.nn.sigmoid(gd) @ g_up
    if vres is None:
        v_first = v
    else:
        v0, v_down, v_up = vres
        v = v + (v_first - v) * jax.nn.sigmoid(v0 + (v @ v_down) @ v_up)
    kk = (k * k_k).reshape(B_, T, A_HEADS, HEAD_DIM).astype(f32)
    kk = kk / jnp.maximum(jnp.sqrt(jnp.sum(kk * kk, axis=-1, keepdims=True)), 1e-12)
    k = k * (1.0 + (a - 1.0) * k_a)
    hs = lambda t: t.reshape(B_, T, A_HEADS, HEAD_DIM).astype(f32)
    r_h, k_h, v_h, w_h, a_h = hs(r), hs(k), hs(v), hs(decay), hs(a)

    def step(S, inp):
        r_t, k_t, v_t, w_t, kk_t, a_t = inp
        sa = jnp.einsum('bhvk,bhk->bhv', S, -kk_t)
        S = (S * w_t[:, :, None, :] + sa[..., None] * (kk_t * a_t)[:, :, None, :]
             + v_t[..., None] * k_t[:, :, None, :])
        return S, jnp.einsum('bhvk,bhk->bhv', S, r_t)

    xs = tuple(jnp.moveaxis(t, 1, 0) for t in (r_h, k_h, v_h, w_h, kk, a_h))
    S0 = jnp.zeros((B_, A_HEADS, HEAD_DIM, HEAD_DIM), f32)
    _, y = lax.scan(step, S0, xs)
    y = jnp.moveaxis(y, 0, 1)
    mean = jnp.mean(y, axis=-1, keepdims=True)
    var = jnp.mean(jnp.square(y - mean), axis=-1, keepdims=True)
    y = ((y - mean) * lax.rsqrt(var + A_GN_EPS)).reshape(B_, T, A_WIDTH) * gn_g + gn_b
    bonus = (jnp.sum(r_h * k_h * r_k, axis=-1, keepdims=True) * v_h).reshape(B_, T, A_WIDTH)
    return ((y + bonus) * g).astype(p.dtype), v_first

def chunk_attention(q, k, v, q_gain, k_gain, rel_bias):
    B_, T, _ = q.shape
    NC = T // CHUNK
    q = rms_norm(q.reshape(B_, T, B_HEADS, HEAD_DIM), q_gain)
    k = rms_norm(k.reshape(B_, T, B_HEADS, HEAD_DIM), k_gain)
    v = v.reshape(B_, T, B_HEADS, HEAD_DIM)
    qc = q.reshape(B_, NC, CHUNK, B_HEADS, HEAD_DIM)
    pad = ((0, 0), (B_PREV_CHUNKS * CHUNK, 0), (0, 0), (0, 0))
    kc = jnp.pad(k, pad).reshape(B_, NC + B_PREV_CHUNKS, CHUNK, B_HEADS, HEAD_DIM)
    vc = jnp.pad(v, pad).reshape(B_, NC + B_PREV_CHUNKS, CHUNK, B_HEADS, HEAD_DIM)
    band_idx = np.arange(NC)[:, None] + np.arange(B_PREV_CHUNKS + 1)[None, :]
    kb = kc[:, band_idx].reshape(B_, NC, B_BAND, B_HEADS, HEAD_DIM)
    vb = vc[:, band_idx].reshape(B_, NC, B_BAND, B_HEADS, HEAD_DIM)
    s = jnp.einsum('bnihd,bnjhd->bhnij', qc, kb).astype(jnp.float32) * (HEAD_DIM ** -0.5)
    dist = B_PREV_CHUNKS * CHUNK + np.arange(CHUNK)[:, None] - np.arange(B_BAND)[None, :]
    rel_idx = np.clip(dist, -(CHUNK - 1), REL_MAX) + (CHUNK - 1)
    bias = rel_bias.astype(jnp.float32)[:, rel_idx]
    valid = (np.arange(NC)[:, None] + (np.arange(B_BAND) // CHUNK)[None, :]) >= B_PREV_CHUNKS
    s = jnp.where(valid[None, None, :, None, :], s + bias[:, None], NEG_INF)
    prob = jax.nn.softmax(s, axis=-1).astype(v.dtype)
    o = jnp.einsum('bhnij,bnjhd->bnihd', prob, vb)
    return o.reshape(B_, T, B_WIDTH)

def multiscale_pool(u, pool_w, pool_scale):
    B_, T, _ = u.shape
    uf = u.astype(jnp.float32).reshape(B_, T, C_GROUPS, C_GROUP_DIM)
    cs = jnp.cumsum(uf, axis=1)
    t1 = jnp.arange(1, T + 1, dtype=jnp.float32)
    outs = []
    for gi, win in enumerate(POOL_WINDOWS):
        c = cs[:, :, gi]
        prev = jnp.pad(c, ((0, 0), (win, 0), (0, 0)))[:, :T]
        cnt = jnp.minimum(t1, float(win))[None, :, None]
        outs.append((c - prev) / cnt - uf[:, :, gi])
    pooled = jnp.stack(outs, axis=2)
    y = jnp.einsum('btgc,gcd->btgd', pooled, pool_w.astype(jnp.float32)).reshape(B_, T, C_WIDTH)
    return (y * pool_scale).astype(u.dtype)

def memory_cross_attention(h, mem_n, wq, wkv, wo, q_gain, k_gain):
    B_, T, _ = h.shape
    M = mem_n.shape[1]
    q = rms_norm((h @ wq).reshape(B_, T, X_HEADS, X_HEAD_DIM), q_gain)
    k, v = jnp.split(mem_n @ wkv, 2, axis=-1)
    k = rms_norm(k.reshape(B_, M, X_HEADS, X_HEAD_DIM), k_gain)
    v = v.reshape(B_, M, X_HEADS, X_HEAD_DIM)
    s = jnp.einsum('bthd,bmhd->bhtm', q, k).astype(jnp.float32) * (X_HEAD_DIM ** -0.5)
    prob = jax.nn.softmax(s, axis=-1).astype(v.dtype)
    o = jnp.einsum('bhtm,bmhd->bthd', prob, v).reshape(B_, T, D_MODEL)
    return o @ wo

def second_inputs(seed: int = 0) -> dict:
    key = jax.random.key(seed)
    ks = iter(jax.random.split(key, 64))
    f32 = jnp.float32
    L, D = DEPTH_2, D_MODEL

    def nrm(shape, scale):
        return scale * jax.random.normal(next(ks), shape, f32)

    def gain(shape, base=1.0, noise=0.1):
        return base + noise * jax.random.normal(next(ks), shape, f32)

    return {
        "x": nrm((BATCH, SEQ, D), 1.0),
        "mem": nrm((BATCH, N_MEM, D), 1.0),
        "norm_ffn1": gain((L, D)),
        "ffn1_wi": nrm((L, D, 2 * D_FF), D ** -0.5),
        "ffn1_wo": nrm((L, D_FF, D), D_FF ** -0.5),
        "norm_mix": gain((L, D)),
        "w_in": nrm((L, D, IN_PROJ), D ** -0.5),
        "w_out": nrm((L, MIX_WIDTH, D), MIX_WIDTH ** -0.5),
        "a_mu": jax.random.uniform(next(ks), (L, A_PROJ), f32),
        "a_w0": nrm((L, A_WIDTH), 0.5),
        "a_w_up": nrm((L, A_DECAY_LORA, A_WIDTH), 0.5 * A_DECAY_LORA ** -0.5),
        "a_a0": nrm((L, A_WIDTH), 0.5),
        "a_a_up": nrm((L, A_ICLR_LORA, A_WIDTH), 0.5 * A_ICLR_LORA ** -0.5),
        "a_g_up": nrm((L, A_GATE_LORA, A_WIDTH), A_GATE_LORA ** -0.5),
        "a_k_k": gain((L, A_WIDTH), 0.85, 0.05),
        "a_k_a": gain((L, A_WIDTH), 1.0, 0.05),
        "a_r_k": nrm((L, A_HEADS, HEAD_DIM), 0.1),
        "a_gn_g": gain((L, A_WIDTH)),
        "a_gn_b": nrm((L, A_WIDTH), 0.02),
        "a_v0": nrm((L - 1, A_WIDTH), 0.5),
        "a_v_down": nrm((L - 1, A_WIDTH, A_VRES_LORA), A_WIDTH ** -0.5),
        "a_v_up": nrm((L - 1, A_VRES_LORA, A_WIDTH), 0.5 * A_VRES_LORA ** -0.5),
        "b_q_gain": gain((L, HEAD_DIM)),
        "b_k_gain": gain((L, HEAD_DIM)),
        "b_rel_bias": nrm((L, B_HEADS, N_REL), 0.5),
        "c_pool_w": nrm((L, C_GROUPS, C_GROUP_DIM, C_GROUP_DIM), C_GROUP_DIM ** -0.5),
        "c_pool_scale": gain((L, C_WIDTH)),
        "norm_cross": gain((L, D)),
        "norm_mem": gain((L, D)),
        "x_wq": nrm((L, D, D), D ** -0.5),
        "x_wkv": nrm((L, D, 2 * D), D ** -0.5),
        "x_wo": nrm((L, D, D), D ** -0.5),
        "x_q_gain": gain((L, X_HEAD_DIM)),
        "x_k_gain": gain((L, X_HEAD_DIM)),
        "norm_ffn2": gain((L, D)),
        "ffn2_wi": nrm((L, D, 2 * D_FF), D ** -0.5),
        "ffn2_wo": nrm((L, D_FF, D), D_FF ** -0.5),
    }

def second_block(x, mem, norm_ffn1, ffn1_wi, ffn1_wo, norm_mix, w_in, w_out,
              a_mu, a_w0, a_w_up, a_a0, a_a_up, a_g_up, a_k_k, a_k_a, a_r_k, a_gn_g, a_gn_b,
              a_v0, a_v_down, a_v_up, b_q_gain, b_k_gain, b_rel_bias, c_pool_w, c_pool_scale,
              norm_cross, norm_mem, x_wq, x_wkv, x_wo, x_q_gain, x_k_gain,
              norm_ffn2, ffn2_wi, ffn2_wo):
    split_pts = [A_PROJ, A_PROJ + B_WIDTH, A_PROJ + 2 * B_WIDTH, A_PROJ + 3 * B_WIDTH]
    v_first = None
    for l in range(DEPTH_2):
        x = x + 0.5 * swiglu(rms_norm(x, norm_ffn1[l]), ffn1_wi[l], ffn1_wo[l])
        h = rms_norm(x, norm_mix[l])
        p = h @ w_in[l]
        p_a, p_q, p_k, p_v, p_c = jnp.split(p, split_pts, axis=-1)
        vres = None if l == 0 else (a_v0[l - 1], a_v_down[l - 1], a_v_up[l - 1])
        y_a, v_first = rwkv7_mixer(p_a, v_first, a_mu[l], a_w0[l], a_w_up[l], a_a0[l], a_a_up[l],
                                   a_g_up[l], a_k_k[l], a_k_a[l], a_r_k[l], a_gn_g[l], a_gn_b[l], vres)
        y_b = chunk_attention(p_q, p_k, p_v, b_q_gain[l], b_k_gain[l], b_rel_bias[l])
        y_c = multiscale_pool(p_c, c_pool_w[l], c_pool_scale[l])
        x = x + jnp.concatenate([y_a, y_b, y_c], axis=-1) @ w_out[l]
        x = x + memory_cross_attention(rms_norm(x, norm_cross[l]), rms_norm(mem, norm_mem[l]),
                                       x_wq[l], x_wkv[l], x_wo[l], x_q_gain[l], x_k_gain[l])
        x = x + 0.5 * swiglu(rms_norm(x, norm_ffn2[l]), ffn2_wi[l], ffn2_wo[l])
    return x


def setup_inputs(seed=0):
    out = dict(first_inputs(seed))
    for name, value in second_inputs(seed + 1).items():
        if name != "x":
            out[name + "_2"] = value
    return out


def reference(
    x, g_mix, w_in, conv_a_w, conv_a_b, lru_w_r, lru_b_r, lru_w_i, lru_b_i, lru_lambda, w_a_out,
    conv_b_w, conv_b_b, filt_w1, filt_b1, filt_w2, filt_b2, filt_w3, filt_freq, filt_bias,
    w_b_out, w_o, g_ffn, w_router, w_gate, w_up, w_down, g_final, mem_2, norm_ffn1_2, ffn1_wi_2,
    ffn1_wo_2, norm_mix_2, w_in_2, w_out_2, a_mu_2, a_w0_2, a_w_up_2, a_a0_2, a_a_up_2,
    a_g_up_2, a_k_k_2, a_k_a_2, a_r_k_2, a_gn_g_2, a_gn_b_2, a_v0_2, a_v_down_2, a_v_up_2,
    b_q_gain_2, b_k_gain_2, b_rel_bias_2, c_pool_w_2, c_pool_scale_2, norm_cross_2, norm_mem_2,
    x_wq_2, x_wkv_2, x_wo_2, x_q_gain_2, x_k_gain_2, norm_ffn2_2, ffn2_wi_2, ffn2_wo_2,
):
    x = first_block(
        x, g_mix, w_in, conv_a_w, conv_a_b, lru_w_r, lru_b_r, lru_w_i, lru_b_i, lru_lambda,
        w_a_out, conv_b_w, conv_b_b, filt_w1, filt_b1, filt_w2, filt_b2, filt_w3, filt_freq,
        filt_bias, w_b_out, w_o, g_ffn, w_router, w_gate, w_up, w_down, g_final,
    )
    return second_block(
        x, mem_2, norm_ffn1_2, ffn1_wi_2, ffn1_wo_2, norm_mix_2, w_in_2, w_out_2, a_mu_2,
        a_w0_2, a_w_up_2, a_a0_2, a_a_up_2, a_g_up_2, a_k_k_2, a_k_a_2, a_r_k_2, a_gn_g_2,
        a_gn_b_2, a_v0_2, a_v_down_2, a_v_up_2, b_q_gain_2, b_k_gain_2, b_rel_bias_2,
        c_pool_w_2, c_pool_scale_2, norm_cross_2, norm_mem_2, x_wq_2, x_wkv_2, x_wo_2,
        x_q_gain_2, x_k_gain_2, norm_ffn2_2, ffn2_wi_2, ffn2_wo_2,
    )


_drawn_inputs = setup_inputs


def setup_inputs(seed=0):
    import zlib

    import numpy as np

    out = dict(_drawn_inputs(seed))
    spreads = {}
    factors = {'g_mix': 3.905,
     'lru_b_r': 8.0,
     'lru_b_i': 8.0,
     'conv_b_b': 8.0,
     'filt_b1': 5.806,
     'filt_b2': 2.816,
     'filt_freq': 8.0,
     'g_ffn': 3.399,
     'g_final': 4.459,
     'a_k_k_2': 8.0,
     'a_gn_b_2': 6.207,
     'b_q_gain_2': 5.756,
     'b_k_gain_2': 5.164,
     'norm_cross_2': 4.269,
     'norm_mem_2': 2.908,
     'x_q_gain_2': 4.378,
     'x_k_gain_2': 4.433}
    for name, (base, spread) in spreads.items():
        noise = np.random.default_rng([zlib.crc32(name.encode()), seed]).standard_normal(out[name].shape)
        drawn = base * np.exp(spread * noise) if base else spread * noise
        out[name] = __import__('jax').numpy.asarray(drawn.astype(out[name].dtype))
    for name, factor in factors.items():
        out[name] = (out[name] * factor).astype(out[name].dtype)
    return out
```

```python
import math
from contextlib import ExitStack

import numpy as np

import concourse.bass as bass
from concourse import mybir

F32 = mybir.dt.float32
ALU = mybir.AluOpType
ACT = mybir.ActivationFunctionType
AXX = mybir.AxisListType.X

P = 128
T = 256
TT = T // P
D = 1024
KD = D // P
SLOT = 2048
RING = 8
EXPERTS, CAP, FE = 16, 32, 2048
EPS = 1e-6
LAYERS = 2
FF = 2816
FSTEPS = FF // 256
AW = 384
HP = AW // P
NPB = 21
CH = 32
SUB = 16
GN_EPS = 64e-5
L2 = 1.5 * 2.0 ** 23
TWO_PI_HI, TWO_PI_LO = 6.28125, 2 * math.pi - 6.28125


def param_columns():
    cols, at = {}, 0
    sizes = [("g_mix", 8), ("conv_a_w", 32), ("conv_a_b", 8), ("lru_b_r", 16), ("lru_b_i", 16),
             ("lru_lambda", 16), ("conv_b_w", 72), ("conv_b_b", 24), ("filt_b1", 1), ("filt_b2", 1),
             ("filt_freq", 2), ("g_ffn", 8), ("g_final", 8)]
    for l in range(LAYERS):
        sizes += [(f"{n}{l}", c) for n, c in (
            ("norm_ffn1", 8), ("norm_mix", 8), ("a_mu", 10), ("a_w0", 3), ("a_a0", 3), ("a_k_k", 3),
            ("a_k_a", 3), ("a_r_k", 3), ("a_gn_g", 3), ("a_gn_b", 3), ("b_q_gain", 1), ("b_k_gain", 1),
            ("c_pool_scale", 2), ("norm_cross", 8), ("norm_mem", 8), ("x_q_gain", 2), ("x_k_gain", 2),
            ("norm_ffn2", 8))]
    sizes += [("a_v0", 3)]
    for n, c in sizes:
        cols[n] = at
        at += c
    return cols, at


def constant_columns():
    cols, at = {}, 0
    for n, c in (("ident", 128), ("ones", 128), ("bones", 128), ("low16", 128), ("up16", 128),
                 ("off32", 128), ("up32", 128), ("upi32", 128), ("iota", 32), ("chunk", 4),
                 ("reset", 256), ("invcnt", 512), ("eps", 1), ("gneps", 1), ("negt", 2)):
        cols[n] = at
        at += c
    return cols, at


def constants():
    cols, n = constant_columns()
    c = np.zeros((P, n), np.float32)
    i = np.arange(P)[:, None]
    j = np.arange(P)[None, :]

    def put(name, a):
        c[:, cols[name]:cols[name] + a.shape[1]] = a

    put("ident", np.eye(P))
    put("ones", np.ones((P, P)))
    put("bones", (i // 64 == j // 64) * 1.0)
    put("low16", ((i // SUB == j // SUB) & (j < i)) * 1.0)
    put("up16", ((i // SUB == j // SUB) & (j > i)) * 1.0)
    put("off32", ((i // CH == j // CH) & (i // SUB > j // SUB)) * 1.0)
    put("up32", ((i // CH == j // CH) & (j > i)) * 1.0)
    put("upi32", ((i // CH == j // CH) & (j >= i)) * 1.0)
    put("iota", np.ones((P, 1)) * np.arange(1, CAP + 1)[None, :])
    put("chunk", (i // CH == np.arange(4)[None, :]) * 1.0)
    t = np.arange(T)[None, :]
    put("reset", np.ones((P, 1)) * (t % CH != 0))
    wins = np.array([[2, 8], [4, 16]])
    inv = np.zeros((P, 2, T))
    for half in range(2):
        for tile in range(2):
            inv[64 * half:64 * half + 64, tile] = 1.0 / np.minimum(t + 1, wins[half, tile])
    put("invcnt", inv.reshape(P, 512))
    put("eps", np.full((P, 1), EPS))
    put("gneps", np.full((P, 1), GN_EPS))
    put("negt", -(i + P * np.arange(2)[None, :]) / (T - 1.0))
    m = np.arange(T, dtype=np.float64)
    th = np.pi * (2 * m + 1) / (2 * T)
    ang = np.arange(T)[:, None] * th[None, :]
    fwd = np.concatenate([np.cos(ang), -np.sin(ang)], axis=1)
    inv = np.concatenate([np.cos(ang).T, -np.sin(ang).T], axis=0) / T
    dft = np.concatenate([fwd.reshape(2, P, 2 * T).transpose(1, 0, 2).reshape(P, 4 * T),
                          inv.reshape(4, P, T).transpose(1, 0, 2).reshape(P, 4 * T)], axis=1)
    f4 = np.float32
    tt = np.linspace(0.0, 1.0, T, dtype=f4)[:, None]
    w = f4(2.0 * math.pi / T) * np.arange(T, dtype=f4)[:, None]
    f = np.linspace(1e-4, 15, 16, dtype=f4)[None, :]
    z = np.concatenate([tt, np.cos(w * f), -np.sin(w * f)], axis=-1)
    lo, hi = math.log(1e-2) / 1.5, math.log(1e-2) / 0.3
    deltas = np.abs(np.linspace(lo, hi, D, dtype=f4))[None, :]
    return {"consts": c, "dft": dft.astype(f4), "zT": np.ascontiguousarray(z.T.astype(f4)), "deltas": deltas.astype(f4)}


def stream_plan():
    plan = []
    for part, first, count in (("a_x", 0, 4), ("hy_v", 8, 4), ("hy_x1", 12, 4), ("hy_x2", 16, 4),
                               ("a_gate", 4, 4), ("gates", 20, 8)):
        plan += [(part, i, "w_in", first + i) for i in range(count)]
    for part in ("w_a_out", "w_b_out", "w_o"):
        plan += [(part, i, part, i) for i in range(4)]
    moe = len(plan)
    after = []

    def ffn(l, which):
        for f in range(FSTEPS + 1):
            if f < FSTEPS:
                after.append(((which, l, "gate", f), f, f"{which}_wi", (l, f)))
                after.append(((which, l, "up", f), f, f"{which}_wi", (l, FSTEPS + f)))
            if f:
                after.append(((which, l, "down", f - 1), f - 1, f"{which}_wo", (l, f - 1)))

    for l in range(LAYERS):
        ffn(l, "ffn1")
        after += [(("mix_in", l), i, "mix_in", (l, i)) for i in range(11)]
        after += [(("mix_out", l), i, "mix_out", (l, i)) for i in range(4)]
        after += [(("x_k", l), i, "x_wkv", (l, i)) for i in range(4)]
        after += [(("x_v", l), i, "x_wkv", (l, 4 + i)) for i in range(4)]
        after += [(("x_q", l), i, "x_wq", (l, i)) for i in range(4)]
        after += [(("x_o", l), i, "x_wo", (l, i)) for i in range(4)]
        ffn(l, "ffn2")
    return plan, moe, after


class Banks:

    def __init__(self, plan, banks, sems):
        self.banks, self.sems, self.reader, self.count, self.at = banks, sems, [], [], {}
        seen = {"act": 0, "dve": 0, None: 0}
        for g, (key, reader) in enumerate(plan):
            seen[reader] += 1
            self.at[key] = g
            self.reader.append(reader)
            self.count.append(seen[reader])
        self.next = 0

    def bank(self, key):
        return self.banks[self.at[key] % 4]

    def was_read(self, eng, key):
        g = self.at[key]
        eng.wait_ge(self.sems[self.reader[g]], self.count[g])

    def claim(self, pe, key):
        g = self.at[key]
        assert g == self.next, (key, g, self.next)
        self.next += 1
        if g >= 4 and self.reader[g - 4]:
            pe.wait_ge(self.sems[self.reader[g - 4]], self.count[g - 4])
        return self.banks[g % 4]


def dense_plan():
    plan = []
    for part, count, reader in (("a_x", 4, "dve"), ("hy_v", 4, "dve"), ("hy_x1", 4, "dve"), ("hy_x2", 4, "dve"),
                                ("a_gate", 4, "act"), ("gates", 8, "act"),
                                ("w_a_out", 4, "dve"), ("w_b_out", 4, "dve"), ("w_o", 4, "dve")):
        plan += [((part, i), reader) for i in range(count)]
    plan += [(("moe", i), None) for i in range(4)]

    def ffn(l, which):
        for f in range(FSTEPS):
            plan.append(((which, l, "gate", f), "act"))
            plan.append(((which, l, "up", f), "dve"))

    for l in range(LAYERS):
        ffn(l, "ffn1")
        for part, count, reader in (("mix_in", 11, "act"), ("mix_out", 4, "dve"), ("x_k", 4, "act"),
                                    ("x_v", 4, "act"), ("x_q", 4, "act"), ("x_o", 4, "dve")):
            plan += [(((part, l), i), reader) for i in range(count)]
        ffn(l, "ffn2")
    return plan


def small_plan():
    plan = []

    def add(reader, *key):
        plan.append((key, reader))

    add("act", "norm", "g_mix")
    for part in ("v", "x1"):
        for i in range(4):
            add("act", "hy_tr", part, i)
    for d in range(2):
        for kind in range(2):
            for i in range(4):
                add("act", "lru", d, kind, i)
    add("dve", "filt", 0)
    add("dve", "filt", 1)
    for n in range(2):
        for tt in range(TT):
            for half in range(2):
                for d in range(2):
                    add("dve", "taps", n, tt, half, d)
        for m in range(4):
            for half in range(2):
                add("act", "spec_k", n, m, half)
        for half in range(2):
            for f in range(2):
                for im in range(2):
                    add("dve", "spec_u", n, half, f, im)
        for i in range(4):
            add("dve", "inv", n, i)
    add("act", "norm", "g_ffn")
    add("dve", "router")
    for tt in range(TT):
        for i in range(2):
            add("act", "h_tok", tt, i)
    add("dve", "affT")
    add("dve", "slot_tr")
    for i in range(8):
        add("act", "PT", i)
    for i in range(8):
        add("dve", "xe", i)
    for i in range(4):
        add("dve", "moe_acc", i)
    add("act", "norm", "g_final")
    for l in range(LAYERS):
        add("act", "norm", f"norm_ffn1{l}")
        for i in range(4):
            add("dve", "ffn1", l, i)
        add("act", "norm", f"norm_mix{l}")
        for i in range(3):
            add("act", "qk_norm", l, i)
        add("act", "av_tr", l, 0)
        add("act", "av_tr", l, 1)
        for h in range(6):
            for it in range(2):
                add("dve", "score", l, h, it)
        for h in range(6):
            add("act", "prob_tr", l, h)
        for q in range(HP):
            add("act", "att", l, q)
        add("act", "pool", l)
        for kind in range(3):
            for i in range(2):
                add("act", "lora", l, kind, i)
        if l:
            add("act", "vdown", l)
            for i in range(2):
                add("act", "vup", l, i)
        for i in range(2):
            add("act", "kk_norm", l, i)
        for tt in range(TT):
            for x in "abkv":
                add("dve" if x == "b" else "act", "rw_tr", l, tt, x)
            for x, r in (("A", "dve"), ("AT", "dve"), ("BT", "dve"), ("CT", "dve"), ("DT", "dve"),
                         ("P2", "act"), ("P2T", "act"), ("Q2", "dve"), ("P4", "act"), ("P4T", "act"), ("Q4", "dve"),
                         ("P8", "act"), ("Q8", "dve"), ("TR", "act"), ("X1", "act"), ("Q32", "dve"),
                         ("BV", "act"), ("WU", "act")):
                for p in range(2):
                    add(r, x, l, tt, p)
            for q in range(HP):
                add("dve", "M", l, tt, q)
                add("dve", "N", l, tt, q)
                add("dve", "RY", l, tt, q)
            for c in range(4):
                add("dve", "S", l, tt, c)
            for p in range(2):
                add("dve", "y", l, tt, p)
        for x, r in (("mean", "dve"), ("var", "act"), ("bonus", "dve")):
            for i in range(2):
                add(r, x, l, i)
        add("act", "norm", f"norm_mem{l}")
        add("act", "norm", f"norm_cross{l}")
        for x in "kq":
            for i in range(2):
                add("act", "xnorm", l, x, i)
        for h in range(4):
            for it in range(2):
                add("dve", "xscore", l, h, it)
        for h in range(4):
            add("act", "xprob_tr", l, h)
        for h in range(4):
            add("act", "xatt", l, h)
        add("act", "norm", f"norm_ffn2{l}")
        for i in range(4):
            add("dve", "ffn2", l, i)
    return plan


def program(nc, A, out):
    ctx = ExitStack()
    with ctx:
        def sb(name, shape):
            return ctx.enter_context(nc.sbuf_tensor(name, shape, F32))

        sems = {}

        def S(name):
            if name not in sems:
                sems[name] = ctx.enter_context(nc.semaphore(name))
            return sems[name]

        PCOL, npc = param_columns()
        CCOL, ncc = constant_columns()
        par = sb("par", [P, npc])
        con = sb("con", [P, ncc])
        ring = [sb(f"ring{i}", [P, SLOT]) for i in range(RING)]
        x = sb("x", [P, KD, T])
        h = sb("h", [P, KD, T])
        sq = sb("sq", [P, KD, T])
        rstd = sb("rstd", [P, T])
        tiny = sb("tiny", [P, 64])
        v_first = sb("v_first", [P, HP, T])
        SCR = 104 * 256
        scr = sb("scr", [P, SCR])
        psd = [ctx.enter_context(nc.psum_tensor(f"psd{i}", [P, 512], F32)) for i in range(4)]
        psx = [ctx.enter_context(nc.psum_tensor(f"psx{i}", [P, 512], F32)) for i in range(4)]

        def at(kib, *shape, parts=P):
            n = math.prod(shape)
            v = scr[0:parts, int(kib * 256):int(kib * 256) + n]
            assert kib * 256 + n <= SCR
            names = " ".join("abcd"[:len(shape)])
            return v if len(shape) == 1 else v.rearrange(
                f"p ({names}) -> p {names}", **{k: s for k, s in zip("abcd", shape)})

        def pc(name, i=0, lo=0, hi=P):
            return par[lo:hi, PCOL[name] + i:PCOL[name] + i + 1]

        def cst(name, n):
            return con[:, CCOL[name]:CCOL[name] + n]

        ident, ones, bones = cst("ident", P), cst("ones", P), cst("bones", P)
        eps_col = con[:, CCOL["eps"]:CCOL["eps"] + 1]
        gneps_col = con[:, CCOL["gneps"]:CCOL["gneps"] + 1]

        plan, MOE, after = stream_plan()
        AFTER = MOE + EXPERTS * 24
        SN = {(k, i): n for n, (k, i, _, _) in enumerate(plan)}
        SN.update({(k, i): AFTER + n for n, (k, i, _, _) in enumerate(after)})
        land = [S(f"landed{i}") for i in range(RING)]
        slots_done = S("slots_done")
        x_done = S("small_done")
        d_read = {"act": S("dense_read_act"), "dve": S("dense_read_dve")}
        x_read = {"act": S("small_read_act"), "dve": S("small_read_dve")}
        DB = Banks(dense_plan(), psd, d_read)
        XB = Banks(small_plan(), psx, x_read)

        def slot_of(key):
            return SN[key if key in SN else (key, key[3])]

        def d_ready(eng, key):
            eng.wait_ge(slots_done, slot_of(key) + 1)
            return DB.bank(key)

        def x_ready(eng, *key):
            eng.wait_ge(x_done, XB.at[key] + 1)
            return XB.bank(key)

        def m2(bank):
            return bank[:, :].rearrange("p (m t) -> p m t", m=2)

        def tri(bank, n=P):
            return bank[:, 0:HP * n].rearrange("p (q n) -> p q n", q=HP)

        PHASES = ["lru", "conv", "merge"] + [
            f"{n}{l}" for l in range(LAYERS) for n in ("ffn1", "att", "rwkv", "cross", "ffn2")]
        phase_end = S("phase_end")

        def barrier(eng, name):
            eng.drain().then_inc(phase_end, 1)
            eng.wait_ge(phase_end, 4 * (PHASES.index(name) + 1))

        XEV = ["w_o", "moe", "final"] + [f"{n}{l}" for l in range(LAYERS) for n in ("ffn1", "mix", "cross", "ffn2")]
        NORMS = ["g_mix", "g_ffn", "g_final"]
        for l in range(LAYERS):
            NORMS += [f"norm_ffn1{l}", f"norm_mix{l}", f"norm_mem{l}", f"norm_cross{l}", f"norm_ffn2{l}"]
        sq_ready, sd_ready, h_ready, x_ready_s = S("sq_ready"), S("sd_ready"), S("h_ready"), S("x_ready")

        xa, ga, gs = at(0, 8, T), at(8, 8, T), at(16, 16, T)
        v_tok, x1_tok, x2 = at(32, TT, D), at(40, TT, D), at(48, 8, T)
        bd, lr, li, le, lh = at(56, 4, 8, P), at(72, 8, T), at(80, 8, T), at(88, 8, T), at(96, 8, T)
        w3h, decay, taps_s, taps_d = at(56, 2, 2, 512, parts=64), at(64, TT, D), at(72, TT, D), at(80, TT, D)
        spec_k, spec_y = at(88, 4, D), at(72, 4, D)
        fwd, inv = at(0, TT, 2 * T), at(4, 4, T)
        filt_w = rstd
        gated = h

        h_tok, onehot, weighted = at(0, TT, D), at(8, TT, EXPERTS, CAP), at(12, TT, EXPERTS, P)
        PT, xe = at(28, EXPERTS, T), at(44, KD, EXPERTS * CAP)
        wr = at(60, KD, EXPERTS)
        xs, sg_e, act_e = at(61, KD, CAP), at(62, 512), at(64, 512)
        actT, ye = at(66, 4, P), at(68, 2, 512)
        aff, lg, affT, wk, msk, slotT, slots = (at(72, TT, 16), at(72.25, TT, 16), at(73, T, parts=16),
                                                at(74, T, parts=16), at(75, T, parts=16), at(76, T, parts=16),
                                                at(77, TT, 16))
        top8 = at(78, 8, parts=16)
        ones16 = at(79, T, parts=16)

        sg, fa = at(0, 2, 2, T), at(4, 2, 2, T)
        ycat, pb, ts = at(0, 8, T), at(8, NPB, T), at(29, 10, T)
        al, rt, be, kt = at(39, HP, T), at(42, HP, T), at(45, HP, T), at(48, HP, T)
        rs6 = at(39, 6, T)
        v_tm, ab, bm, km = at(51, TT, AW), at(54, 6, P), at(57, HP, 4, P), at(63, HP, 4, P)
        MATS = {n: [at(69 + 1.5 * (2 * i + p), HP, P) for p in range(2)] for i, n in enumerate(
            ("A", "AT", "Aoff", "BT", "CT", "DT", "Q", "P2", "P2T", "P4", "P4T"))}
        e1, e2, e3, kk, aa, gg, yy = (pb[:, 0:3, :], pb[:, 3:6, :], pb[:, 6:9, :], pb[:, 9:12, :],
                                      pb[:, 12:15, :], pb[:, 15:18, :], pb[:, 18:21, :])
        MT = h[:, 0:6, :].rearrange("p a t -> p (a t)").rearrange("p (c q n) -> p c q n", c=4, q=HP)
        y0T = h[:, 6:8, :].rearrange("p a t -> p (a t)")[:, 0:HP * P].rearrange("p (q n) -> p q n", q=HP)
        sqf = sq[:, :, :].rearrange("p a t -> p (a t)")
        Np = sqf[:, 0:768].rearrange("p (c q n) -> p c q n", c=4, q=HP)
        Xs = sqf[:, 768:768 + 960].rearrange("p (c q n) -> p c q n", c=5, q=HP)
        RT = at(102, HP, P)
        lora_up = at(101, AW)
        lo = ts[:, 9, :]
        rbias, prob = at(69, 6, 384), at(78, 6, 384)
        probT = at(87, 6, 3, P)
        up, wa, wb = at(29, 2, 16 + T), at(32, 2, 16 + T), at(35, 2, 16 + T)
        poolw = at(99, 2, P)
        mn, xk, xv, xq = at(0, 8, T), at(8, 8, T), at(16, TT, D), at(24, 8, T)
        xprob, xpT, xo = at(32, 8, T), at(40, 4, 2, T), at(48, 8, T)
        vdn, vup, vtmp = at(96, HP, 32), at(97, AW, parts=32), at(99, T, parts=32)
        memT = at(56, 8, T)

        block = ctx.enter_context(nc.Block())

        @block.tensor
        def _(pe):
            def arrived(n):
                pe.wait_ge(land[n % RING], 16 * (n // RING + 1))

            def done(ins):
                ins.then_inc(x_done, 1)

            def w8(n):
                return ring[n % RING][:, :].rearrange("p (k c) -> p k c", k=KD)

            def w2(n):
                return ring[n % RING][:, :].rearrange("p (i c) -> p i c", i=2)

            def norm(g):
                q = NORMS.index(g)
                b = XB.claim(pe, ("norm", g))
                for k in range(KD):
                    if k % 2 == 0:
                        pe.wait_ge(sq_ready, 4 * q + k // 2 + 1)
                    mm = pe.matmul(b[:, 0:T], ones, sq[:, k, :], start=(k == 0), stop=(k == KD - 1))
                done(mm)

            def dense(key, rhs, g=None, n=None, i=0):
                n = slot_of(key) if n is None else n
                b = m2(DB.claim(pe, key))
                arrived(n)
                for m in range(2):
                    for k in range(KD):
                        if g is not None and m == 0:
                            pe.wait_ge(h_ready, KD * NORMS.index(g) + k + 1)
                        mm = pe.matmul(b[:, m, :], w8(n)[:, k, m * P:(m + 1) * P], rhs[:, k, :],
                                       start=(k == 0), stop=(k == KD - 1))
                mm.then_inc(slots_done, 1)

            def ffn(which, l):
                for f in range(FSTEPS + 1):
                    if f < FSTEPS:
                        g = f"norm_{which}{l}" if f == 0 else None
                        dense((which, l, "gate", f), h, g)
                        dense((which, l, "up", f), h)
                    if f:
                        e = f - 1
                        if e == 0:
                            acc = [m2(XB.claim(pe, (which, l, i))) for i in range(4)]
                        n = SN[((which, l, "down", e), e)]
                        arrived(n)
                        DB.was_read(pe, (which, l, "up", e))
                        for i in range(2):
                            for dt in range(KD):
                                mm = pe.matmul(acc[dt // 2][:, dt % 2, :], w2(n)[:, i, dt * P:(dt + 1) * P],
                                               fa[:, e % 2, i, :], start=(e == 0 and i == 0 and dt % 2 == 0),
                                               stop=(e == FSTEPS - 1 and i == 1), skip_group_check=True)
                        mm.then_inc(slots_done, 1)
                pe.drain().then_inc(x_done, 4)

            pe.wait_ge(S("par_in"), 16)
            pe.wait_ge(S("con_in"), 16)
            norm("g_mix")
            for i in range(4):
                dense(("a_x", i), h, "g_mix" if i == 0 else None)

            def conv_turn(part, i):
                DB.was_read(pe, ("hy_" + part, i))
                b = XB.claim(pe, ("hy_tr", part, i))
                for tt in range(TT):
                    for m in range(2):
                        mm = pe.transpose(b[:, (2 * tt + m) * P:(2 * tt + m + 1) * P],
                                          sq[:, 2 * (i % 2) + m, tt * P:(tt + 1) * P], ident)
                done(mm)

            for part in ("v", "x1"):
                for i in range(4):
                    dense(("hy_" + part, i), h)
                    if i:
                        conv_turn(part, i - 1)
                conv_turn(part, 3)
            for part, count in (("hy_x2", 4), ("a_gate", 4), ("gates", 8)):
                for i in range(count):
                    dense((part, i), h)

            pe.wait_ge(S("bd_in"), 16)
            DB.was_read(pe, ("a_x", 3))
            for d in range(2):
                for kind in range(2):
                    for i in range(4):
                        b = m2(XB.claim(pe, ("lru", d, kind, i)))
                        for m in range(2):
                            mm = pe.matmul(b[:, m, :], bd[:, 2 * d + kind, 2 * i + m, :], xa[:, 2 * i + m, :],
                                           start=True, stop=True)
                        done(mm)
            pe.wait_ge(S("lru_out"), 1)
            for i in range(4):
                dense(("w_a_out", i), lh)
            barrier(pe, "lru")

            b = XB.claim(pe, ("filt", 0))
            pe.wait_ge(S("filt_in"), 64)
            pe.wait_ge(S("dft_in"), 16)
            done(pe.matmul(b[0:64, 0:T], filt_w[0:33, 0:64], sq[0:33, 0, :], start=True, stop=True))
            pe.wait_ge(S("filt_sin"), 1)
            b = XB.claim(pe, ("filt", 1))
            done(pe.matmul(b[0:64, 0:T], filt_w[0:64, 64:128], sq[0:64, 1, :], start=True, stop=True))
            pe.wait_ge(S("filt_sin"), 2)
            for n in range(2):
                pe.wait_ge(S(f"w3_in{n}"), 16)
                for tt in range(TT):
                    for half in range(2):
                        for d in range(2):
                            b = XB.claim(pe, ("taps", n, tt, half, d))
                            done(pe.matmul(b[:, :], sq[0:64, 2, tt * P:(tt + 1) * P], w3h[:, d, half, :],
                                           start=True, stop=True))
                pe.wait_ge(S("taps_ready"), n + 1)
                for m in range(4):
                    src = taps_s if m < 2 else taps_d
                    for half in range(2):
                        b = XB.claim(pe, ("spec_k", n, m, half))
                        for tt in range(TT):
                            mm = pe.matmul(b[:, :], fwd[:, tt, m * P:(m + 1) * P],
                                           src[:, tt, half * 512:(half + 1) * 512], start=(tt == 0), stop=(tt == 1))
                        done(mm)
                if n:
                    pe.wait_ge(S("z_tok"), 4)
                for half in range(2):
                    for f in range(2):
                        for im in range(2):
                            b = XB.claim(pe, ("spec_u", n, half, f, im))
                            m = 2 * im + f
                            for tt in range(TT):
                                mm = pe.matmul(b[:, :], fwd[:, tt, m * P:(m + 1) * P],
                                               v_tok[:, tt, half * 512:(half + 1) * 512],
                                               start=(tt == 0), stop=(tt == 1))
                            done(mm)
                pe.wait_ge(S("spec_y"), 4 * (n + 1))
                for i in range(4):
                    b = XB.claim(pe, ("inv", n, i))
                    if n == 0:
                        tt, half = i // 2, i % 2
                        for m in range(4):
                            mm = pe.matmul(b[:, :], inv[:, m, tt * P:(tt + 1) * P],
                                           spec_y[:, m, half * 512:(half + 1) * 512], start=(m == 0), stop=(m == 3))
                    else:
                        for c in range(2):
                            for m in range(4):
                                mm = pe.matmul(m2(b)[:, c, :], spec_y[:, m, (2 * i + c) * P:(2 * i + c + 1) * P],
                                               inv[:, m, :], start=(m == 0), stop=(m == 3))
                    done(mm)
            XB.was_read(pe, ("inv", 1, 3))
            for i in range(4):
                dense(("w_b_out", i), x2)
            pe.wait_ge(S("merged"), 1)
            for i in range(4):
                dense(("w_o", i), gated)
            barrier(pe, "conv")

            norm("g_ffn")
            b = XB.claim(pe, ("router",))
            pe.wait_ge(S("wr_in"), 16)
            for tt in range(TT):
                for k in range(KD):
                    if tt == 0:
                        pe.wait_ge(h_ready, KD * NORMS.index("g_ffn") + k + 1)
                    mm = pe.matmul(b[:, tt * 16:tt * 16 + 16], h[:, k, tt * P:(tt + 1) * P], wr[:, k, :],
                                   start=(k == 0), stop=(k == KD - 1))
            done(mm)
            for tt in range(TT):
                for i in range(2):
                    b = XB.claim(pe, ("h_tok", tt, i))
                    for c in range(4):
                        mm = pe.transpose(b[:, c * P:(c + 1) * P], h[:, 4 * i + c, tt * P:(tt + 1) * P], ident)
                    done(mm)
            b = XB.claim(pe, ("affT",))
            pe.wait_ge(S("aff"), 1)
            for tt in range(TT):
                mm = pe.transpose(b[0:16, tt * P:(tt + 1) * P], aff[:, tt, :], ident)
            done(mm)
            b = XB.claim(pe, ("slot_tr",))
            pe.wait_ge(S("slotT"), 1)
            for tt in range(TT):
                mm = pe.transpose(b[:, tt * 16:tt * 16 + 16], slotT[:, tt * P:(tt + 1) * P], ident[0:16, 0:16])
            done(mm)
            pe.wait_ge(S("weighted"), 1)
            for i in range(8):
                b = XB.claim(pe, ("PT", i))
                for c in range(2):
                    for tt in range(TT):
                        mm = pe.transpose(b[:, (2 * c + tt) * P:(2 * c + tt + 1) * P], weighted[:, tt, 2 * i + c, :],
                                          ident)
                done(mm)
            XB.was_read(pe, ("h_tok", 1, 1))
            for i in range(8):
                b = XB.claim(pe, ("xe", i))
                for tt in range(TT):
                    mm = pe.matmul(b[:, :], h_tok[:, tt, i * P:(i + 1) * P],
                                   onehot[:, tt, :, :].rearrange("p e c -> p (e c)"), start=(tt == 0), stop=(tt == 1))
                done(mm)
            acc = [m2(XB.claim(pe, ("moe_acc", i))) for i in range(4)]
            for k in range(KD):
                pe.matmul(acc[k // 2][:, k % 2, :], ident, x[:, k, :], start=(k % 2 == 0), stop=False,
                          skip_group_check=True)
            XB.was_read(pe, ("xe", 7))
            XB.was_read(pe, ("PT", 7))

            for i in range(4):
                DB.claim(pe, ("moe", i))
            turn = psd[0][:, :].rearrange("p (b n) -> p b n", b=4)
            with pe.Fori(0, EXPERTS) as e:
                pe.wait_ge(S("xs_ready"), e + 1)
                for s in range(16):
                    n = MOE + s
                    pe.wait_ge(land[n % RING], e * (16 * 24 // RING) + 16 * (n // RING + 1))
                    for j in range(4):
                        mm = pe.matmul(psd[s // 8][32 * j:32 * j + 32, :], xs[:, s % 8, :],
                                       ring[n % RING][:, j * 512:(j + 1) * 512], start=(s % 8 == 0), stop=(s % 8 == 7),
                                       skip_group_check=True)
                    mm.then_inc(slots_done, 1)
                pe.wait_ge(S("act_e"), e + 1)
                for b4 in range(4):
                    mm = pe.transpose(turn[:, b4, :], act_e[:, b4 * P:(b4 + 1) * P], ident)
                mm.then_inc(S("turned"), 1)
                pe.wait_ge(S("actT"), e + 1)
                for s in range(0, 8, 2):
                    for q in (s, s + 1):
                        n = MOE + 16 + q
                        pe.wait_ge(land[n % RING], e * (16 * 24 // RING) + 16 * (n // RING + 1))
                    for half in range(2):
                        for j in range(4):
                            n, kt_ = MOE + 16 + s + j // 2, 2 * s + j
                            mm = pe.matmul(psd[2 + half][32 * j:32 * j + 32, :],
                                           actT[:, kt_ % 4, 32 * (kt_ // 4):32 * (kt_ // 4) + 32],
                                           w2(n)[:, j % 2, half * 512:(half + 1) * 512], start=(s == 0), stop=(s == 6),
                                           skip_group_check=True)
                            if half == 1 and j >= 2:
                                mm.then_inc(slots_done, 1)
                pe.wait_ge(S("ye_ready"), 2 * e + 2)
                for k in range(KD):
                    pe.matmul(acc[k // 2][:, k % 2, :], ye[:, k // 4, (k % 4) * P:(k % 4 + 1) * P],
                                   PT[:, bass.ds(e, 1), :].rearrange("p a t -> p (a t)"), start=False, stop=False,
                                   skip_group_check=True)
            pe.drain().then_inc(x_done, 4)
            barrier(pe, "merge")
            norm("g_final")

            for l in range(LAYERS):
                norm(f"norm_ffn1{l}")
                ffn("ffn1", l)
                barrier(pe, f"ffn1{l}")
                norm(f"norm_mix{l}")
                for i in range(11):
                    key = (("mix_in", l), i)
                    if i < 10:
                        dense(key, h, f"norm_mix{l}" if i == 0 else None)
                    else:
                        b, n = m2(DB.claim(pe, key)), slot_of(key)
                        arrived(n)
                        for k in range(KD):
                            mm = pe.matmul(b[:, 0, :], ring[n % RING][:, k * P:(k + 1) * P], h[:, k, :],
                                           start=(k == 0), stop=(k == KD - 1))
                        mm.then_inc(slots_done, 1)

                for i in range(3):
                    b = m2(XB.claim(pe, ("qk_norm", l, i)))
                    pe.wait_ge(S("qk_sq"), 3 * l + i + 1)
                    for m in range(2):
                        mm = pe.matmul(b[:, m, :], bones, sq[:, 2 * i + m, :], start=True, stop=True)
                    done(mm)
                for tt in range(TT):
                    b = XB.claim(pe, ("av_tr", l, tt))
                    for q in range(HP):
                        mm = pe.transpose(tri(b)[:, q, :], pb[:, 16 + q, tt * P:(tt + 1) * P], ident)
                    done(mm)
                pe.wait_ge(S("qk_ready"), l + 1)
                for hd in range(6):
                    r = 64 * (hd % 2)
                    for it in range(2):
                        b = XB.claim(pe, ("score", l, hd, it))
                        done(pe.matmul(b[:, 0:P * (it + 1)], pb[r:r + 64, 10 + hd // 2, it * P:(it + 1) * P],
                                       pb[r:r + 64, 13 + hd // 2, 0:P * (it + 1)], start=True, stop=True))
                for hd in range(6):
                    pe.wait_ge(S("prob"), 6 * l + hd + 1)
                    b = XB.claim(pe, ("prob_tr", l, hd))
                    for j in range(3):
                        mm = pe.transpose(tri(b)[:, j, :], prob[:, hd, j * P:(j + 1) * P], ident)
                    done(mm)
                for q in range(HP):
                    b = XB.claim(pe, ("att", l, q))
                    XB.was_read(pe, ("prob_tr", l, 2 * q + 1))
                    for p in range(2):
                        hd = 2 * q + p
                        o = b[64 * p:64 * p + 64, :]
                        v = [v_tm[:, tt, hd * 64:hd * 64 + 64] for tt in range(TT)]
                        pe.matmul(o[:, 0:P], v[0], probT[:, hd, 0, :], start=True, stop=True)
                        pe.matmul(o[:, P:T], v[0], probT[:, hd, 1, :], start=True, stop=False)
                        mm = pe.matmul(o[:, P:T], v[1], probT[:, hd, 2, :], start=False, stop=True)
                    done(mm)
                b = m2(XB.claim(pe, ("pool", l)))
                pe.wait_ge(S("pooled"), l + 1)
                pe.wait_ge(S(f"att_in{l}"), 32)
                for m in range(2):
                    mm = pe.matmul(b[:, m, :], poolw[:, m, :], up[:, m, 16:16 + T], start=True, stop=True)
                done(mm)
                barrier(pe, f"att{l}")

                pe.wait_ge(S("lora_act"), l + 1)
                pe.wait_ge(S(f"lora_in{l}"), 16 * (3 if l else 1))
                for kind, (r, n) in enumerate(((0, 32), (32, 32), (64, 64))):
                    for i in range(2):
                        b = m2(XB.claim(pe, ("lora", l, kind, i)))
                        for m in range(2 if i == 0 else 1):
                            c = (2 * i + m) * P
                            mm = pe.matmul(b[:, m, :], lora_up[r:r + n, c:c + P], lo[r:r + n, :], start=True, stop=True)
                        done(mm)
                if l:
                    b = XB.claim(pe, ("vdown", l))
                    for q in range(HP):
                        mm = pe.matmul(b[0:32, 0:T], vdn[:, q, :], ts[:, 6 + q, :], start=(q == 0), stop=(q == 2))
                    done(mm)
                    XB.was_read(pe, ("vdown", l))
                    for i in range(2):
                        b = m2(XB.claim(pe, ("vup", l, i)))
                        for m in range(2 if i == 0 else 1):
                            c = (2 * i + m) * P
                            mm = pe.matmul(b[:, m, :], vup[:, c:c + P], vtmp, start=True, stop=True)
                        done(mm)
                pe.wait_ge(S("kk_sq"), l + 1)
                for i in range(2):
                    b = m2(XB.claim(pe, ("kk_norm", l, i)))
                    for m in range(2 if i == 0 else 1):
                        mm = pe.matmul(b[:, m, :], bones, sq[:, 2 * i + m, :], start=True, stop=True)
                    done(mm)
                pe.wait_ge(S("rw_scaled"), l + 1)
                for tt in range(TT):
                    tok = slice(tt * P, (tt + 1) * P)
                    for xk_, src in (("a", al), ("b", be), ("k", kt), ("v", ts[:, 6:9, :])):
                        b = XB.claim(pe, ("rw_tr", l, tt, xk_))
                        for q in range(HP):
                            mm = pe.transpose(tri(b)[:, q, :], src[:, q, tok], ident)
                        done(mm)

                    def mats(name, body, n=P, wait=()):
                        for p in range(2):
                            for w in wait:
                                w(p)
                            b = XB.claim(pe, (name, l, tt, p))
                            for q in range(HP):
                                mm = body(tri(b, n)[:, q, :], p, q)
                            done(mm)

                    def pair(lhs, rhs):
                        def body(o, p, q):
                            r = slice(64 * p, 64 * p + 64)
                            return pe.matmul(o, lhs[r, q, tok], rhs[r, q, tok], start=True, stop=True)
                        return body

                    def prod(lhs, rhs):
                        def body(o, p, q):
                            return pe.matmul(o, MATS[lhs][p][:, q, :], MATS[rhs][p][:, q, :], start=True, stop=True)
                        return body

                    def after(*names):
                        return [lambda p, x=x_: XB.was_read(pe, (x, l, tt, p)) for x_ in names]

                    mats("A", pair(al, be))
                    mats("AT", pair(be, al))
                    mats("BT", pair(kt, al))
                    mats("CT", pair(be, rt))
                    mats("DT", pair(kt, rt))
                    mats("P2", prod("AT", "A"), wait=after("A", "AT"))
                    mats("P2T", prod("A", "AT"))
                    mats("Q2", prod("P2", "Q"), wait=after("P2"))
                    mats("P4", prod("P2T", "P2"), wait=after("P2T"))
                    mats("P4T", prod("P2", "P2T"))
                    mats("Q4", prod("P4", "Q"), wait=after("P4", "Q2"))
                    mats("P8", prod("P4T", "P4"), wait=after("P4T"))
                    mats("Q8", prod("P2", "Q"), wait=after("P8", "Q4"))
                    mats("TR", lambda o, p, q: pe.transpose(o, MATS["Q"][p][:, q, :], ident), wait=after("Q8"))
                    mats("X1", prod("Aoff", "Q"))
                    mats("Q32", prod("P2T", "P4"), wait=after("TR", "X1"))
                    XB.was_read(pe, ("rw_tr", l, tt, "v"))
                    mats("BV", lambda o, p, q: pe.matmul(
                        o, MATS["BT"][p][:, q, :], v_tm[:, tt, (2 * q + p) * 64:(2 * q + p) * 64 + 64],
                        start=True, stop=True), n=64)
                    mats("WU", lambda o, p, q: pe.matmul(o, MATS["Q"][p][:, q, :], ab[:, 2 * q + p, :],
                                                         start=True, stop=True), wait=after("Q32", "BV"))
                    for w in after("WU"):
                        w(0)
                        w(1)
                    XB.was_read(pe, ("rw_tr", l, tt, "b"))
                    XB.was_read(pe, ("rw_tr", l, tt, "k"))
                    for q in range(HP):
                        wu = [MATS["P4T"][p][:, q, :] for p in range(2)]
                        rows = [slice(64 * p, 64 * p + 64) for p in range(2)]
                        b = XB.claim(pe, ("M", l, tt, q))
                        for p in range(2):
                            mm = pe.matmul(b[rows[p], 0:T], wu[p][:, 0:64], bm[:, q, :, rows[p]],
                                           start=True, stop=True)
                        done(mm)
                        b = XB.claim(pe, ("N", l, tt, q))
                        for p in range(2):
                            hd = 2 * q + p
                            for c in range(4):
                                o = b[rows[p], c * 64:c * 64 + 64]
                                pe.matmul(o, bm[:, q, c, rows[p]], wu[p][:, 64:128], start=True, stop=False)
                                mm = pe.matmul(o, km[:, q, c, rows[p]], v_tm[:, tt, hd * 64:hd * 64 + 64],
                                               start=False, stop=True)
                        done(mm)
                        b = XB.claim(pe, ("RY", l, tt, q))
                        for p in range(2):
                            hd = 2 * q + p
                            pe.matmul(b[rows[p], 0:P], wu[p][:, 0:64], MATS["CT"][p][:, q, :], start=True, stop=True)
                            pe.matmul(b[rows[p], P:T], wu[p][:, 64:128], MATS["CT"][p][:, q, :],
                                      start=True, stop=False)
                            mm = pe.matmul(b[rows[p], P:T], v_tm[:, tt, hd * 64:hd * 64 + 64],
                                           MATS["DT"][p][:, q, :], start=False, stop=True)
                        done(mm)
                    for c in range(4):
                        if c == 0:
                            pe.wait_ge(S("state0"), 2 * l + tt + 1)
                            XB.was_read(pe, ("RY", l, tt, HP - 1))
                        else:
                            XB.was_read(pe, ("S", l, tt, c - 1))
                        b = XB.claim(pe, ("S", l, tt, c))
                        for q in range(HP):
                            mm = pe.matmul(tri(b, 64)[:, q, :], MT[:, c, q, :], Xs[:, c, q, :], start=True, stop=True)
                        done(mm)
                    for p in range(2):
                        b = XB.claim(pe, ("y", l, tt, p))
                        r = slice(64 * p, 64 * p + 64)
                        for q in range(HP):
                            for c in range(4):
                                mm = pe.matmul(tri(b)[r, q, c * CH:(c + 1) * CH], Xs[r, c, q, :],
                                               RT[r, q, c * CH:(c + 1) * CH], start=True, stop=True)
                        done(mm)
                for name, src, flag in (("mean", yy, "y_ready"), ("var", sq[:, 0:3, :], "yc_sq"),
                                        ("bonus", e1, "rk_ready")):
                    pe.wait_ge(S(flag), l + 1)
                    for i in range(2):
                        b = m2(XB.claim(pe, (name, l, i)))
                        for m in range(2 if i == 0 else 1):
                            mm = pe.matmul(b[:, m, :], bones, src[:, 2 * i + m, :], start=True, stop=True)
                        done(mm)
                pe.wait_ge(S("mix_cat"), l + 1)
                for i in range(4):
                    dense((("mix_out", l), i), ycat)
                barrier(pe, f"rwkv{l}")

                norm(f"norm_mem{l}")
                for i in range(4):
                    dense((("x_k", l), i), mn, f"norm_mem{l}" if i == 0 else None)
                for i in range(4):
                    key = (("x_v", l), i)
                    n, b = slot_of(key), m2(DB.claim(pe, key))
                    arrived(n)
                    for tt in range(TT):
                        for k in range(KD):
                            mm = pe.matmul(b[:, tt, :], mn[:, k, tt * P:(tt + 1) * P], w8(n)[:, k, :],
                                           start=(k == 0), stop=(k == KD - 1))
                    mm.then_inc(slots_done, 1)
                norm(f"norm_cross{l}")
                for i in range(4):
                    dense((("x_q", l), i), h, f"norm_cross{l}" if i == 0 else None)
                for j, name in enumerate("kq"):
                    for i in range(2):
                        b = m2(XB.claim(pe, ("xnorm", l, name, i)))
                        pe.wait_ge(S("x_sq"), 4 * l + 2 * j + i + 1)
                        for m in range(2):
                            for c in range(2):
                                mm = pe.matmul(b[:, m, :], ones, sq[:, 4 * i + 2 * m + c, :], start=(c == 0), stop=(c == 1))
                        done(mm)
                pe.wait_ge(S("xqk_ready"), l + 1)
                for hd in range(4):
                    for it in range(TT):
                        b = XB.claim(pe, ("xscore", l, hd, it))
                        for c in range(2):
                            mm = pe.matmul(b[:, 0:T], xq[:, 2 * hd + c, it * P:(it + 1) * P], xk[:, 2 * hd + c, :],
                                           start=(c == 0), stop=(c == 1))
                        done(mm)
                for hd in range(4):
                    pe.wait_ge(S("xprob"), 4 * l + hd + 1)
                    b = XB.claim(pe, ("xprob_tr", l, hd))
                    for mt in range(2):
                        for it in range(TT):
                            mm = pe.transpose(m2(b)[:, mt, it * P:(it + 1) * P],
                                              xprob[:, 2 * hd + it, mt * P:(mt + 1) * P], ident)
                    done(mm)
                for hd in range(4):
                    b = m2(XB.claim(pe, ("xatt", l, hd)))
                    XB.was_read(pe, ("xprob_tr", l, hd))
                    for c in range(2):
                        for mt in range(2):
                            mm = pe.matmul(b[:, c, :], xv[:, mt, (2 * hd + c) * P:(2 * hd + c + 1) * P],
                                           xpT[:, hd, mt, :], start=(mt == 0), stop=(mt == 1))
                    done(mm)
                XB.was_read(pe, ("xatt", l, 3))
                for i in range(4):
                    dense((("x_o", l), i), xo)
                barrier(pe, f"cross{l}")
                norm(f"norm_ffn2{l}")
                ffn("ffn2", l)
                barrier(pe, f"ffn2{l}")

        @block.scalar
        def _(act):
            def read(ins):
                ins.then_inc(x_read["act"], 1)

            def copy(o, i):
                return act.activation(o, i, ACT.Copy)

            def norm(g, event=None, src=None):
                q = NORMS.index(g)
                src = x if src is None else src
                if event:
                    act.wait_ge(x_ready_s, XEV.index(event) + 1)
                for i in range(4):
                    act.activation(sq[:, 2 * i:2 * i + 2, :], src[:, 2 * i:2 * i + 2, :],
                                   ACT.Square).then_inc(sq_ready, 1)
                b = x_ready(act, "norm", g)
                if q:
                    act.wait_ge(h_ready, KD * q)
                read(act.activation(rstd[:, :], b[:, 0:T], ACT.Sqrt, bias=eps_col, scale=1.0 / D))

            def ffn(which, l):
                for f in range(FSTEPS):
                    b = d_ready(act, (which, l, "gate", f))
                    if f > 1:
                        DB.was_read(act, (which, l, "up", f - 2))
                    act.activation(sg[:, f % 2, :, :], m2(b), ACT.Silu).then_inc(d_read["act"], 1)

            act.dma_start(x[:, :, :], A["xT"].rearrange("(k p) t -> p k t", p=P)).then_inc(S("x_in"), 16)
            act.dma_start(con[:, :], A["consts"]).then_inc(S("con_in"), 16)
            act.dma_start(par[:, :], A["params"]).then_inc(S("par_in"), 16)
            act.wait_ge(S("x_in"), 16)
            act.wait_ge(S("con_in"), 16)
            norm("g_mix")
            act.wait_ge(S("lam_abs"), 1)
            act.activation(tiny[:, 16:32], tiny[:, 0:16], ACT.Exp, scale=-1.0).then_inc(S("lam_exp"), 1)
            for part, dst in (("v", v_tok), ("x1", x1_tok)):
                for i in range(4):
                    b = x_ready(act, "hy_tr", part, i)
                    read(copy(dst[:, :, i * 256:(i + 1) * 256], b[:, :].rearrange("p (t c) -> p t c", t=TT)))
            for i in range(4):
                b = d_ready(act, ("a_gate", i))
                act.activation(ga[:, 2 * i:2 * i + 2, :], m2(b), ACT.Gelu_apprx_tanh).then_inc(d_read["act"], 1)
            for i in range(8):
                b = d_ready(act, ("gates", i))
                act.activation(gs[:, 2 * i:2 * i + 2, :], m2(b), ACT.Sigmoid).then_inc(d_read["act"], 1)
            act.wait_ge(S("lru_c"), 1)
            act.wait_ge(S("par_in"), 16)
            for d in range(2):
                if d:
                    act.wait_ge(S("lru_scan"), 1)
                for kind, (dst, bias) in enumerate(((lr, "lru_b_r"), (li, "lru_b_i"))):
                    for i in range(4):
                        b = m2(x_ready(act, "lru", d, kind, i))
                        for m in range(2):
                            c = 2 * i + m
                            ins = act.activation(dst[:, c, :], b[:, m, :], ACT.Sigmoid, bias=pc(bias, 8 * d + c))
                        read(ins)
                act.drain()
                for c in range(KD):
                    act.activation(le[:, c, :], lr[:, c, :], ACT.Exp, scale=tiny[:, 48 + 8 * d + c:49 + 8 * d + c])
                act.drain()
                for c in range(KD):
                    act.activation(lr[:, c, :], lr[:, c, :], ACT.Exp, scale=tiny[:, 32 + 8 * d + c:33 + 8 * d + c])
                act.drain().then_inc(S("lru_exp"), 1)
                act.wait_ge(S("lru_neg"), d + 1)
                act.activation(le[:, :, :], le[:, :, :], ACT.Sqrt, bias=1.0).then_inc(S("lru_mult"), 1)
            barrier(act, "lru")

            for i in range(2):
                act.wait_ge(S("filt_red"), i + 1)
                act.activation(sq[0:64, 1 + i, :], sq[0:64, 1 + i, :], ACT.Sin).then_inc(S("filt_sin"), 1)
            act.wait_ge(S("filt_in"), 64)
            for tt in (0, 1):
                act.activation(decay[:, tt, :], decay[:, 1, :], ACT.Exp,
                               scale=con[:, CCOL["negt"] + tt:CCOL["negt"] + tt + 1])
                act.drain()
            act.drain().then_inc(S("decay"), 1)
            for n in range(2):
                for m in range(4):
                    for half in range(2):
                        b = x_ready(act, "spec_k", n, m, half)
                        read(copy(spec_k[:, m, half * 512:(half + 1) * 512], b[:, :]))
            barrier(act, "conv")

            norm("g_ffn", "w_o")
            act.wait_ge(S("lg_shift"), 1)
            for tt in range(TT):
                act.activation(aff[:, tt, :], lg[:, tt, :], ACT.Exp, accum_out=tiny[:, tt:tt + 1])
            act.drain().then_inc(S("aff_exp"), 1)
            for tt in range(TT):
                for i in range(2):
                    b = x_ready(act, "h_tok", tt, i)
                    read(copy(h_tok[:, tt, i * 512:(i + 1) * 512], b[:, :]))
            for i in range(8):
                b = x_ready(act, "PT", i)
                read(copy(PT[:, 2 * i:2 * i + 2, :], m2(b)))
            with act.Fori(0, EXPERTS) as e:
                act.wait_ge(slots_done, 24 * e + MOE + 8)
                act.activation(sg_e, psd[0][:, :], ACT.Silu).then_inc(S("sg_e"), 1)
                act.wait_ge(S("turned"), e + 1)
                copy(actT[:, :, :], psd[0][:, :].rearrange("p (b n) -> p b n", b=4)).then_inc(S("actT"), 1)
                act.wait_ge(slots_done, 24 * e + MOE + 24)
                copy(ye[:, 0, :], psd[2][:, :]).then_inc(S("ye_ready"), 1)
            barrier(act, "merge")
            norm("g_final", "moe")

            for l in range(LAYERS):
                norm(f"norm_ffn1{l}", "final" if l == 0 else f"ffn2{l - 1}")
                ffn("ffn1", l)
                barrier(act, f"ffn1{l}")
                norm(f"norm_mix{l}", f"ffn1{l}")
                for i in range(11):
                    b, m = m2(d_ready(act, (("mix_in", l), i))), 2 if i < 10 else 1
                    copy(pb[:, 2 * i:2 * i + m, :], b[:, 0:m, :]).then_inc(d_read["act"], 1)
                act.drain()
                for i in range(3):
                    act.activation(sq[:, 2 * i:2 * i + 2, :], pb[:, 10 + 2 * i:12 + 2 * i, :],
                                   ACT.Square).then_inc(S("qk_sq"), 1)
                for i in range(3):
                    b = x_ready(act, "qk_norm", l, i)
                    read(act.activation(rs6[:, 2 * i:2 * i + 2, :], m2(b), ACT.Sqrt, bias=eps_col, scale=1.0 / 64))
                for tt in range(TT):
                    b = x_ready(act, "av_tr", l, tt)
                    read(copy(v_tm[:, tt, :], b[:, 0:AW]))
                for hd in range(6):
                    act.wait_ge(S("score_max"), 6 * l + hd + 1)
                    for it, (lo_, hi_) in enumerate(((0, P), (P, AW))):
                        act.activation(prob[:, hd, lo_:hi_], prob[:, hd, lo_:hi_], ACT.Exp,
                                       bias=tiny[:, 2 * hd + it:2 * hd + it + 1],
                                       accum_out=tiny[:, 12 + 2 * hd + it:13 + 2 * hd + it])
                    act.drain().then_inc(S("score_exp"), 1)
                for hd in range(6):
                    b = x_ready(act, "prob_tr", l, hd)
                    read(copy(probT[:, hd, :, :], tri(b)))
                for q in range(HP):
                    b = x_ready(act, "att", l, q)
                    read(copy(ycat[:, 3 + q, :], b[:, 0:T]))
                b = m2(x_ready(act, "pool", l))
                for m in range(2):
                    ins = act.activation(ycat[:, 6 + m, :], b[:, m, :], ACT.Copy, scale=pc(f"c_pool_scale{l}", m))
                read(ins)
                barrier(act, f"att{l}")

                act.wait_ge(S("shifted"), l + 1)
                act.activation(lo[0:32, :], lo[0:32, :], ACT.Tanh)
                act.activation(lo[64:128, :], lo[64:128, :], ACT.Sigmoid)
                act.drain().then_inc(S("lora_act"), 1)
                for kind, (dst, bias) in enumerate(((rt, "a_w0"), (aa, "a_a0"), (gg, None))):
                    for i in range(2):
                        b = m2(x_ready(act, "lora", l, kind, i))
                        for m in range(2 if i == 0 else 1):
                            j = 2 * i + m
                            ins = copy(dst[:, j, :], b[:, m, :]) if bias is None else act.activation(
                                dst[:, j, :], b[:, m, :], ACT.Sigmoid, bias=pc(f"{bias}{l}", j))
                        read(ins)
                if l:
                    b = x_ready(act, "vdown", l)
                    read(copy(vtmp, b[0:32, 0:T]))
                    for i in range(2):
                        b = m2(x_ready(act, "vup", l, i))
                        for m in range(2 if i == 0 else 1):
                            j = 2 * i + m
                            ins = act.activation(be[:, j, :], b[:, m, :], ACT.Sigmoid, bias=pc("a_v0", j))
                        read(ins)
                act.wait_ge(S("kk_raw"), l + 1)
                act.activation(sq[:, 0:3, :], kk, ACT.Square).then_inc(S("kk_sq"), 1)
                for i in range(2):
                    b, m = m2(x_ready(act, "kk_norm", l, i)), 2 - i
                    read(act.activation(al[:, 2 * i:2 * i + m, :], b[:, 0:m, :], ACT.Sqrt))
                act.wait_ge(S("decays"), l + 1)
                act.activation(e1, kt[:, :, :], ACT.Exp)
                act.activation(e2, kt[:, :, :], ACT.Exp, scale=-1.0)
                act.activation(e3, be[:, :, :], ACT.Exp)
                act.drain().then_inc(S("decay_exp"), 1)
                for tt in range(TT):
                    b = tri(x_ready(act, "rw_tr", l, tt, "a"))
                    read(copy(ab[:, :, 0:64], b.rearrange("p q (h n) -> p (q h) n", h=2)))
                    b = tri(x_ready(act, "rw_tr", l, tt, "k"))
                    for c in range(4):
                        ins = act.activation(km[:, :, c, :], b, ACT.Copy,
                                             scale=con[:, CCOL["chunk"] + c:CCOL["chunk"] + c + 1])
                    read(ins)
                    b = x_ready(act, "rw_tr", l, tt, "v")
                    read(copy(v_tm[:, tt, :], b[:, 0:AW]))
                    for name, dst in (("P2", "P2"), ("P2T", "P2T"), ("P4", "P4"), ("P4T", "P4T"), ("P8", "P2"),
                                      ("TR", "P2T"), ("X1", "P4"), ("BV", None), ("WU", "P4T")):
                        for p in range(2):
                            b = x_ready(act, name, l, tt, p)
                            if name == "BV":
                                ab_p = ab[:, :, :].rearrange("p (q h) n -> p q h n", h=2)
                                read(copy(ab_p[:, :, p, 64:128], tri(b, 64)))
                            else:
                                read(copy(MATS[dst][p][:, :, :], tri(b)))
                act.wait_ge(S("y_mean"), l + 1)
                act.activation(sq[:, 0:3, :], yy, ACT.Square).then_inc(S("yc_sq"), 1)
                for i in range(2):
                    b, m = m2(x_ready(act, "var", l, i)), 2 - i
                    read(act.activation(al[:, 2 * i:2 * i + m, :], b[:, 0:m, :], ACT.Sqrt, bias=gneps_col,
                                        scale=1.0 / 64))
                barrier(act, f"rwkv{l}")

                act.wait_ge(S("mem_in"), 16 * (l + 1))
                norm(f"norm_mem{l}", src=memT)
                for i in range(4):
                    b = d_ready(act, (("x_k", l), i))
                    copy(xk[:, 2 * i:2 * i + 2, :], m2(b)).then_inc(d_read["act"], 1)
                for i in range(4):
                    b = d_ready(act, (("x_v", l), i))
                    copy(xv[:, :, i * 256:(i + 1) * 256], m2(b)).then_inc(d_read["act"], 1)
                norm(f"norm_cross{l}", f"mix{l}")
                for i in range(4):
                    b = d_ready(act, (("x_q", l), i))
                    copy(xq[:, 2 * i:2 * i + 2, :], m2(b)).then_inc(d_read["act"], 1)
                act.drain()
                for j, (name, src) in enumerate((("k", xk), ("q", xq))):
                    if j:
                        x_ready(act, "xnorm", l, "k", 1)
                    for i in range(2):
                        act.activation(sq[:, 4 * i:4 * i + 4, :], src[:, 4 * i:4 * i + 4, :],
                                       ACT.Square).then_inc(S("x_sq"), 1)
                    for i in range(2):
                        b = x_ready(act, "xnorm", l, name, i)
                        k4 = 4 * j + 2 * i
                        read(act.activation(memT[:, k4:k4 + 2, :], m2(b), ACT.Sqrt, bias=eps_col, scale=1.0 / 256))
                for hd in range(4):
                    act.wait_ge(S("xscore_max"), 4 * l + hd + 1)
                    for it in range(TT):
                        j = 2 * hd + it
                        act.activation(xprob[:, j, :], xprob[:, j, :], ACT.Exp, bias=tiny[:, j:j + 1],
                                       accum_out=tiny[:, 12 + j:13 + j])
                    act.drain().then_inc(S("xscore_exp"), 1)
                for hd in range(4):
                    b = x_ready(act, "xprob_tr", l, hd)
                    read(copy(xpT[:, hd, :, :], m2(b)))
                for hd in range(4):
                    b = x_ready(act, "xatt", l, hd)
                    read(copy(xo[:, 2 * hd:2 * hd + 2, :], m2(b)))
                barrier(act, f"cross{l}")
                norm(f"norm_ffn2{l}", f"cross{l}")
                ffn("ffn2", l)
                barrier(act, f"ffn2{l}")

        @block.vector
        def _(dve):
            def read(ins):
                ins.then_inc(x_read["dve"], 1)

            def dread(ins):
                ins.then_inc(d_read["dve"], 1)

            def tt_(o, a, b, op):
                return dve.tensor_tensor(o, a, b, op)

            def norm(g, dst, src=None):
                src = x if src is None else src
                XB.was_read(dve, ("norm", g))
                dve.reciprocal(rstd[:, :], rstd[:, :])
                dve.drain()
                for k in range(KD):
                    dve.scalar_tensor_tensor(out=dst[:, k, :], in0=src[:, k, :], scalar=pc(g, k), in1=rstd[:, :],
                                             op0=ALU.mult, op1=ALU.mult).then_inc(h_ready, 1)

            def x_event():
                dve.drain().then_inc(x_ready_s, 1)

            def ffn(which, l):
                for f in range(FSTEPS):
                    b = m2(d_ready(dve, (which, l, "up", f)))
                    DB.was_read(dve, (which, l, "gate", f))
                    if f > 1:
                        dve.wait_ge(slots_done, SN[((which, l, "down", f - 2), f - 2)] + 1)
                    dread(tt_(fa[:, f % 2, :, :], b, sg[:, f % 2, :, :], ALU.mult))
                for i in range(4):
                    b = m2(x_ready(dve, which, l, i))
                    read(dve.scalar_tensor_tensor(out=x[:, 2 * i:2 * i + 2, :], in0=b, scalar=0.5,
                                                  in1=x[:, 2 * i:2 * i + 2, :], op0=ALU.mult, op1=ALU.add))
                x_event()

            dve.wait_ge(S("par_in"), 16)
            dve.wait_ge(S("con_in"), 16)
            lam = par[:, PCOL["lru_lambda"]:PCOL["lru_lambda"] + 16]
            t0, t1, t2, t3 = (tiny[:, i:i + 16] for i in (0, 16, 32, 48))
            dve.tensor_scalar(t0, lam, -1.0, None, ALU.mult)
            dve.drain()
            tt_(t0, t0, lam, ALU.max)
            dve.drain().then_inc(S("lam_abs"), 1)
            norm("g_mix", h)
            dve.wait_ge(S("lam_exp"), 1)
            dve.tensor_scalar(t2, t1, 2.0, None, ALU.add)
            dve.drain()
            dve.reciprocal(t2, t2)
            dve.drain()
            tt_(t1, t1, t2, ALU.mult)
            dve.drain()
            tt_(t2, t1, t1, ALU.mult)
            dve.memset(t3, 1.0 / 21)
            for n in range(19, 0, -2):
                dve.drain()
                tt_(t3, t3, t2, ALU.mult)
                dve.drain()
                dve.tensor_scalar(t3, t3, 1.0 / n, None, ALU.add)
            dve.drain()
            tt_(t3, t3, t1, ALU.mult)
            dve.tensor_scalar(t0, lam, -1.0, 0.0, ALU.mult, ALU.max)
            dve.drain()
            dve.scalar_tensor_tensor(out=t3, in0=t3, scalar=2.0, in1=t0, op0=ALU.mult, op1=ALU.add)
            dve.drain()
            dve.tensor_scalar(t2, t3, -8.0, None, ALU.mult)
            dve.tensor_scalar(t3, t3, -16.0, None, ALU.mult)
            dve.drain().then_inc(S("lru_c"), 1)

            def conv(b, dst, taps, centre, w, bias):
                b = m2(b)
                order = [centre] + [j for j in range(taps) if j != centre]
                for j in order:
                    o = j - centre
                    for m in range(2):
                        if o == 0:
                            ins = dve.tensor_scalar(dst[m], b[:, m, :], w(j, m), bias(m), ALU.mult, ALU.add)
                        else:
                            a0, a1 = max(0, -o), T - max(0, o)
                            ins = dve.scalar_tensor_tensor(out=dst[m][:, a0:a1], in0=b[:, m, a0 + o:a1 + o],
                                                           scalar=w(j, m), in1=dst[m][:, a0:a1],
                                                           op0=ALU.mult, op1=ALU.add)
                    if j != order[-1]:
                        dve.drain()
                dread(ins)

            for i in range(4):
                conv(d_ready(dve, ("a_x", i)), [xa[:, 2 * i + m, :] for m in range(2)], 4, 2,
                     lambda j, m: pc("conv_a_w", 8 * j + 2 * i + m), lambda m: pc("conv_a_b", 2 * i + m))
            tr = []
            for part, base in (("v", 0), ("x1", 8), ("x2", 16)):
                for i in range(4):
                    b = d_ready(dve, ("hy_" + part, i))
                    if part == "x2":
                        dst = [x2[:, 2 * i + m, :] for m in range(2)]
                    else:
                        dst = [sq[:, 2 * (i % 2) + m, :] for m in range(2)]
                        if len(tr) > 1:
                            x_ready(dve, "hy_tr", *tr[-2])
                        tr.append((part, i))
                    conv(b, dst, 3, 1, lambda j, m: pc("conv_b_w", 24 * j + base + 2 * i + m),
                         lambda m: pc("conv_b_b", base + 2 * i + m))

            for d in range(2):
                dve.wait_ge(S("lru_exp"), d + 1)
                dve.tensor_scalar(le[:, :, :], le[:, :, :], 1.0, -1.0, ALU.min, ALU.mult)
                tt_(li[:, :, :], li[:, :, :], xa, ALU.mult)
                dve.drain()
                first = 0 if d == 0 else T - 1
                dve.memset(le[:, :, first:first + 1], 0.0)
                dve.drain().then_inc(S("lru_neg"), 1)
                dve.wait_ge(S("lru_mult"), d + 1)
                tt_(li[:, :, :], li[:, :, :], le[:, :, :], ALU.mult)
                dve.drain()
                for c in range(KD):
                    if d == 0:
                        dve.tensor_tensor_scan(lh[:, c, :], lr[:, c, :], li[:, c, :], 0.0, ALU.mult, ALU.add)
                    else:
                        dve.tensor_tensor_scan(le[:, c, ::-1], lr[:, c, ::-1], li[:, c, ::-1], 0.0,
                                               ALU.mult, ALU.add)
                dve.drain().then_inc(S("lru_scan"), 1)
            tt_(lh[:, :, :], lh[:, :, :], le[:, :, :], ALU.add)
            dve.drain()
            DB.was_read(dve, ("a_gate", 3))
            tt_(lh[:, :, :], lh[:, :, :], ga, ALU.mult)
            dve.drain().then_inc(S("lru_out"), 1)
            DB.was_read(dve, ("gates", 7))
            for i in range(4):
                b = m2(d_ready(dve, ("w_a_out", i)))
                dread(tt_(gated[:, 2 * i:2 * i + 2, :], b, gs[:, 2 * i:2 * i + 2, :], ALU.mult))
            barrier(dve, "lru")

            dve.wait_ge(S("filt_in"), 64)
            for i in range(2):
                b = x_ready(dve, "filt", i)[0:64, 0:T]
                v, k = sq[0:64, 1 + i, :], sq[0:64, 3, :]
                read(dve.tensor_scalar(v, b, pc(f"filt_b{i + 1}", 0, 0, 64), pc("filt_freq", i, 0, 64),
                                       ALU.add, ALU.mult))
                dve.drain()
                dve.tensor_scalar(k, v, 1 / (2 * math.pi), L2, ALU.mult, ALU.add)
                dve.drain()
                dve.tensor_scalar(k, k, L2, None, ALU.subtract)
                dve.drain()
                for part in (TWO_PI_HI, TWO_PI_LO):
                    dve.scalar_tensor_tensor(out=v, in0=k, scalar=-part, in1=v, op0=ALU.mult, op1=ALU.add)
                    dve.drain()
                dve.tensor_scalar(v, v, 3.1415925, -3.1415925, ALU.min, ALU.max)
                dve.drain().then_inc(S("filt_red"), 1)
            dve.wait_ge(S("decay"), 1)
            bias_row = at(8, 2, D, parts=1)
            f0, f1 = (sq[:, i:i + 2, :].rearrange("p a t -> p (a t)") for i in (4, 6))
            dve.wait_ge(S("bias_in"), 16)
            for n in range(2):
                for tt in range(TT):
                    for half in range(2):
                        cs = slice(half * 512, (half + 1) * 512)
                        for d, dst in ((0, f0), (1, f1)):
                            b = x_ready(dve, "taps", n, tt, half, d)
                            read(tt_(dst, b[:, :], decay[:, tt, cs], ALU.mult))
                        dve.drain()
                        if tt == 0:
                            dve.memset(f1[0:1, :], 0.0)
                            tt_(f0[0:1, :], f0[0:1, :], bias_row[:, n, cs], ALU.add)
                            dve.drain()
                        tt_(taps_s[:, tt, cs], f0, f1, ALU.add)
                        tt_(taps_d[:, tt, cs], f0, f1, ALU.subtract)
                        dve.drain()
                dve.drain().then_inc(S("taps_ready"), 1)
                XB.was_read(dve, ("spec_k", n, 3, 1))
                for half in range(2):
                    cs = slice(half * 512, (half + 1) * 512)
                    for f in range(2):
                        kr, ki = spec_k[:, f, cs], spec_k[:, 2 + f, cs]
                        yr, yi = spec_y[:, f, cs], spec_y[:, 2 + f, cs]
                        ur = x_ready(dve, "spec_u", n, half, f, 0)
                        tt_(yr, ur[:, :], kr, ALU.mult)
                        read(tt_(yi, ur[:, :], ki, ALU.mult))
                        ui = x_ready(dve, "spec_u", n, half, f, 1)
                        tt_(f0, ui[:, :], ki, ALU.mult)
                        read(tt_(f1, ui[:, :], kr, ALU.mult))
                        dve.drain()
                        tt_(yr, yr, f0, ALU.subtract)
                        tt_(yi, yi, f1, ALU.add)
                        dve.drain().then_inc(S("spec_y"), 1)
                for i in range(4):
                    b = x_ready(dve, "inv", n, i)
                    if n == 0:
                        tt, cs = i // 2, slice((i % 2) * 512, (i % 2 + 1) * 512)
                        read(tt_(v_tok[:, tt, cs], b[:, :], x1_tok[:, tt, cs], ALU.mult))
                    else:
                        read(tt_(x2[:, 2 * i:2 * i + 2, :], m2(b), x2[:, 2 * i:2 * i + 2, :], ALU.mult))
                if n == 0:
                    dve.drain().then_inc(S("z_tok"), 4)
            for i in range(4):
                b = m2(d_ready(dve, ("w_b_out", i)))
                two = slice(2 * i, 2 * i + 2)
                dread(tt_(sq[:, two, :], b, gs[:, KD + 2 * i:KD + 2 * i + 2, :], ALU.mult))
            dve.drain()
            tt_(gated[:, :, :], gated[:, :, :], sq[:, :, :], ALU.add)
            dve.drain().then_inc(S("merged"), 1)
            for i in range(4):
                b = m2(d_ready(dve, ("w_o", i)))
                two = slice(2 * i, 2 * i + 2)
                dread(tt_(x[:, two, :], b, x[:, two, :], ALU.add))
            x_event()
            barrier(dve, "conv")

            norm("g_ffn", h)
            b = x_ready(dve, "router")[:, 0:32].rearrange("p (t e) -> p t e", t=TT)
            dve.tensor_reduce(tiny[:, 4:6], b, AXX, ALU.max)
            dve.drain()
            read(tt_(lg, b, tiny[:, 4:6].unsqueeze(2).broadcast_to([P, TT, 16]), ALU.subtract))
            dve.drain().then_inc(S("lg_shift"), 1)
            dve.wait_ge(S("aff_exp"), 1)
            dve.reciprocal(tiny[:, 2:4], tiny[:, 0:2])
            dve.drain()
            tt_(aff, aff, tiny[:, 2:4].unsqueeze(2).broadcast_to([P, TT, 16]), ALU.mult)
            dve.drain().then_inc(S("aff"), 1)
            b = x_ready(dve, "affT")
            dve.memset(ones16, 1.0)
            read(dve.tensor_copy(wk, b[0:16, 0:T]))
            for _ in range(CAP // 8):
                dve.drain()
                dve.max(top8, wk)
                dve.drain()
                dve.match_replace(wk, top8, wk, -1.0)
            dve.drain()
            dve.tensor_scalar(msk, wk, 0.0, None, ALU.is_lt)
            dve.drain()
            dve.tensor_tensor_scan(slotT, ones16, msk, 0.0, ALU.mult, ALU.add)
            dve.drain()
            tt_(slotT, slotT, msk, ALU.mult)
            dve.drain().then_inc(S("slotT"), 1)
            b = x_ready(dve, "slot_tr")[:, 0:32].rearrange("p (t e) -> p t e", t=TT)
            read(dve.tensor_copy(slots, b))
            dve.drain()
            for tt in range(TT):
                tt_(onehot[:, tt, :, :], cst("iota", CAP).unsqueeze(1).broadcast_to([P, EXPERTS, CAP]),
                    slots[:, tt, :].unsqueeze(2).broadcast_to([P, EXPERTS, CAP]), ALU.is_equal)
            dve.drain()
            for tt in range(TT):
                for j in range(4):
                    tt_(weighted[:, tt, :, j * CAP:(j + 1) * CAP], onehot[:, tt, :, :],
                        aff[:, tt, :].unsqueeze(2).broadcast_to([P, EXPERTS, CAP]), ALU.mult)
            dve.drain().then_inc(S("weighted"), 1)
            for i in range(8):
                b = x_ready(dve, "xe", i)
                read(dve.tensor_copy(xe[:, i, :], b[:, :]))
            dve.drain()
            with dve.Fori(0, EXPERTS) as e:
                dve.wait_ge(slots_done, 24 * e + (MOE - 8))
                dve.tensor_copy(xs, xe[:, :, bass.ds(e * CAP, CAP)]).then_inc(S("xs_ready"), 1)
                dve.wait_ge(slots_done, 24 * e + MOE + 16)
                dve.wait_ge(S("sg_e"), e + 1)
                tt_(act_e, psd[1][:, :], sg_e, ALU.mult).then_inc(S("act_e"), 1)
                dve.wait_ge(slots_done, 24 * e + MOE + 24)
                dve.tensor_copy(ye[:, 1, :], psd[3][:, :]).then_inc(S("ye_ready"), 1)
            for i in range(4):
                b = m2(x_ready(dve, "moe_acc", i))
                read(dve.tensor_copy(x[:, 2 * i:2 * i + 2, :], b))
            x_event()
            barrier(dve, "merge")
            norm("g_final", x)
            x_event()

            for l in range(LAYERS):
                norm(f"norm_ffn1{l}", h)
                ffn("ffn1", l)
                barrier(dve, f"ffn1{l}")
                norm(f"norm_mix{l}", h)

                XB.was_read(dve, ("qk_norm", l, 2))
                dve.reciprocal(rs6, rs6)
                dve.drain()
                for j in range(6):
                    g = pc(f"b_{'q' if j < 3 else 'k'}_gain{l}")
                    dve.scalar_tensor_tensor(out=pb[:, 10 + j, :], in0=pb[:, 10 + j, :], scalar=g, in1=rs6[:, j, :],
                                             op0=ALU.mult, op1=ALU.mult)
                dve.drain().then_inc(S("qk_ready"), 1)
                dve.memset(up[:, :, 0:16], 0.0)
                dve.tensor_copy(up[:, :, 16:16 + T], pb[:, 19:21, :])
                dve.drain()
                src, start = up, 0
                for step, dst in ((1, wa), (2, wb), (4, wa), (8, wb)):
                    start += step
                    tt_(dst[:, :, start:], src[:, :, start:], src[:, :, start - step:16 + T - step], ALU.add)
                    dve.drain()
                    tile, half = ((0, 0), (0, 1), (1, 0), (1, 1))[int(math.log2(step))]
                    r = slice(64 * half, 64 * half + 64)
                    inv_n = con[r, CCOL["invcnt"] + tile * T:CCOL["invcnt"] + (tile + 1) * T]
                    tt_(sq[r, 6 + tile, :], dst[r, tile, 16:16 + T], inv_n, ALU.mult)
                    src = dst
                dve.drain()
                tt_(up[:, :, 16:16 + T], sq[:, 6:8, :], up[:, :, 16:16 + T], ALU.subtract)
                dve.drain().then_inc(S("pooled"), 1)
                dve.wait_ge(S(f"att_in{l}"), 32)
                for hd in range(6):
                    for it, (lo_, hi_) in enumerate(((0, P), (P, AW))):
                        b = x_ready(dve, "score", l, hd, it)
                        pr = prob[:, hd, lo_:hi_]
                        read(dve.scalar_tensor_tensor(out=pr, in0=b[:, 0:hi_ - lo_], scalar=64 ** -0.5,
                                                      in1=rbias[:, hd, lo_:hi_], op0=ALU.mult, op1=ALU.add))
                        dve.drain()
                        dve.tensor_reduce(tiny[:, 24 + 2 * hd + it:25 + 2 * hd + it], pr, AXX, ALU.max)
                    dve.drain()
                    dve.tensor_scalar(tiny[:, 2 * hd:2 * hd + 2], tiny[:, 24 + 2 * hd:26 + 2 * hd], -1.0, None, ALU.mult)
                    dve.drain().then_inc(S("score_max"), 1)
                for hd in range(6):
                    dve.wait_ge(S("score_exp"), 6 * l + hd + 1)
                    dve.reciprocal(tiny[:, 40 + 2 * hd:42 + 2 * hd], tiny[:, 12 + 2 * hd:14 + 2 * hd])
                    dve.drain()
                    for it, (lo_, hi_) in enumerate(((0, P), (P, AW))):
                        j = 40 + 2 * hd + it
                        dve.tensor_scalar(prob[:, hd, lo_:hi_], prob[:, hd, lo_:hi_], tiny[:, j:j + 1], None, ALU.mult)
                    dve.drain().then_inc(S("prob"), 1)
                barrier(dve, f"att{l}")

                mu = par[:, PCOL[f"a_mu{l}"]:PCOL[f"a_mu{l}"] + 10]
                dve.tensor_scalar(tiny[:, 0:10], mu, -1.0, 1.0, ALU.mult, ALU.add)
                dve.memset(MT, 0.0)
                dve.drain()
                for j in range(10):
                    dve.tensor_scalar(ts[:, j, :], pb[:, j, :], tiny[:, j:j + 1], None, ALU.mult)
                dve.drain()
                for j in range(10):
                    dve.scalar_tensor_tensor(out=ts[:, j, 1:T], in0=pb[:, j, 0:T - 1], scalar=mu[:, j:j + 1],
                                             in1=ts[:, j, 1:T], op0=ALU.mult, op1=ALU.add)
                dve.drain().then_inc(S("shifted"), 1)
                r_, k_, v_ = ts[:, 0:3, :], ts[:, 3:6, :], ts[:, 6:9, :]
                for j in range(HP):
                    dve.tensor_scalar(kk[:, j, :], k_[:, j, :], pc(f"a_k_k{l}", j), None, ALU.mult)
                dve.drain().then_inc(S("kk_raw"), 1)
                XB.was_read(dve, ("lora", l, 0, 1))
                dve.tensor_scalar(rt[:, :, :], rt[:, :, :], -math.exp(-0.5), None, ALU.mult)
                dve.drain()
                for j in range(HP):
                    dve.tensor_tensor_scan(kt[:, j, :], cst("reset", T), rt[:, j, :], 0.0, ALU.mult, ALU.add)
                if l:
                    XB.was_read(dve, ("vup", l, 1))
                    tt_(v_first[:, :, :], v_first[:, :, :], v_, ALU.subtract)
                    dve.drain()
                    tt_(v_first[:, :, :], v_first[:, :, :], be[:, :, :], ALU.mult)
                    dve.drain()
                    tt_(v_, v_, v_first[:, :, :], ALU.add)
                else:
                    dve.tensor_copy(v_first[:, :, :], v_)
                dve.drain()
                tt_(be[:, :, :], kt[:, :, :], rt[:, :, :], ALU.subtract)
                dve.drain().then_inc(S("decays"), 1)
                XB.was_read(dve, ("lora", l, 2, 1))
                XB.was_read(dve, ("kk_norm", l, 1))
                dve.tensor_scalar(al[:, :, :], al[:, :, :], 1e-12, None, ALU.max)
                for j in range(HP):
                    dve.tensor_scalar(rt[:, j, :], aa[:, j, :], -1.0, pc(f"a_k_a{l}", j), ALU.add, ALU.mult)
                dve.drain()
                dve.reciprocal(al[:, :, :], al[:, :, :])
                dve.scalar_tensor_tensor(out=k_, in0=rt[:, :, :], scalar=1.0, in1=k_, op0=ALU.add, op1=ALU.mult)
                dve.drain()
                tt_(kk, kk, al[:, :, :], ALU.mult)
                dve.wait_ge(S("decay_exp"), l + 1)
                dve.drain()
                dve.scalar_tensor_tensor(out=al[:, :, :], in0=kk, scalar=-1.0, in1=e3, op0=ALU.mult, op1=ALU.mult)
                tt_(be[:, :, :], kk, aa, ALU.mult)
                tt_(rt[:, :, :], r_, e1, ALU.mult)
                tt_(kt[:, :, :], k_, e2, ALU.mult)
                dve.drain()
                tt_(be[:, :, :], be[:, :, :], e2, ALU.mult)
                dve.drain().then_inc(S("rw_scaled"), 1)

                rows = [slice(64 * p, 64 * p + 64) for p in range(2)]
                for tt in range(TT):
                    tok = slice(tt * P, (tt + 1) * P)
                    b = tri(x_ready(dve, "rw_tr", l, tt, "b"))
                    for c in range(4):
                        ins = dve.tensor_scalar(bm[:, :, c, :], b, con[:, CCOL["chunk"] + c:CCOL["chunk"] + c + 1],
                                                None, ALU.mult)
                    read(ins)

                    def mask(name):
                        return cst(name, P).unsqueeze(1).broadcast_to([P, HP, P])

                    for name, kinds in (("A", (("Aoff", "off32"), ("A", "low16"))), ("AT", (("AT", "up16"),)),
                                        ("BT", (("BT", "up32"),)), ("CT", (("CT", "upi32"),)),
                                        ("DT", (("DT", "upi32"),))):
                        for p in range(2):
                            b = tri(x_ready(dve, name, l, tt, p))
                            if name == "BT" and p == 0:
                                dve.drain()
                                for pp in range(2):
                                    tt_(MATS["Q"][pp], MATS["AT"][pp], mask("ident"), ALU.add)
                            for dst, mk in kinds:
                                ins = tt_(MATS[dst][p], b, mask(mk), ALU.mult)
                            read(ins)
                    for name in ("Q2", "Q4", "Q8", "Q32"):
                        dve.drain()
                        for p in range(2):
                            b = tri(x_ready(dve, name, l, tt, p))
                            read(tt_(MATS["Q"][p], b, MATS["Q"][p], ALU.add))
                    for q in range(HP):
                        b = x_ready(dve, "M", l, tt, q)
                        for p in range(2):
                            ins = tt_(MT[rows[p], :, q, rows[p]],
                                      b[rows[p], 0:T].rearrange("p (c n) -> p c n", c=4),
                                      ident[rows[p], rows[p]].unsqueeze(1).broadcast_to([64, 4, 64]), ALU.add)
                        read(ins)
                        ends = e1[:, q, tt * P + CH - 1:(tt + 1) * P:CH]
                        b = x_ready(dve, "N", l, tt, q)
                        read(tt_(Np[:, :, q, :], b[:, 0:T].rearrange("p (c n) -> p c n", c=4),
                                 ends.unsqueeze(2).broadcast_to([P, 4, 64]), ALU.mult))
                        b = x_ready(dve, "RY", l, tt, q)
                        tt_(RT[:, q, :], b[:, 0:P], rt[:, q, tok], ALU.add)
                        read(dve.tensor_copy(y0T[:, q, :], b[:, P:T]))
                    if tt == 0:
                        dve.memset(Xs[:, 0, :, :], 0.0)
                    else:
                        dve.tensor_copy(Xs[:, 0, :, :], Xs[:, 4, :, :])
                    dve.drain().then_inc(S("state0"), 1)
                    for c in range(4):
                        b = tri(x_ready(dve, "S", l, tt, c), 64)
                        for q in range(HP):
                            end = tt * P + (c + 1) * CH - 1
                            ins = dve.scalar_tensor_tensor(out=Xs[:, c + 1, q, :], in0=b[:, q, :],
                                                           scalar=e1[:, q, end:end + 1], in1=Np[:, c, q, :],
                                                           op0=ALU.mult, op1=ALU.add)
                        read(ins)
                    for p in range(2):
                        b = tri(x_ready(dve, "y", l, tt, p))
                        read(tt_(yy[rows[p], :, tok], b[rows[p], :, :], y0T[rows[p], :, :], ALU.add))
                    dve.drain()
                dve.drain().then_inc(S("y_ready"), 1)
                for i in range(2):
                    b, m = m2(x_ready(dve, "mean", l, i)), 2 - i
                    yv = yy[:, 2 * i:2 * i + m, :]
                    read(dve.scalar_tensor_tensor(out=yv, in0=b[:, 0:m, :], scalar=-1.0 / 64, in1=yv,
                                                  op0=ALU.mult, op1=ALU.add))
                dve.drain().then_inc(S("y_mean"), 1)
                for j in range(HP):
                    dve.scalar_tensor_tensor(out=e1[:, j, :], in0=r_[:, j, :], scalar=pc(f"a_r_k{l}", j),
                                             in1=k_[:, j, :], op0=ALU.mult, op1=ALU.mult)
                dve.drain().then_inc(S("rk_ready"), 1)
                XB.was_read(dve, ("var", l, 1))
                dve.reciprocal(al[:, :, :], al[:, :, :])
                dve.drain()
                tt_(yy, yy, al[:, :, :], ALU.mult)
                dve.drain()
                for j in range(HP):
                    dve.tensor_scalar(yy[:, j, :], yy[:, j, :], pc(f"a_gn_g{l}", j), pc(f"a_gn_b{l}", j),
                                      ALU.mult, ALU.add)
                for i in range(2):
                    b, m = m2(x_ready(dve, "bonus", l, i)), 2 - i
                    two = slice(2 * i, 2 * i + m)
                    read(tt_(e2[:, two, :], b[:, 0:m, :], v_[:, two, :], ALU.mult))
                dve.drain()
                tt_(yy, yy, e2, ALU.add)
                dve.drain()
                tt_(ycat[:, 0:3, :], yy, gg, ALU.mult)
                dve.drain().then_inc(S("mix_cat"), 1)
                for i in range(4):
                    b = m2(d_ready(dve, (("mix_out", l), i)))
                    two = slice(2 * i, 2 * i + 2)
                    dread(tt_(x[:, two, :], b, x[:, two, :], ALU.add))
                x_event()
                barrier(dve, f"rwkv{l}")

                norm(f"norm_mem{l}", mn, memT)
                norm(f"norm_cross{l}", h)
                for j, (name, v) in enumerate((("k", xk), ("q", xq))):
                    XB.was_read(dve, ("xnorm", l, name, 1))
                    rs4 = memT[:, 4 * j:4 * j + 4, :]
                    dve.reciprocal(rs4, rs4)
                    dve.drain()
                    for c in range(KD):
                        dve.scalar_tensor_tensor(out=v[:, c, :], in0=v[:, c, :], scalar=pc(f"x_{name}_gain{l}", c % 2),
                                                 in1=rs4[:, c // 2, :], op0=ALU.mult, op1=ALU.mult)
                dve.drain().then_inc(S("xqk_ready"), 1)
                for hd in range(4):
                    for it in range(TT):
                        j = 2 * hd + it
                        b = x_ready(dve, "xscore", l, hd, it)
                        read(dve.tensor_scalar(xprob[:, j, :], b[:, 0:T], 1.0 / 16, None, ALU.mult))
                        dve.drain()
                        dve.tensor_reduce(tiny[:, 24 + j:25 + j], xprob[:, j, :], AXX, ALU.max)
                    dve.drain()
                    dve.tensor_scalar(tiny[:, 2 * hd:2 * hd + 2], tiny[:, 24 + 2 * hd:26 + 2 * hd], -1.0, None, ALU.mult)
                    dve.drain().then_inc(S("xscore_max"), 1)
                for hd in range(4):
                    dve.wait_ge(S("xscore_exp"), 4 * l + hd + 1)
                    dve.reciprocal(tiny[:, 40 + 2 * hd:42 + 2 * hd], tiny[:, 12 + 2 * hd:14 + 2 * hd])
                    dve.drain()
                    for it in range(TT):
                        j = 2 * hd + it
                        dve.tensor_scalar(xprob[:, j, :], xprob[:, j, :], tiny[:, 40 + j:41 + j], None, ALU.mult)
                    dve.drain().then_inc(S("xprob"), 1)
                for i in range(4):
                    b = m2(d_ready(dve, (("x_o", l), i)))
                    two = slice(2 * i, 2 * i + 2)
                    dread(tt_(x[:, two, :], b, x[:, two, :], ALU.add))
                x_event()
                barrier(dve, f"cross{l}")
                norm(f"norm_ffn2{l}", h)
                ffn("ffn2", l)
                barrier(dve, f"ffn2{l}")

        @block.gpsimd
        def _(pool):
            def load(dst, src, flag):
                pool.dma_start(dst, src).then_inc(S(flag), 16)

            load(bd[:, :, :, :], A["lru_bd"].rearrange("p (s c n) -> p s c n", s=4, c=KD), "bd_in")
            barrier(pool, "lru")
            load(at(0, 8 * T), A["dft"], "dft_in")
            load(sq[0:33, 0, :], A["zT"], "filt_in")
            load(filt_w[0:33, 0:64], A["filt_w1"], "filt_in")
            load(filt_w[0:64, 64:128], A["filt_w2"], "filt_in")
            load(decay[:, 1, :], A["deltas"].broadcast_to([P, D]), "filt_in")
            load(at(8, 2 * D, parts=1), A["filt_bias"], "bias_in")
            w3 = A["filt_w3"].rearrange("i (n d h c) -> n i d h c", n=2, d=2, h=2)
            load(w3h[:, :, :, :], w3[0], "w3_in0")
            x_ready(pool, "taps", 0, 1, 1, 1)
            load(w3h[:, :, :, :], w3[1], "w3_in1")
            barrier(pool, "conv")
            load(wr[:, :, :], A["w_router"].rearrange("(k p) e -> p k e", p=P), "wr_in")
            barrier(pool, "merge")
            for l in range(LAYERS):
                barrier(pool, f"ffn1{l}")
                load(rbias[:, :, :], A["rel_bias"][l].rearrange("p (h n) -> p h n", h=6), f"att_in{l}")
                load(poolw[:, :, :], A["pool_w"][l].rearrange("p (m n) -> p m n", m=2), f"att_in{l}")
                barrier(pool, f"att{l}")
                load(lora_up, A["lora_up"][l], f"lora_in{l}")
                if l:
                    load(vdn[:, :, :], A["a_v_down"].rearrange("(q p) n -> p q n", p=P), f"lora_in{l}")
                    load(vup, A["a_v_up"], f"lora_in{l}")
                barrier(pool, f"rwkv{l}")
                load(memT[:, :, :], A["memT"].rearrange("(k p) t -> p k t", p=P), "mem_in")
                barrier(pool, f"cross{l}")
                barrier(pool, f"ffn2{l}")

        @block.sync
        def _(sp):
            def slot(n, src, words=SLOT):
                if n >= RING:
                    sp.wait_ge(slots_done, n - RING + 1)
                sp.dma_start(ring[n % RING][:, 0:words], src).then_inc(land[n % RING], 16)

            for n, (_, _, name, i) in enumerate(plan):
                slot(n, A[name][i])
            with sp.Fori(0, EXPERTS) as e:
                for s in range(24):
                    n = MOE + s
                    sp.wait_ge(slots_done, 24 * e + (n - RING + 1))
                    if s < 16:
                        src = A["w_gate" if s < 8 else "w_up"][bass.ds(8 * e + s % 8, 1), :, :]
                        src = src.rearrange("a p c -> (a p) c")
                        dst = ring[n % RING][:, :]
                    else:
                        src = A["w_down"][bass.ds(8 * e + s - 16, 1), :, :, :].rearrange("a i p c -> p (a i) c")
                        dst = ring[n % RING][:, :].rearrange("p (i c) -> p i c", i=2)
                    sp.dma_start(dst, src).then_inc(land[n % RING], 16)
            for m, (_, _, name, (l, i)) in enumerate(after):
                n = AFTER + m
                sp.wait_ge(slots_done, n - RING + 1)
                src, words = A[name][l, i], SLOT
                dst = ring[n % RING][:, :]
                if name.endswith("_wo") and name.startswith("ffn"):
                    src = src.rearrange("i p c -> p i c")
                    dst = dst.rearrange("p (i c) -> p i c", i=2)
                elif name == "mix_in" and i == 10:
                    src, dst = src[:, 0:KD * P], dst[:, 0:KD * P]
                sp.dma_start(dst, src).then_inc(land[n % RING], 16)
            sp.wait_ge(x_ready_s, len(XEV))
            sp.dma_start(out.rearrange("(k p) t -> p k t", p=P), x[:, :, :]).then_inc(S("out_stored"), 16)
            sp.wait_ge(S("out_stored"), 16)


def kernel(**inputs):
    import concourse.bacc as bacc
    from concourse.bass_utils import run_bass_kernel_spmd

    a = {k: np.asarray(v) for k, v in inputs.items()}

    def tiles(w):
        f = w.shape[1] // 256
        return np.ascontiguousarray(w.reshape(KD, P, f, 256).transpose(2, 1, 0, 3)).reshape(f, P, SLOT)

    def columns(v, n):
        v = v.reshape(-1)
        v = np.concatenate([v.reshape(-1, 64)] * 2, axis=1).reshape(-1, P) if v.size in (64, 128) and n * P > v.size \
            else v.reshape(-1, P)
        assert v.shape[0] == n
        return v.T

    PCOL, npc = param_columns()
    params = np.zeros((P, npc), np.float32)
    order = sorted(PCOL, key=PCOL.get)
    for name, nxt in zip(order, order[1:] + [None]):
        n = (PCOL[nxt] if nxt else npc) - PCOL[name]
        if name in a:
            v = a[name]
        elif name == "a_v0":
            v = a["a_v0_2"]
        else:
            v = a[name[:-1] + "_2"][int(name[-1])]
        params[:, PCOL[name]:PCOL[name] + n] = columns(v, n)

    bd = np.zeros((2, 64, 2, 2, KD, 2, 64), np.float32)
    pw = np.zeros((LAYERS, 2, 64, 2, 2, 64), np.float32)
    for half in range(2):
        for kind, name in enumerate(("lru_w_r", "lru_w_i")):
            w = a[name][0].reshape(2, KD, 2, 64, 64)[:, :, half]
            bd[half, :, :, kind, :, half, :] = w.transpose(2, 0, 1, 3)
        pw[:, half, :, :, half, :] = a["c_pool_w_2"].reshape(LAYERS, 2, 2, 64, 64)[:, :, half].transpose(0, 2, 1, 3)

    i, j = np.arange(T)[:, None], np.arange(T)[None, :]
    rel = a["b_rel_bias_2"][:, :, np.clip(i - j, -63, 256) + 63]
    rel = np.where((i // 64 >= j // 64)[None, None], rel, np.float32(-1e30))
    rel = np.concatenate([rel[:, :, 0:P, 0:P], rel[:, :, P:T, :]], axis=3).transpose(0, 2, 1, 3)

    feed = {
        "xT": a["x"][0].T, "memT": a["mem_2"][0].T, "params": params,
        "w_in": tiles(a["w_in"][0]), "w_a_out": tiles(a["w_a_out"][0]), "w_b_out": tiles(a["w_b_out"][0]),
        "w_o": tiles(a["w_o"][0]),
        "lru_bd": bd.reshape(P, -1), "filt_w1": a["filt_w1"][0], "filt_w2": a["filt_w2"][0],
        "filt_w3": a["filt_w3"][0], "filt_bias": a["filt_bias"].reshape(1, 2 * D),
        "w_router": a["w_router"][0],
        "w_gate": a["w_gate"].reshape(EXPERTS * KD, P, FE), "w_up": a["w_up"].reshape(EXPERTS * KD, P, FE),
        "w_down": a["w_down"].reshape(EXPERTS * 8, 2, P, D),
        "mix_in": np.stack([np.concatenate(
            [tiles(w[:, 0:2560]), np.pad(w[:, 2560:].reshape(KD, P, P).transpose(1, 0, 2).reshape(1, P, KD * P),
                                         ((0, 0), (0, 0), (0, SLOT - KD * P)))]) for w in a["w_in_2"]]),
        "mix_out": np.stack([tiles(w) for w in a["w_out_2"]]),
        "x_wkv": np.stack([tiles(w) for w in a["x_wkv_2"]]),
        "x_wq": np.stack([tiles(w) for w in a["x_wq_2"]]),
        "x_wo": np.stack([tiles(w) for w in a["x_wo_2"]]),
        "rel_bias": rel.reshape(LAYERS, P, 6 * 384), "pool_w": pw.reshape(LAYERS, P, 2 * P),
        "lora_up": np.concatenate([a["a_w_up_2"], a["a_a_up_2"], a["a_g_up_2"]], axis=1),
        "a_v_down": a["a_v_down_2"][0], "a_v_up": a["a_v_up_2"][0],
    }
    for which in ("ffn1", "ffn2"):
        feed[f"{which}_wi"] = np.stack([tiles(w) for w in a[f"{which}_wi_2"]])
        feed[f"{which}_wo"] = a[f"{which}_wo_2"].reshape(LAYERS, FSTEPS, 2, P, D)
    feed.update(constants())

    nc = bacc.Bacc("TRN2", target_bir_lowering=False, num_devices=1)
    A, arrays = {}, {}
    for name, v in feed.items():
        arrays[f"in_{name}"] = np.ascontiguousarray(v)
        A[name] = nc.dram_tensor(f"in_{name}", v.shape, F32, kind="ExternalInput").ap()
    out = nc.dram_tensor("out_x", (D, T), F32, kind="ExternalOutput").ap()
    program(nc, A, out)
    r = run_bass_kernel_spmd(nc, [arrays], core_ids=[0])
    return np.ascontiguousarray(r.results[0]["out_x"].T)[None]
```

```python
import math
from contextlib import ExitStack

import numpy as np

import concourse.bass as bass
from concourse import mybir

F32 = mybir.dt.float32
F32R = mybir.dt.float32r
ALU = mybir.AluOpType
ACT = mybir.ActivationFunctionType
AXX = mybir.AxisListType.X

P = 128
T = 256
TT = T // P
D = 1024
KD = D // P
SLOT = 2048
RING = 4
EXPERTS, CAP, FE = 16, 32, 2048
EPS = 1e-6
LAYERS = 2
FF = 2816
FSTEPS = FF // 256
AW = 384
HP = AW // P
NPB = 21
CH = 32
SUB = 16
GN_EPS = 64e-5
L2 = 1.5 * 2.0 ** 23
TWO_PI_HI, TWO_PI_LO = 6.28125, 2 * math.pi - 6.28125


def param_columns():
    cols, at = {}, 0
    sizes = [("g_mix", 8), ("conv_a_w", 32), ("conv_a_b", 8), ("lru_b_r", 16), ("lru_b_i", 16),
             ("lru_lambda", 16), ("conv_b_w", 72), ("conv_b_b", 24), ("filt_b1", 1), ("filt_b2", 1),
             ("filt_freq", 2), ("g_ffn", 8), ("g_final", 8)]
    for l in range(LAYERS):
        sizes += [(f"{n}{l}", c) for n, c in (
            ("norm_ffn1", 8), ("norm_mix", 8), ("a_mu", 10), ("a_w0", 3), ("a_a0", 3), ("a_k_k", 3),
            ("a_k_a", 3), ("a_r_k", 3), ("a_gn_g", 3), ("a_gn_b", 3), ("b_q_gain", 1), ("b_k_gain", 1),
            ("c_pool_scale", 2), ("norm_cross", 8), ("norm_mem", 8), ("x_q_gain", 2), ("x_k_gain", 2),
            ("norm_ffn2", 8))]
    sizes += [("a_v0", 3)]
    for n, c in sizes:
        cols[n] = at
        at += c
    return cols, at


def constant_columns():
    cols, at = {}, 0
    for n, c in (("ident", 128), ("ones", 128), ("bones", 128), ("low16", 128), ("up16", 128),
                 ("off32", 128), ("up32", 128), ("upi32", 128), ("iota", 32), ("chunk", 4),
                 ("reset", 256), ("invcnt", 512), ("eps", 1), ("gneps", 1), ("negt", 2)):
        cols[n] = at
        at += c
    return cols, at


def constants():
    cols, n = constant_columns()
    c = np.zeros((P, n), np.float32)
    i = np.arange(P)[:, None]
    j = np.arange(P)[None, :]

    def put(name, a):
        c[:, cols[name]:cols[name] + a.shape[1]] = a

    put("ident", np.eye(P))
    put("ones", np.ones((P, P)))
    put("bones", (i // 64 == j // 64) * 1.0)
    put("low16", ((i // SUB == j // SUB) & (j < i)) * 1.0)
    put("up16", ((i // SUB == j // SUB) & (j > i)) * 1.0)
    put("off32", ((i // CH == j // CH) & (i // SUB > j // SUB)) * 1.0)
    put("up32", ((i // CH == j // CH) & (j > i)) * 1.0)
    put("upi32", ((i // CH == j // CH) & (j >= i)) * 1.0)
    put("iota", np.ones((P, 1)) * np.arange(1, CAP + 1)[None, :])
    put("chunk", (i // CH == np.arange(4)[None, :]) * 1.0)
    t = np.arange(T)[None, :]
    put("reset", np.ones((P, 1)) * (t % CH != 0))
    wins = np.array([[2, 8], [4, 16]])
    inv = np.zeros((P, 2, T))
    for half in range(2):
        for tile in range(2):
            inv[64 * half:64 * half + 64, tile] = 1.0 / np.minimum(t + 1, wins[half, tile])
    put("invcnt", inv.reshape(P, 512))
    put("eps", np.full((P, 1), EPS))
    put("gneps", np.full((P, 1), GN_EPS))
    put("negt", -(i + P * np.arange(2)[None, :]) / (T - 1.0))
    m = np.arange(T, dtype=np.float64)
    th = np.pi * (2 * m + 1) / (2 * T)
    ang = np.arange(T)[:, None] * th[None, :]
    fwd = np.concatenate([np.cos(ang), -np.sin(ang)], axis=1)
    inv = np.concatenate([np.cos(ang).T, -np.sin(ang).T], axis=0) / T
    dft = np.concatenate([fwd.reshape(2, P, 2 * T).transpose(1, 0, 2).reshape(P, 4 * T),
                          inv.reshape(4, P, T).transpose(1, 0, 2).reshape(P, 4 * T)], axis=1)
    f4 = np.float32
    tt = np.linspace(0.0, 1.0, T, dtype=f4)[:, None]
    w = f4(2.0 * math.pi / T) * np.arange(T, dtype=f4)[:, None]
    f = np.linspace(1e-4, 15, 16, dtype=f4)[None, :]
    z = np.concatenate([tt, np.cos(w * f), -np.sin(w * f)], axis=-1)
    lo, hi = math.log(1e-2) / 1.5, math.log(1e-2) / 0.3
    deltas = np.abs(np.linspace(lo, hi, D, dtype=f4))[None, :]
    return {"consts": c, "dft": dft.astype(f4), "zT": np.ascontiguousarray(z.T.astype(f4)), "deltas": deltas.astype(f4)}


def stream_plan():
    plan = []
    for part, first, count in (("a_x", 0, 4), ("hy_v", 8, 4), ("hy_x1", 12, 4), ("hy_x2", 16, 4),
                               ("a_gate", 4, 4), ("gates", 20, 8)):
        plan += [(part, i, "w_in", first + i) for i in range(count)]
    for part in ("w_a_out", "w_b_out", "w_o"):
        plan += [(part, i, part, i) for i in range(4)]
    moe = len(plan)
    after = []

    def ffn(l, which):
        for f in range(FSTEPS + 1):
            if f < FSTEPS:
                after.append(((which, l, "gate", f), f, f"{which}_wi", (l, f)))
                after.append(((which, l, "up", f), f, f"{which}_wi", (l, FSTEPS + f)))
            if f:
                after.append(((which, l, "down", f - 1), f - 1, f"{which}_wo", (l, f - 1)))

    for l in range(LAYERS):
        ffn(l, "ffn1")
        after += [(("mix_in", l), i, "mix_in", (l, i)) for i in range(11)]
        after += [(("mix_out", l), i, "mix_out", (l, i)) for i in range(4)]
        after += [(("x_k", l), i, "x_wkv", (l, i)) for i in range(4)]
        after += [(("x_v", l), i, "x_wkv", (l, 4 + i)) for i in range(4)]
        after += [(("x_q", l), i, "x_wq", (l, i)) for i in range(4)]
        after += [(("x_o", l), i, "x_wo", (l, i)) for i in range(4)]
        ffn(l, "ffn2")
    return plan, moe, after


class Banks:

    def __init__(self, plan, banks, sems):
        self.banks, self.sems, self.reader, self.count, self.at = banks, sems, [], [], {}
        seen = {"act": 0, "dve": 0, None: 0}
        for g, (key, reader) in enumerate(plan):
            seen[reader] += 1
            self.at[key] = g
            self.reader.append(reader)
            self.count.append(seen[reader])
        self.next = 0

    def bank(self, key):
        return self.banks[self.at[key] % 4]

    def was_read(self, eng, key):
        g = self.at[key]
        eng.wait_ge(self.sems[self.reader[g]], self.count[g])

    def claim(self, pe, key):
        g = self.at[key]
        assert g == self.next, (key, g, self.next)
        self.next += 1
        if g >= 4 and self.reader[g - 4]:
            pe.wait_ge(self.sems[self.reader[g - 4]], self.count[g - 4])
        return self.banks[g % 4]


def dense_plan():
    plan = []
    for part, count, reader in (("a_x", 4, "dve"), ("hy_v", 4, "dve"), ("hy_x1", 4, "dve"), ("hy_x2", 4, "dve"),
                                ("a_gate", 4, "act"), ("gates", 8, "act"),
                                ("w_a_out", 4, "dve"), ("w_b_out", 4, "dve"), ("w_o", 4, "dve")):
        plan += [((part, i), reader) for i in range(count)]
    plan += [(("moe", i), None) for i in range(4)]

    def ffn(l, which):
        for f in range(FSTEPS):
            plan.append(((which, l, "gate", f), "act"))
            plan.append(((which, l, "up", f), "dve"))

    for l in range(LAYERS):
        ffn(l, "ffn1")
        for part, count, reader in (("mix_in", 11, "act"), ("mix_out", 4, "dve"), ("x_k", 4, "act"),
                                    ("x_v", 4, "act"), ("x_q", 4, "act"), ("x_o", 4, "dve")):
            plan += [(((part, l), i), reader) for i in range(count)]
        ffn(l, "ffn2")
    return plan


def small_plan():
    plan = []

    def add(reader, *key):
        plan.append((key, reader))

    add("act", "norm", "g_mix")
    for part in ("v", "x1"):
        for i in range(4):
            add("act", "hy_tr", part, i)
    for d in range(2):
        for kind in range(2):
            for i in range(4):
                add("act", "lru", d, kind, i)
    add("dve", "filt", 0)
    add("dve", "filt", 1)
    for n in range(2):
        for tt in range(TT):
            for half in range(2):
                for d in range(2):
                    add("dve", "taps", n, tt, half, d)
        for m in range(4):
            for half in range(2):
                add("act", "spec_k", n, m, half)
        for half in range(2):
            for f in range(2):
                for im in range(2):
                    add("dve", "spec_u", n, half, f, im)
        for i in range(4):
            add("dve", "inv", n, i)
    add("act", "norm", "g_ffn")
    add("dve", "router")
    for tt in range(TT):
        for i in range(2):
            add("act", "h_tok", tt, i)
    add("dve", "affT")
    add("dve", "slot_tr")
    for i in range(8):
        add("act", "PT", i)
    for i in range(8):
        add("dve", "xe", i)
    for i in range(4):
        add("dve", "moe_acc", i)
    add("act", "norm", "g_final")
    for l in range(LAYERS):
        add("act", "norm", f"norm_ffn1{l}")
        for i in range(4):
            add("dve", "ffn1", l, i)
        add("act", "norm", f"norm_mix{l}")
        for i in range(3):
            add("act", "qk_norm", l, i)
        add("act", "av_tr", l, 0)
        add("act", "av_tr", l, 1)
        for h in range(6):
            for it in range(2):
                add("dve", "score", l, h, it)
        for h in range(6):
            add("act", "prob_tr", l, h)
        for q in range(HP):
            add("act", "att", l, q)
        add("act", "pool", l)
        for kind in range(3):
            for i in range(2):
                add("act", "lora", l, kind, i)
        if l:
            add("act", "vdown", l)
            for i in range(2):
                add("act", "vup", l, i)
        for i in range(2):
            add("act", "kk_norm", l, i)
        for tt in range(TT):
            for x in "abkv":
                add("dve" if x == "b" else "act", "rw_tr", l, tt, x)
            for x, r in (("A", "dve"), ("AT", "dve"), ("BT", "dve"), ("CT", "dve"), ("DT", "dve"),
                         ("P2", "act"), ("P2T", "act"), ("Q2", "dve"), ("P4", "act"), ("P4T", "act"), ("Q4", "dve"),
                         ("P8", "act"), ("Q8", "dve"), ("TR", "act"), ("X1", "act"), ("Q32", "dve"),
                         ("BV", "act"), ("WU", "act")):
                for p in range(2):
                    add(r, x, l, tt, p)
            for q in range(HP):
                add("dve", "M", l, tt, q)
                add("dve", "N", l, tt, q)
                add("dve", "RY", l, tt, q)
            for c in range(4):
                add("dve", "S", l, tt, c)
            for p in range(2):
                add("dve", "y", l, tt, p)
        for x, r in (("mean", "dve"), ("var", "act"), ("bonus", "dve")):
            for i in range(2):
                add(r, x, l, i)
        add("act", "norm", f"norm_mem{l}")
        add("act", "norm", f"norm_cross{l}")
        for x in "kq":
            for i in range(2):
                add("act", "xnorm", l, x, i)
        for h in range(4):
            for it in range(2):
                add("dve", "xscore", l, h, it)
        for h in range(4):
            add("act", "xprob_tr", l, h)
        for h in range(4):
            add("dve", "xatt", l, h)
        add("act", "norm", f"norm_ffn2{l}")
        for i in range(4):
            add("dve", "ffn2", l, i)
    return plan


def program(nc, A, out):
    ctx = ExitStack()
    with ctx:
        def sb(name, shape, dt=F32):
            return ctx.enter_context(nc.sbuf_tensor(name, shape, dt))

        def shared(name, words, parts):
            with nc.sbuf_tensor(name, [P, words], F32) as whole:
                pass
            return [whole] + [sb(n, shape, F32R) for n, shape in parts]

        sems = {}

        def S(name):
            if name not in sems:
                sems[name] = ctx.enter_context(nc.semaphore(name))
            return sems[name]

        PCOL, npc = param_columns()
        CCOL, ncc = constant_columns()
        par = sb("par", [P, npc])
        con = sb("con", [P, ncc])
        ring = [sb(f"ring{i}", [P, SLOT]) for i in range(RING)]
        x = sb("x", [P, KD, T])
        sq = sb("sq", [P, KD, T])
        rstd = sb("rstd", [P, T])
        tiny = sb("tiny", [P, 64])
        v_first = sb("v_first", [P, HP, T])
        w_hi = [sb(f"w_hi{i}", [P, SLOT], F32R) for i in range(2)]
        w_lo = [sb(f"w_lo{i}", [P, SLOT], F32R) for i in range(2)]
        hx, h_hi, h_lo = shared("hx", 2 * KD * T, [("h_hi", [P, KD, T]), ("h_lo", [P, KD, T])])
        h = sq
        SCR = 96 * 256
        scr, halves = shared("scr", SCR, [("halves", [P, 2 * KD * T])])
        ctx.enter_context(nc.sbuf_tensor("scr_rest", [P, SCR - 2 * KD * T], F32))
        psd = [ctx.enter_context(nc.psum_tensor(f"psd{i}", [P, 512], F32)) for i in range(4)]
        psx = [ctx.enter_context(nc.psum_tensor(f"psx{i}", [P, 512], F32)) for i in range(4)]

        def at(kib, *shape, parts=P):
            n = math.prod(shape)
            v = scr[0:parts, int(kib * 256):int(kib * 256) + n]
            assert kib * 256 + n <= SCR
            names = " ".join("abcd"[:len(shape)])
            return v if len(shape) == 1 else v.rearrange(
                f"p ({names}) -> p {names}", **{k: s for k, s in zip("abcd", shape)})

        def pc(name, i=0, lo=0, hi=P):
            return par[lo:hi, PCOL[name] + i:PCOL[name] + i + 1]

        def cst(name, n):
            return con[:, CCOL[name]:CCOL[name] + n]

        ident, ones, bones = cst("ident", P), cst("ones", P), cst("bones", P)
        eps_col = con[:, CCOL["eps"]:CCOL["eps"] + 1]
        gneps_col = con[:, CCOL["gneps"]:CCOL["gneps"] + 1]

        plan, MOE, after = stream_plan()
        AFTER = MOE + EXPERTS * 24
        SN = {(k, i): n for n, (k, i, _, _) in enumerate(plan)}
        SN.update({(k, i): AFTER + n for n, (k, i, _, _) in enumerate(after)})
        dense_slots = [n for n in range(AFTER + len(after)) if not MOE <= n < AFTER]
        dense_at = {n: j for j, n in enumerate(dense_slots)}
        hi_cut, lo_cut = S("w_hi_cut"), S("w_lo_cut")
        land = [S(f"landed{i}") for i in range(RING)]
        slots_done = S("slots_done")
        x_done = S("small_done")
        d_read = {"act": S("dense_read_act"), "dve": S("dense_read_dve")}
        x_read = {"act": S("small_read_act"), "dve": S("small_read_dve")}
        DB = Banks(dense_plan(), psd, d_read)
        XB = Banks(small_plan(), psx, x_read)

        def slot_of(key):
            return SN[key if key in SN else (key, key[3])]

        def d_ready(eng, key):
            eng.wait_ge(slots_done, slot_of(key) + 1)
            return DB.bank(key)

        def x_ready(eng, *key):
            eng.wait_ge(x_done, XB.at[key] + 1)
            return XB.bank(key)

        half_slot = {SN[(("mix_in", l), 10)] for l in range(LAYERS)}

        class Cutter:

            def __init__(self, eng, cut):
                self.eng, self.cut, self.next = eng, cut, 0

            def upto(self, n):
                while self.next < len(dense_slots) and dense_slots[self.next] <= n:
                    j = self.next
                    if j >= 2:
                        self.eng.wait_ge(slots_done, dense_slots[j - 2] + 1)
                    self.cut(j, dense_slots[j])
                    self.next += 1

        def cut_ahead(cutter, key):
            n = slot_of(key)
            last = max(s for s in dense_slots if (s < MOE) == (n < MOE))
            cutter.upto(min(dense_slots[min(dense_at[n] + 2, len(dense_slots) - 1)], last))

        def prime(cutter, key):
            cutter.upto(dense_slots[dense_at[slot_of(key)] + 1])

        def m2(bank):
            return bank[:, :].rearrange("p (m t) -> p m t", m=2)

        def tri(bank, n=P):
            return bank[:, 0:HP * n].rearrange("p (q n) -> p q n", q=HP)

        PHASES = ["conv", "merge"] + [
            f"{n}{l}" for l in range(LAYERS) for n in ("ffn1", "att", "rwkv", "cross", "ffn2")]
        phase_end = S("phase_end")

        def barrier(eng, name):
            eng.drain().then_inc(phase_end, 1)
            eng.wait_ge(phase_end, 4 * (PHASES.index(name) + 1))

        XEV = ["w_o", "moe", "final"] + [f"{n}{l}" for l in range(LAYERS) for n in ("ffn1", "mix", "cross", "ffn2")]
        NORMS = ["g_mix", "g_ffn", "g_final"]
        for l in range(LAYERS):
            NORMS += [f"norm_ffn1{l}", f"norm_mix{l}", f"norm_mem{l}", f"norm_cross{l}", f"norm_ffn2{l}"]
        sq_ready, sd_ready, h_ready, x_ready_s = S("sq_ready"), S("sd_ready"), S("h_ready"), S("x_ready")

        def hx_at(kib, *shape):
            n = math.prod(shape)
            names = " ".join("abcd"[:len(shape)])
            return hx[:, int(kib * 256):int(kib * 256) + n].rearrange(
                f"p ({names}) -> p {names}", **{k: s for k, s in zip("abcd", shape)})

        xa, ga, gs = at(0, 8, T), at(8, 8, T), at(16, 16, T)
        v_tok, x1_tok, x2 = at(32, TT, D), at(40, TT, D), at(48, 8, T)
        bd, lr, li, le, lh = at(56, 4, 8, P), at(72, 8, T), at(80, 8, T), at(88, 8, T), sq
        w3h, decay, taps_s, taps_d = at(56, 2, 2, 512, parts=64), at(64, TT, D), hx_at(0, TT, D), hx_at(8, TT, D)
        spec_k, spec_y = at(72, 4, D), hx_at(0, 4, D)
        fwd, inv = at(0, TT, 2 * T), at(4, 4, T)
        filt_w, zT = rstd, at(72, T, parts=33)
        gated = at(88, 8, T)

        h_tok, onehot, weighted = at(0, TT, D), at(8, TT, EXPERTS, CAP), at(12, TT, EXPERTS, P)
        PT, xe = at(28, EXPERTS, T), at(44, KD, EXPERTS * CAP)
        wr = at(60, KD, EXPERTS)
        xs, sg_e, act_e = at(61, KD, CAP), at(62, 512), at(64, 512)
        actT, ye = at(66, 4, P), at(68, 2, 512)
        aff, lg, affT, wk, msk, slotT, slots = (at(72, TT, 16), at(72.25, TT, 16), at(73, T, parts=16),
                                                at(74, T, parts=16), at(75, T, parts=16), at(76, T, parts=16),
                                                at(77, TT, 16))
        top8 = at(78, 8, parts=16)
        ones16 = at(79, T, parts=16)

        sg, fa = at(0, 2, 2, T), at(4, 2, 2, T)
        fa_hi, fa_lo = (halves[:, i * 1024:(i + 1) * 1024].rearrange("p (f i t) -> p f i t", f=2, i=2) for i in (2, 3))
        ycat, pb, ts = at(0, 8, T), at(8, NPB, T), at(29, 10, T)
        al, rt, be, kt = at(39, HP, T), at(42, HP, T), at(45, HP, T), at(48, HP, T)
        rs6 = at(39, 6, T)
        v_tm, ab, bm, km = hx_at(8, TT, AW), hx_at(11, 6, P), at(51, HP, 4, P), at(57, HP, 4, P)
        MATS = {n: [at(63 + 1.5 * (2 * i + p), HP, P) for p in range(2)] for i, n in enumerate(
            ("A", "AT", "Aoff", "BT", "CT", "DT", "Q", "P2", "P2T", "P4", "P4T"))}
        e1, e2, e3, kk, aa, gg, yy = (pb[:, 0:3, :], pb[:, 3:6, :], pb[:, 6:9, :], pb[:, 9:12, :],
                                      pb[:, 12:15, :], pb[:, 15:18, :], pb[:, 18:21, :])
        MT, y0T, RT = hx_at(0, 4, HP, P), hx_at(6, HP, P), hx_at(14, HP, P)
        sqf = sq[:, :, :].rearrange("p a t -> p (a t)")
        Np = sqf[:, 0:768].rearrange("p (c q n) -> p c q n", c=4, q=HP)
        Xs = sqf[:, 768:768 + 960].rearrange("p (c q n) -> p c q n", c=5, q=HP)
        lora_up = at(90, AW)
        lo = ts[:, 9, :]
        rbias, prob = at(63, 6, 384), at(72, 6, 384)
        probT = at(81, 6, 3, P)
        up, wa, wb = at(29, 2, 16 + T), at(32, 2, 16 + T), at(35, 2, 16 + T)
        poolw = at(90, 2, P)
        mn_hi, mn_lo = (halves[:, i * 2048:(i + 1) * 2048].rearrange("p (k t) -> p k t", k=KD) for i in (0, 1))
        xk, xv, xq = at(16, 8, T), at(24, TT, D), at(32, 8, T)
        xprob, xpT, xo = at(40, 8, T), at(48, 4, 2, T), at(56, 8, T)
        vdn, vup, vtmp = at(92, HP, 32), at(93, AW, parts=32), at(94.5, T, parts=32)
        memT = at(64, 8, T)

        block = ctx.enter_context(nc.Block())

        @block.tensor
        def _(pe):
            def done(ins):
                ins.then_inc(x_done, 1)

            def cut(n, **kw):
                j = dense_at[n]
                pe.wait_ge(lo_cut, j + 1)
                name = list(kw)[0]
                return [w[j % 2][:, :].rearrange(f"p ({name} c) -> p {name} c", **kw) for w in (w_hi, w_lo)]

            def three(o, w, a, start, stop, **kw):
                for i, (u, v) in enumerate(((0, 0), (0, 1), (1, 0))):
                    mm = pe.matmul(o, w[u], a[v], start=start and i == 0, stop=stop and i == 2, **kw)
                return mm

            def norm(g):
                q = NORMS.index(g)
                b = XB.claim(pe, ("norm", g))
                for k in range(KD):
                    if k % 2 == 0:
                        pe.wait_ge(sq_ready, 4 * q + k // 2 + 1)
                    mm = pe.matmul(b[:, 0:T], ones, sq[:, k, :], start=(k == 0), stop=(k == KD - 1))
                done(mm)

            act_halves = (h_hi, h_lo)

            def dense(key, rhs=act_halves, g=None, tiles=2):
                b = m2(DB.claim(pe, key))
                w = cut(slot_of(key), k=KD)
                for m in range(tiles):
                    for k in range(KD):
                        if g is not None and m == 0 and k % 2 == 0:
                            pe.wait_ge(h_ready, 4 * NORMS.index(g) + k // 2 + 1)
                        c = slice(m * P, (m + 1) * P)
                        mm = three(b[:, m, :], [v[:, k, c] for v in w], [v[:, k, :] for v in rhs],
                                   k == 0, k == KD - 1)
                mm.then_inc(slots_done, 1)

            def ffn(which, l):
                for f in range(FSTEPS + 1):
                    if f < FSTEPS:
                        dense((which, l, "gate", f), g=f"norm_{which}{l}" if f == 0 else None)
                        dense((which, l, "up", f))
                    if f:
                        e = f - 1
                        if e == 0:
                            acc = [m2(XB.claim(pe, (which, l, i))) for i in range(4)]
                        w = cut(SN[((which, l, "down", e), e)], i=2)
                        pe.wait_ge(S("fa_cut"), (2 * l + (which == "ffn2")) * FSTEPS + e + 1)
                        for i in range(2):
                            for dt in range(KD):
                                c = slice(dt * P, (dt + 1) * P)
                                mm = three(acc[dt // 2][:, dt % 2, :], [v[:, i, c] for v in w],
                                           [v[:, e % 2, i, :] for v in (fa_hi, fa_lo)],
                                           e == 0 and i == 0 and dt % 2 == 0, e == FSTEPS - 1 and i == 1,
                                           skip_group_check=True)
                        mm.then_inc(slots_done, 1)
                pe.drain().then_inc(x_done, 4)

            pe.wait_ge(S("par_in"), 16)
            pe.wait_ge(S("con_in"), 16)
            norm("g_mix")
            for i in range(4):
                dense(("a_x", i), g="g_mix" if i == 0 else None)

            def conv_turn(part, i):
                DB.was_read(pe, ("hy_" + part, i))
                b = XB.claim(pe, ("hy_tr", part, i))
                for tt in range(TT):
                    for m in range(2):
                        mm = pe.transpose(b[:, (2 * tt + m) * P:(2 * tt + m + 1) * P],
                                          sq[:, 2 * (i % 2) + m, tt * P:(tt + 1) * P], ident)
                done(mm)

            turns = [(part, i) for part in ("v", "x1") for i in range(4)]
            for n, (part, i) in enumerate(turns):
                dense(("hy_" + part, i))
                if n:
                    conv_turn(*turns[n - 1])
            dense(("hy_x2", 0))
            conv_turn(*turns[-1])
            for i in range(1, 4):
                dense(("hy_x2", i))

            def lru_gates(d):
                for kind in range(2):
                    for i in range(4):
                        b = m2(XB.claim(pe, ("lru", d, kind, i)))
                        for m in range(2):
                            mm = pe.matmul(b[:, m, :], bd[:, 2 * d + kind, 2 * i + m, :], xa[:, 2 * i + m, :],
                                           start=True, stop=True)
                        done(mm)

            pe.wait_ge(S("bd_in"), 16)
            DB.was_read(pe, ("a_x", 3))
            lru_gates(0)
            for i in range(4):
                dense(("a_gate", i))
            for i in range(2):
                dense(("gates", i))
            lru_gates(1)
            for i in range(2, 8):
                dense(("gates", i))
            pe.wait_ge(S("lru_out"), 1)
            dense(("w_a_out", 0))

            b = XB.claim(pe, ("filt", 0))
            pe.wait_ge(S("filt_in"), 64)
            done(pe.matmul(b[0:64, 0:T], filt_w[0:33, 0:64], zT, start=True, stop=True))
            dense(("w_a_out", 1))
            dense(("w_a_out", 2))
            pe.wait_ge(S("filt_sin"), 1)
            b = XB.claim(pe, ("filt", 1))
            done(pe.matmul(b[0:64, 0:T], filt_w[0:64, 64:128], sq[0:64, 1, :], start=True, stop=True))
            dense(("w_a_out", 3))
            pe.wait_ge(S("filt_sin"), 2)
            pe.wait_ge(S("dft_in"), 16)
            for n in range(2):
                pe.wait_ge(S(f"w3_in{n}"), 16)
                for tt in range(TT):
                    for half in range(2):
                        for d in range(2):
                            b = XB.claim(pe, ("taps", n, tt, half, d))
                            done(pe.matmul(b[:, :], sq[0:64, 2, tt * P:(tt + 1) * P], w3h[:, d, half, :],
                                           start=True, stop=True))
                pe.wait_ge(S("taps_ready"), n + 1)
                for m in range(4):
                    src = taps_s if m < 2 else taps_d
                    for half in range(2):
                        b = XB.claim(pe, ("spec_k", n, m, half))
                        for tt in range(TT):
                            mm = pe.matmul(b[:, :], fwd[:, tt, m * P:(m + 1) * P],
                                           src[:, tt, half * 512:(half + 1) * 512], start=(tt == 0), stop=(tt == 1))
                        done(mm)
                if n:
                    pe.wait_ge(S("z_tok"), 4)
                for half in range(2):
                    for f in range(2):
                        for im in range(2):
                            b = XB.claim(pe, ("spec_u", n, half, f, im))
                            m = 2 * im + f
                            for tt in range(TT):
                                mm = pe.matmul(b[:, :], fwd[:, tt, m * P:(m + 1) * P],
                                               v_tok[:, tt, half * 512:(half + 1) * 512],
                                               start=(tt == 0), stop=(tt == 1))
                            done(mm)
                pe.wait_ge(S("spec_y"), 4 * (n + 1))
                for i in range(4):
                    b = XB.claim(pe, ("inv", n, i))
                    if n == 0:
                        tt, half = i // 2, i % 2
                        for m in range(4):
                            mm = pe.matmul(b[:, :], inv[:, m, tt * P:(tt + 1) * P],
                                           spec_y[:, m, half * 512:(half + 1) * 512], start=(m == 0), stop=(m == 3))
                    else:
                        for c in range(2):
                            for m in range(4):
                                mm = pe.matmul(m2(b)[:, c, :], spec_y[:, m, (2 * i + c) * P:(2 * i + c + 1) * P],
                                               inv[:, m, :], start=(m == 0), stop=(m == 3))
                    done(mm)
            pe.wait_ge(S("z_cut"), 1)
            for i in range(4):
                dense(("w_b_out", i))
            pe.wait_ge(S("merged"), 1)
            for i in range(4):
                dense(("w_o", i))
            barrier(pe, "conv")

            norm("g_ffn")
            b = XB.claim(pe, ("router",))
            pe.wait_ge(S("wr_in"), 16)
            for tt in range(TT):
                for k in range(KD):
                    if tt == 0 and k % 2 == 0:
                        pe.wait_ge(h_ready, 4 * NORMS.index("g_ffn") + k // 2 + 1)
                    mm = pe.matmul(b[:, tt * 16:tt * 16 + 16], h[:, k, tt * P:(tt + 1) * P], wr[:, k, :],
                                   start=(k == 0), stop=(k == KD - 1))
            done(mm)
            for tt in range(TT):
                for i in range(2):
                    b = XB.claim(pe, ("h_tok", tt, i))
                    for c in range(4):
                        mm = pe.transpose(b[:, c * P:(c + 1) * P], h[:, 4 * i + c, tt * P:(tt + 1) * P], ident)
                    done(mm)
            b = XB.claim(pe, ("affT",))
            pe.wait_ge(S("aff"), 1)
            for tt in range(TT):
                mm = pe.transpose(b[0:16, tt * P:(tt + 1) * P], aff[:, tt, :], ident)
            done(mm)
            b = XB.claim(pe, ("slot_tr",))
            pe.wait_ge(S("slotT"), 1)
            for tt in range(TT):
                mm = pe.transpose(b[:, tt * 16:tt * 16 + 16], slotT[:, tt * P:(tt + 1) * P], ident[0:16, 0:16])
            done(mm)
            pe.wait_ge(S("weighted"), 1)
            for i in range(8):
                b = XB.claim(pe, ("PT", i))
                for c in range(2):
                    for tt in range(TT):
                        mm = pe.transpose(b[:, (2 * c + tt) * P:(2 * c + tt + 1) * P], weighted[:, tt, 2 * i + c, :],
                                          ident)
                done(mm)
            XB.was_read(pe, ("h_tok", 1, 1))
            for i in range(8):
                b = XB.claim(pe, ("xe", i))
                for tt in range(TT):
                    mm = pe.matmul(b[:, :], h_tok[:, tt, i * P:(i + 1) * P],
                                   onehot[:, tt, :, :].rearrange("p e c -> p (e c)"), start=(tt == 0), stop=(tt == 1))
                done(mm)
            acc = [m2(XB.claim(pe, ("moe_acc", i))) for i in range(4)]
            for k in range(KD):
                pe.matmul(acc[k // 2][:, k % 2, :], ident, x[:, k, :], start=(k % 2 == 0), stop=False,
                          skip_group_check=True)
            XB.was_read(pe, ("xe", 7))
            XB.was_read(pe, ("PT", 7))

            for i in range(4):
                DB.claim(pe, ("moe", i))
            turn = psd[0][:, :].rearrange("p (b n) -> p b n", b=4)
            def down_rows(n):
                return ring[n % RING][:, :].rearrange("p (i c) -> p i c", i=2)

            with pe.Fori(0, EXPERTS) as e:
                pe.wait_ge(S("xs_ready"), e + 1)
                for s in range(16):
                    n = MOE + s
                    pe.wait_ge(land[n % RING], e * (16 * 24 // RING) + 16 * (n // RING + 1))
                    for j in range(4):
                        mm = pe.matmul(psd[s // 8][32 * j:32 * j + 32, :], xs[:, s % 8, :],
                                       ring[n % RING][:, j * 512:(j + 1) * 512], start=(s % 8 == 0), stop=(s % 8 == 7),
                                       skip_group_check=True)
                    mm.then_inc(slots_done, 1)
                pe.wait_ge(S("act_e"), e + 1)
                for b4 in range(4):
                    mm = pe.transpose(turn[:, b4, :], act_e[:, b4 * P:(b4 + 1) * P], ident)
                mm.then_inc(S("turned"), 1)
                pe.wait_ge(S("actT"), e + 1)
                for s in range(0, 8, 2):
                    for q in (s, s + 1):
                        n = MOE + 16 + q
                        pe.wait_ge(land[n % RING], e * (16 * 24 // RING) + 16 * (n // RING + 1))
                    for half in range(2):
                        for j in range(4):
                            n, kt_ = MOE + 16 + s + j // 2, 2 * s + j
                            mm = pe.matmul(psd[2 + half][32 * j:32 * j + 32, :],
                                           actT[:, kt_ % 4, 32 * (kt_ // 4):32 * (kt_ // 4) + 32],
                                           down_rows(n)[:, j % 2, half * 512:(half + 1) * 512], start=(s == 0), stop=(s == 6),
                                           skip_group_check=True)
                            if half == 1 and j >= 2:
                                mm.then_inc(slots_done, 1)
                pe.wait_ge(S("ye_ready"), 2 * e + 2)
                for k in range(KD):
                    pe.matmul(acc[k // 2][:, k % 2, :], ye[:, k // 4, (k % 4) * P:(k % 4 + 1) * P],
                                   PT[:, bass.ds(e, 1), :].rearrange("p a t -> p (a t)"), start=False, stop=False,
                                   skip_group_check=True)
            pe.drain().then_inc(x_done, 4)
            barrier(pe, "merge")
            norm("g_final")

            for l in range(LAYERS):
                norm(f"norm_ffn1{l}")
                ffn("ffn1", l)
                barrier(pe, f"ffn1{l}")
                norm(f"norm_mix{l}")
                for i in range(11):
                    key = (("mix_in", l), i)
                    if i < 10:
                        dense(key, g=f"norm_mix{l}" if i == 0 else None)
                    else:
                        b, j = m2(DB.claim(pe, key)), dense_at[slot_of(key)]
                        pe.wait_ge(lo_cut, j + 1)
                        for k in range(KD):
                            c = slice(k * P, (k + 1) * P)
                            mm = three(b[:, 0, :], [w_hi[j % 2][:, c], w_lo[j % 2][:, c]],
                                       [v[:, k, :] for v in act_halves], k == 0, k == KD - 1)
                        mm.then_inc(slots_done, 1)

                for i in range(3):
                    b = m2(XB.claim(pe, ("qk_norm", l, i)))
                    pe.wait_ge(S("qk_sq"), 3 * l + i + 1)
                    for m in range(2):
                        mm = pe.matmul(b[:, m, :], bones, sq[:, 2 * i + m, :], start=True, stop=True)
                    done(mm)
                for tt in range(TT):
                    b = XB.claim(pe, ("av_tr", l, tt))
                    for q in range(HP):
                        mm = pe.transpose(tri(b)[:, q, :], pb[:, 16 + q, tt * P:(tt + 1) * P], ident)
                    done(mm)
                pe.wait_ge(S("qk_ready"), l + 1)
                for hd in range(6):
                    r = 64 * (hd % 2)
                    for it in range(2):
                        b = XB.claim(pe, ("score", l, hd, it))
                        done(pe.matmul(b[:, 0:P * (it + 1)], pb[r:r + 64, 10 + hd // 2, it * P:(it + 1) * P],
                                       pb[r:r + 64, 13 + hd // 2, 0:P * (it + 1)], start=True, stop=True))
                for hd in range(6):
                    pe.wait_ge(S("prob"), 6 * l + hd + 1)
                    b = XB.claim(pe, ("prob_tr", l, hd))
                    for j in range(3):
                        mm = pe.transpose(tri(b)[:, j, :], prob[:, hd, j * P:(j + 1) * P], ident)
                    done(mm)
                for q in range(HP):
                    b = XB.claim(pe, ("att", l, q))
                    XB.was_read(pe, ("prob_tr", l, 2 * q + 1))
                    for p in range(2):
                        hd = 2 * q + p
                        o = b[64 * p:64 * p + 64, :]
                        v = [v_tm[:, tt, hd * 64:hd * 64 + 64] for tt in range(TT)]
                        pe.matmul(o[:, 0:P], v[0], probT[:, hd, 0, :], start=True, stop=True)
                        pe.matmul(o[:, P:T], v[0], probT[:, hd, 1, :], start=True, stop=False)
                        mm = pe.matmul(o[:, P:T], v[1], probT[:, hd, 2, :], start=False, stop=True)
                    done(mm)
                b = m2(XB.claim(pe, ("pool", l)))
                pe.wait_ge(S("pooled"), l + 1)
                pe.wait_ge(S(f"att_in{l}"), 32)
                for m in range(2):
                    mm = pe.matmul(b[:, m, :], poolw[:, m, :], up[:, m, 16:16 + T], start=True, stop=True)
                done(mm)
                barrier(pe, f"att{l}")

                pe.wait_ge(S("lora_act"), l + 1)
                pe.wait_ge(S(f"lora_in{l}"), 16 * (3 if l else 1))
                for kind, (r, n) in enumerate(((0, 32), (32, 32), (64, 64))):
                    for i in range(2):
                        b = m2(XB.claim(pe, ("lora", l, kind, i)))
                        for m in range(2 if i == 0 else 1):
                            c = (2 * i + m) * P
                            mm = pe.matmul(b[:, m, :], lora_up[r:r + n, c:c + P], lo[r:r + n, :], start=True, stop=True)
                        done(mm)
                if l:
                    b = XB.claim(pe, ("vdown", l))
                    for q in range(HP):
                        mm = pe.matmul(b[0:32, 0:T], vdn[:, q, :], ts[:, 6 + q, :], start=(q == 0), stop=(q == 2))
                    done(mm)
                    XB.was_read(pe, ("vdown", l))
                    for i in range(2):
                        b = m2(XB.claim(pe, ("vup", l, i)))
                        for m in range(2 if i == 0 else 1):
                            c = (2 * i + m) * P
                            mm = pe.matmul(b[:, m, :], vup[:, c:c + P], vtmp, start=True, stop=True)
                        done(mm)
                pe.wait_ge(S("kk_sq"), l + 1)
                for i in range(2):
                    b = m2(XB.claim(pe, ("kk_norm", l, i)))
                    for m in range(2 if i == 0 else 1):
                        mm = pe.matmul(b[:, m, :], bones, sq[:, 2 * i + m, :], start=True, stop=True)
                    done(mm)
                pe.wait_ge(S("rw_scaled"), l + 1)
                for tt in range(TT):
                    tok = slice(tt * P, (tt + 1) * P)
                    for xk_, src in (("a", al), ("b", be), ("k", kt), ("v", ts[:, 6:9, :])):
                        b = XB.claim(pe, ("rw_tr", l, tt, xk_))
                        for q in range(HP):
                            mm = pe.transpose(tri(b)[:, q, :], src[:, q, tok], ident)
                        done(mm)

                    def mats(name, body, n=P, wait=()):
                        for p in range(2):
                            for w in wait:
                                w(p)
                            b = XB.claim(pe, (name, l, tt, p))
                            for q in range(HP):
                                mm = body(tri(b, n)[:, q, :], p, q)
                            done(mm)

                    def pair(lhs, rhs):
                        def body(o, p, q):
                            r = slice(64 * p, 64 * p + 64)
                            return pe.matmul(o, lhs[r, q, tok], rhs[r, q, tok], start=True, stop=True)
                        return body

                    def prod(lhs, rhs):
                        def body(o, p, q):
                            return pe.matmul(o, MATS[lhs][p][:, q, :], MATS[rhs][p][:, q, :], start=True, stop=True)
                        return body

                    def after(*names):
                        return [lambda p, x=x_: XB.was_read(pe, (x, l, tt, p)) for x_ in names]

                    mats("A", pair(al, be))
                    mats("AT", pair(be, al))
                    mats("BT", pair(kt, al))
                    mats("CT", pair(be, rt))
                    mats("DT", pair(kt, rt))
                    mats("P2", prod("AT", "A"), wait=after("A", "AT"))
                    mats("P2T", prod("A", "AT"))
                    mats("Q2", prod("P2", "Q"), wait=after("P2"))
                    mats("P4", prod("P2T", "P2"), wait=after("P2T"))
                    mats("P4T", prod("P2", "P2T"))
                    mats("Q4", prod("P4", "Q"), wait=after("P4", "Q2"))
                    mats("P8", prod("P4T", "P4"), wait=after("P4T"))
                    mats("Q8", prod("P2", "Q"), wait=after("P8", "Q4"))
                    mats("TR", lambda o, p, q: pe.transpose(o, MATS["Q"][p][:, q, :], ident), wait=after("Q8"))
                    mats("X1", prod("Aoff", "Q"))
                    mats("Q32", prod("P2T", "P4"), wait=after("TR", "X1"))
                    XB.was_read(pe, ("rw_tr", l, tt, "v"))
                    mats("BV", lambda o, p, q: pe.matmul(
                        o, MATS["BT"][p][:, q, :], v_tm[:, tt, (2 * q + p) * 64:(2 * q + p) * 64 + 64],
                        start=True, stop=True), n=64)
                    mats("WU", lambda o, p, q: pe.matmul(o, MATS["Q"][p][:, q, :], ab[:, 2 * q + p, :],
                                                         start=True, stop=True), wait=after("Q32", "BV"))
                    for w in after("WU"):
                        w(0)
                        w(1)
                    XB.was_read(pe, ("rw_tr", l, tt, "b"))
                    XB.was_read(pe, ("rw_tr", l, tt, "k"))
                    for q in range(HP):
                        wu = [MATS["P4T"][p][:, q, :] for p in range(2)]
                        rows = [slice(64 * p, 64 * p + 64) for p in range(2)]
                        b = XB.claim(pe, ("M", l, tt, q))
                        for p in range(2):
                            mm = pe.matmul(b[rows[p], 0:T], wu[p][:, 0:64], bm[:, q, :, rows[p]],
                                           start=True, stop=True)
                        done(mm)
                        b = XB.claim(pe, ("N", l, tt, q))
                        for p in range(2):
                            hd = 2 * q + p
                            for c in range(4):
                                o = b[rows[p], c * 64:c * 64 + 64]
                                pe.matmul(o, bm[:, q, c, rows[p]], wu[p][:, 64:128], start=True, stop=False)
                                mm = pe.matmul(o, km[:, q, c, rows[p]], v_tm[:, tt, hd * 64:hd * 64 + 64],
                                               start=False, stop=True)
                        done(mm)
                        b = XB.claim(pe, ("RY", l, tt, q))
                        for p in range(2):
                            hd = 2 * q + p
                            pe.matmul(b[rows[p], 0:P], wu[p][:, 0:64], MATS["CT"][p][:, q, :], start=True, stop=True)
                            pe.matmul(b[rows[p], P:T], wu[p][:, 64:128], MATS["CT"][p][:, q, :],
                                      start=True, stop=False)
                            mm = pe.matmul(b[rows[p], P:T], v_tm[:, tt, hd * 64:hd * 64 + 64],
                                           MATS["DT"][p][:, q, :], start=False, stop=True)
                        done(mm)
                    for c in range(4):
                        if c == 0:
                            pe.wait_ge(S("state0"), 2 * l + tt + 1)
                            XB.was_read(pe, ("RY", l, tt, HP - 1))
                        else:
                            XB.was_read(pe, ("S", l, tt, c - 1))
                        b = XB.claim(pe, ("S", l, tt, c))
                        for q in range(HP):
                            mm = pe.matmul(tri(b, 64)[:, q, :], MT[:, c, q, :], Xs[:, c, q, :], start=True, stop=True)
                        done(mm)
                    for p in range(2):
                        b = XB.claim(pe, ("y", l, tt, p))
                        r = slice(64 * p, 64 * p + 64)
                        for q in range(HP):
                            for c in range(4):
                                mm = pe.matmul(tri(b)[r, q, c * CH:(c + 1) * CH], Xs[r, c, q, :],
                                               RT[r, q, c * CH:(c + 1) * CH], start=True, stop=True)
                        done(mm)
                for name, src, flag in (("mean", yy, "y_ready"), ("var", sq[:, 0:3, :], "yc_sq"),
                                        ("bonus", e1, "rk_ready")):
                    pe.wait_ge(S(flag), l + 1)
                    for i in range(2):
                        b = m2(XB.claim(pe, (name, l, i)))
                        for m in range(2 if i == 0 else 1):
                            mm = pe.matmul(b[:, m, :], bones, src[:, 2 * i + m, :], start=True, stop=True)
                        done(mm)
                pe.wait_ge(S("mix_cat"), l + 1)
                for i in range(4):
                    dense((("mix_out", l), i))
                barrier(pe, f"rwkv{l}")

                norm(f"norm_mem{l}")
                for i in range(4):
                    dense((("x_k", l), i), (mn_hi, mn_lo), f"norm_mem{l}" if i == 0 else None)
                for i in range(4):
                    key = (("x_v", l), i)
                    b = m2(DB.claim(pe, key))
                    w = cut(slot_of(key), k=KD)
                    for tt in range(TT):
                        for k in range(KD):
                            mm = three(b[:, tt, :], [v[:, k, tt * P:(tt + 1) * P] for v in (mn_hi, mn_lo)],
                                       [v[:, k, :] for v in w], k == 0, k == KD - 1)
                    mm.then_inc(slots_done, 1)
                norm(f"norm_cross{l}")
                for i in range(4):
                    dense((("x_q", l), i), g=f"norm_cross{l}" if i == 0 else None)
                for j, name in enumerate("kq"):
                    for i in range(2):
                        b = m2(XB.claim(pe, ("xnorm", l, name, i)))
                        pe.wait_ge(S("x_sq"), 4 * l + 2 * j + i + 1)
                        for m in range(2):
                            for c in range(2):
                                mm = pe.matmul(b[:, m, :], ones, sq[:, 4 * i + 2 * m + c, :], start=(c == 0), stop=(c == 1))
                        done(mm)
                pe.wait_ge(S("xqk_ready"), l + 1)
                for hd in range(4):
                    for it in range(TT):
                        b = XB.claim(pe, ("xscore", l, hd, it))
                        for c in range(2):
                            mm = pe.matmul(b[:, 0:T], xq[:, 2 * hd + c, it * P:(it + 1) * P], xk[:, 2 * hd + c, :],
                                           start=(c == 0), stop=(c == 1))
                        done(mm)
                for hd in range(4):
                    pe.wait_ge(S("xprob"), 4 * l + hd + 1)
                    b = XB.claim(pe, ("xprob_tr", l, hd))
                    for mt in range(2):
                        for it in range(TT):
                            mm = pe.transpose(m2(b)[:, mt, it * P:(it + 1) * P],
                                              xprob[:, 2 * hd + it, mt * P:(mt + 1) * P], ident)
                    done(mm)
                for hd in range(4):
                    b = m2(XB.claim(pe, ("xatt", l, hd)))
                    XB.was_read(pe, ("xprob_tr", l, hd))
                    for c in range(2):
                        for mt in range(2):
                            mm = pe.matmul(b[:, c, :], xv[:, mt, (2 * hd + c) * P:(2 * hd + c + 1) * P],
                                           xpT[:, hd, mt, :], start=(mt == 0), stop=(mt == 1))
                    done(mm)
                pe.wait_ge(S("xo_cut"), l + 1)
                for i in range(4):
                    dense((("x_o", l), i))
                barrier(pe, f"cross{l}")
                norm(f"norm_ffn2{l}")
                ffn("ffn2", l)
                barrier(pe, f"ffn2{l}")

        @block.scalar
        def _(act):
            def read(ins):
                ins.then_inc(x_read["act"], 1)

            def copy(o, i):
                return act.activation(o, i, ACT.Copy)

            def cut_weights(j, n):
                act.wait_ge(land[n % RING], 16 * (n // RING + 1))
                words = KD * P if n in half_slot else SLOT
                act.activation(w_hi[j % 2][:, 0:words], ring[n % RING][:, 0:words], ACT.Copy).then_inc(hi_cut, 1)

            cutter = Cutter(act, cut_weights)
            pieces = [0]

            def cut_act(src, hi, ready=None):
                pieces[0] += 1
                if ready:
                    ready()
                else:
                    act.wait_ge(S("act_made"), pieces[0] - ffn_pieces[0])
                copy(hi, src).then_inc(S("act_hi_cut"), 1)

            ffn_pieces = [0]

            def cut_acts(src, hi):
                for i in range(4):
                    two = slice(2 * i, 2 * i + 2)
                    cut_act(src[:, two, :], hi[:, two, :])

            def norm(g, event=None, src=None, hi=h_hi, before_cut=None):
                q = NORMS.index(g)
                src = x if src is None else src
                if event:
                    act.wait_ge(x_ready_s, XEV.index(event) + 1)
                if q:
                    act.wait_ge(h_ready, 4 * q)
                for i in range(4):
                    act.activation(sq[:, 2 * i:2 * i + 2, :], src[:, 2 * i:2 * i + 2, :],
                                   ACT.Square).then_inc(sq_ready, 1)
                b = x_ready(act, "norm", g)
                read(act.activation(rstd[:, :], b[:, 0:T], ACT.Sqrt, bias=eps_col, scale=1.0 / D))
                if before_cut:
                    before_cut()
                if hi is not None:
                    cut_acts(h, hi)

            def ffn(which, l):
                for f in range(FSTEPS):
                    cut_ahead(cutter, (which, l, "gate", f))
                    b = d_ready(act, (which, l, "gate", f))
                    if f > 1:
                        DB.was_read(act, (which, l, "up", f - 2))
                    act.activation(sg[:, f % 2, :, :], m2(b), ACT.Silu).then_inc(d_read["act"], 1)
                    cut_ahead(cutter, (which, l, "up", f))
                    if f > 1:
                        act.wait_ge(slots_done, SN[((which, l, "down", f - 2), f - 2)] + 1)
                    ffn_pieces[0] += 1
                    cut_act(fa[:, f % 2, :, :], fa_hi[:, f % 2, :, :],
                            lambda: DB.was_read(act, (which, l, "up", f)))

            act.wait_ge(S("x_in"), 16)
            act.wait_ge(S("con_in"), 16)
            norm("g_mix", before_cut=lambda: prime(cutter, ("a_x", 0)))
            act.wait_ge(S("lam_abs"), 1)
            act.activation(tiny[:, 16:32], tiny[:, 0:16], ACT.Exp, scale=-1.0).then_inc(S("lam_exp"), 1)
            cut_ahead(cutter, ("a_x", 3))
            for part, dst in (("v", v_tok), ("x1", x1_tok)):
                for i in range(4):
                    cut_ahead(cutter, ("hy_" + part, i))
                    b = x_ready(act, "hy_tr", part, i)
                    read(copy(dst[:, :, i * 256:(i + 1) * 256], b[:, :].rearrange("p (t c) -> p t c", t=TT)))
            cut_ahead(cutter, ("hy_x2", 3))
            act.wait_ge(S("lru_c"), 1)
            act.wait_ge(S("par_in"), 16)

            def lru(d, first, second):
                if d:
                    act.wait_ge(S("lru_scan"), 1)
                for kind, (dst, bias) in enumerate(((lr, "lru_b_r"), (li, "lru_b_i"))):
                    for i in range(4):
                        b = m2(x_ready(act, "lru", d, kind, i))
                        for m in range(2):
                            c = 2 * i + m
                            ins = act.activation(dst[:, c, :], b[:, m, :], ACT.Sigmoid, bias=pc(bias, 8 * d + c))
                        read(ins)
                act.drain()
                for c in range(KD):
                    act.activation(le[:, c, :], lr[:, c, :], ACT.Exp, scale=tiny[:, 48 + 8 * d + c:49 + 8 * d + c])
                cut_ahead(cutter, first)
                act.drain()
                for c in range(KD):
                    act.activation(lr[:, c, :], lr[:, c, :], ACT.Exp, scale=tiny[:, 32 + 8 * d + c:33 + 8 * d + c])
                act.drain().then_inc(S("lru_exp"), 1)
                cut_ahead(cutter, second)
                act.wait_ge(S("lru_neg"), d + 1)
                act.activation(le[:, :, :], le[:, :, :], ACT.Sqrt, bias=1.0).then_inc(S("lru_mult"), 1)

            def gates(i):
                cut_ahead(cutter, ("gates", i))
                b = d_ready(act, ("gates", i))
                act.activation(gs[:, 2 * i:2 * i + 2, :], m2(b), ACT.Sigmoid).then_inc(d_read["act"], 1)

            lru(0, ("a_gate", 0), ("a_gate", 1))
            for i in range(4):
                cut_ahead(cutter, ("a_gate", i))
                b = d_ready(act, ("a_gate", i))
                act.activation(ga[:, 2 * i:2 * i + 2, :], m2(b), ACT.Gelu_apprx_tanh).then_inc(d_read["act"], 1)
            for i in range(2):
                gates(i)
            lru(1, ("gates", 2), ("gates", 3))
            for i in range(2, 8):
                gates(i)
            cut_acts(le, h_hi)

            for i in range(2):
                cut_ahead(cutter, ("w_a_out", 2 * i))
                act.wait_ge(S("filt_red"), i + 1)
                act.activation(sq[0:64, 1 + i, :], sq[0:64, 1 + i, :], ACT.Sin).then_inc(S("filt_sin"), 1)
            cut_ahead(cutter, ("w_a_out", 3))
            for tt in (0, 1):
                act.activation(decay[:, tt, :], decay[:, 1, :], ACT.Exp,
                               scale=con[:, CCOL["negt"] + tt:CCOL["negt"] + tt + 1])
                act.drain()
            act.drain().then_inc(S("decay"), 1)
            for n in range(2):
                for m in range(4):
                    for half in range(2):
                        b = x_ready(act, "spec_k", n, m, half)
                        read(copy(spec_k[:, m, half * 512:(half + 1) * 512], b[:, :]))
            cut_acts(x2, h_hi)
            cut_ahead(cutter, ("w_b_out", 3))
            cut_acts(gated, h_hi)
            cut_ahead(cutter, ("w_o", 3))
            barrier(act, "conv")

            norm("g_ffn", "w_o", hi=None)
            act.wait_ge(S("lg_shift"), 1)
            for tt in range(TT):
                act.activation(aff[:, tt, :], lg[:, tt, :], ACT.Exp, accum_out=tiny[:, tt:tt + 1])
            act.drain().then_inc(S("aff_exp"), 1)
            for tt in range(TT):
                for i in range(2):
                    b = x_ready(act, "h_tok", tt, i)
                    read(copy(h_tok[:, tt, i * 512:(i + 1) * 512], b[:, :]))
            for i in range(8):
                b = x_ready(act, "PT", i)
                read(copy(PT[:, 2 * i:2 * i + 2, :], m2(b)))
            with act.Fori(0, EXPERTS) as e:
                act.wait_ge(slots_done, 24 * e + MOE + 8)
                act.activation(sg_e, psd[0][:, :], ACT.Silu).then_inc(S("sg_e"), 1)
                act.wait_ge(S("turned"), e + 1)
                copy(actT[:, :, :], psd[0][:, :].rearrange("p (b n) -> p b n", b=4)).then_inc(S("actT"), 1)
                act.wait_ge(slots_done, 24 * e + MOE + 24)
                copy(ye[:, 0, :], psd[2][:, :]).then_inc(S("ye_ready"), 1)
            barrier(act, "merge")
            norm("g_final", "moe", hi=None)

            for l in range(LAYERS):
                if l == 0:
                    prime(cutter, ("ffn1", 0, "gate", 0))
                norm(f"norm_ffn1{l}", "final" if l == 0 else f"ffn2{l - 1}")
                ffn("ffn1", l)
                prime(cutter, (("mix_in", l), 0))
                barrier(act, f"ffn1{l}")
                norm(f"norm_mix{l}", f"ffn1{l}")
                for i in range(11):
                    cut_ahead(cutter, (("mix_in", l), i))
                    b, m = m2(d_ready(act, (("mix_in", l), i))), 2 if i < 10 else 1
                    copy(pb[:, 2 * i:2 * i + m, :], b[:, 0:m, :]).then_inc(d_read["act"], 1)
                act.drain()
                for i in range(3):
                    act.activation(sq[:, 2 * i:2 * i + 2, :], pb[:, 10 + 2 * i:12 + 2 * i, :],
                                   ACT.Square).then_inc(S("qk_sq"), 1)
                for i in range(3):
                    b = x_ready(act, "qk_norm", l, i)
                    read(act.activation(rs6[:, 2 * i:2 * i + 2, :], m2(b), ACT.Sqrt, bias=eps_col, scale=1.0 / 64))
                for tt in range(TT):
                    b = x_ready(act, "av_tr", l, tt)
                    read(copy(v_tm[:, tt, :], b[:, 0:AW]))
                for hd in range(6):
                    act.wait_ge(S("score_max"), 6 * l + hd + 1)
                    for it, (lo_, hi_) in enumerate(((0, P), (P, AW))):
                        act.activation(prob[:, hd, lo_:hi_], prob[:, hd, lo_:hi_], ACT.Exp,
                                       bias=tiny[:, 2 * hd + it:2 * hd + it + 1],
                                       accum_out=tiny[:, 12 + 2 * hd + it:13 + 2 * hd + it])
                    act.drain().then_inc(S("score_exp"), 1)
                for hd in range(6):
                    b = x_ready(act, "prob_tr", l, hd)
                    read(copy(probT[:, hd, :, :], tri(b)))
                for q in range(HP):
                    b = x_ready(act, "att", l, q)
                    read(copy(ycat[:, 3 + q, :], b[:, 0:T]))
                b = m2(x_ready(act, "pool", l))
                for m in range(2):
                    ins = act.activation(ycat[:, 6 + m, :], b[:, m, :], ACT.Copy, scale=pc(f"c_pool_scale{l}", m))
                read(ins)
                barrier(act, f"att{l}")

                act.wait_ge(S("shifted"), l + 1)
                act.activation(lo[0:32, :], lo[0:32, :], ACT.Tanh)
                act.activation(lo[64:128, :], lo[64:128, :], ACT.Sigmoid)
                act.drain().then_inc(S("lora_act"), 1)
                for kind, (dst, bias) in enumerate(((rt, "a_w0"), (aa, "a_a0"), (gg, None))):
                    for i in range(2):
                        b = m2(x_ready(act, "lora", l, kind, i))
                        for m in range(2 if i == 0 else 1):
                            j = 2 * i + m
                            ins = copy(dst[:, j, :], b[:, m, :]) if bias is None else act.activation(
                                dst[:, j, :], b[:, m, :], ACT.Sigmoid, bias=pc(f"{bias}{l}", j))
                        read(ins)
                if l:
                    b = x_ready(act, "vdown", l)
                    read(copy(vtmp, b[0:32, 0:T]))
                    for i in range(2):
                        b = m2(x_ready(act, "vup", l, i))
                        for m in range(2 if i == 0 else 1):
                            j = 2 * i + m
                            ins = act.activation(be[:, j, :], b[:, m, :], ACT.Sigmoid, bias=pc("a_v0", j))
                        read(ins)
                act.wait_ge(S("kk_raw"), l + 1)
                act.activation(sq[:, 0:3, :], kk, ACT.Square).then_inc(S("kk_sq"), 1)
                for i in range(2):
                    b, m = m2(x_ready(act, "kk_norm", l, i)), 2 - i
                    read(act.activation(al[:, 2 * i:2 * i + m, :], b[:, 0:m, :], ACT.Sqrt))
                act.wait_ge(S("decays"), l + 1)
                act.activation(e1, kt[:, :, :], ACT.Exp)
                act.activation(e2, kt[:, :, :], ACT.Exp, scale=-1.0)
                act.activation(e3, be[:, :, :], ACT.Exp)
                act.drain().then_inc(S("decay_exp"), 1)
                for tt in range(TT):
                    b = tri(x_ready(act, "rw_tr", l, tt, "a"))
                    read(copy(ab[:, :, 0:64], b.rearrange("p q (h n) -> p (q h) n", h=2)))
                    b = tri(x_ready(act, "rw_tr", l, tt, "k"))
                    for c in range(4):
                        ins = act.activation(km[:, :, c, :], b, ACT.Copy,
                                             scale=con[:, CCOL["chunk"] + c:CCOL["chunk"] + c + 1])
                    read(ins)
                    b = x_ready(act, "rw_tr", l, tt, "v")
                    read(copy(v_tm[:, tt, :], b[:, 0:AW]))
                    for name, dst in (("P2", "P2"), ("P2T", "P2T"), ("P4", "P4"), ("P4T", "P4T"), ("P8", "P2"),
                                      ("TR", "P2T"), ("X1", "P4"), ("BV", None), ("WU", "P4T")):
                        for p in range(2):
                            b = x_ready(act, name, l, tt, p)
                            if name == "BV":
                                ab_p = ab[:, :, :].rearrange("p (q h) n -> p q h n", h=2)
                                read(copy(ab_p[:, :, p, 64:128], tri(b, 64)))
                            else:
                                read(copy(MATS[dst][p][:, :, :], tri(b)))
                act.wait_ge(S("y_mean"), l + 1)
                act.activation(sq[:, 0:3, :], yy, ACT.Square).then_inc(S("yc_sq"), 1)
                for i in range(2):
                    b, m = m2(x_ready(act, "var", l, i)), 2 - i
                    read(act.activation(al[:, 2 * i:2 * i + m, :], b[:, 0:m, :], ACT.Sqrt, bias=gneps_col,
                                        scale=1.0 / 64))
                cut_acts(ycat, h_hi)
                cut_ahead(cutter, (("mix_out", l), 3))
                barrier(act, f"rwkv{l}")

                act.wait_ge(S("mem_in"), 16 * (l + 1))
                norm(f"norm_mem{l}", src=memT, hi=mn_hi)
                for i in range(4):
                    cut_ahead(cutter, (("x_k", l), i))
                    b = d_ready(act, (("x_k", l), i))
                    copy(xk[:, 2 * i:2 * i + 2, :], m2(b)).then_inc(d_read["act"], 1)
                for i in range(4):
                    cut_ahead(cutter, (("x_v", l), i))
                    b = d_ready(act, (("x_v", l), i))
                    copy(xv[:, :, i * 256:(i + 1) * 256], m2(b)).then_inc(d_read["act"], 1)
                norm(f"norm_cross{l}", f"mix{l}")
                for i in range(4):
                    cut_ahead(cutter, (("x_q", l), i))
                    b = d_ready(act, (("x_q", l), i))
                    copy(xq[:, 2 * i:2 * i + 2, :], m2(b)).then_inc(d_read["act"], 1)
                act.drain()
                for j, (name, src) in enumerate((("k", xk), ("q", xq))):
                    if j:
                        x_ready(act, "xnorm", l, "k", 1)
                    for i in range(2):
                        act.activation(sq[:, 4 * i:4 * i + 4, :], src[:, 4 * i:4 * i + 4, :],
                                       ACT.Square).then_inc(S("x_sq"), 1)
                    for i in range(2):
                        b = x_ready(act, "xnorm", l, name, i)
                        k4 = 4 * j + 2 * i
                        read(act.activation(memT[:, k4:k4 + 2, :], m2(b), ACT.Sqrt, bias=eps_col, scale=1.0 / 256))
                for hd in range(4):
                    act.wait_ge(S("xscore_max"), 4 * l + hd + 1)
                    for it in range(TT):
                        j = 2 * hd + it
                        act.activation(xprob[:, j, :], xprob[:, j, :], ACT.Exp, bias=tiny[:, j:j + 1],
                                       accum_out=tiny[:, 12 + j:13 + j])
                    act.drain().then_inc(S("xscore_exp"), 1)
                for hd in range(4):
                    b = x_ready(act, "xprob_tr", l, hd)
                    read(copy(xpT[:, hd, :, :], m2(b)))
                cut_acts(xo, h_hi)
                cut_ahead(cutter, (("x_o", l), 3))
                barrier(act, f"cross{l}")
                norm(f"norm_ffn2{l}", f"cross{l}")
                ffn("ffn2", l)
                if l < LAYERS - 1:
                    prime(cutter, ("ffn1", l + 1, "gate", 0))
                barrier(act, f"ffn2{l}")

        @block.vector
        def _(dve):
            def read(ins):
                ins.then_inc(x_read["dve"], 1)

            def dread(ins):
                ins.then_inc(d_read["dve"], 1)

            def tt_(o, a, b, op):
                return dve.tensor_tensor(o, a, b, op)

            def cut_weights(j, n):
                dve.wait_ge(hi_cut, j + 1)
                words = KD * P if n in half_slot else SLOT
                tt_(w_lo[j % 2][:, 0:words], ring[n % RING][:, 0:words], w_hi[j % 2][:, 0:words].bitcast(F32),
                    ALU.subtract).then_inc(lo_cut, 1)

            cutter = Cutter(dve, cut_weights)
            pieces = [0]

            def cut_act(src, hi, lo):
                pieces[0] += 1
                dve.wait_ge(S("act_hi_cut"), pieces[0])
                return tt_(lo, src, hi.bitcast(F32), ALU.subtract)

            def cut_acts(src, flag):
                dve.drain().then_inc(S("act_made"), 4)
                for i in range(4):
                    two = slice(2 * i, 2 * i + 2)
                    cut_act(src[:, two, :], h_hi[:, two, :], h_lo[:, two, :])
                dve.drain().then_inc(S(flag), 1)

            def norm(g, dst=None, src=None, halves_=(h_hi, h_lo), before_cut=None):
                src = x if src is None else src
                XB.was_read(dve, ("norm", g))
                dve.reciprocal(rstd[:, :], rstd[:, :])
                dve.drain()
                dst = h if dst is None else dst
                if before_cut:
                    before_cut()
                for i in range(5):
                    if i < 4:
                        for k in (2 * i, 2 * i + 1):
                            ins = dve.scalar_tensor_tensor(out=dst[:, k, :], in0=src[:, k, :], scalar=pc(g, k),
                                                           in1=rstd[:, :], op0=ALU.mult, op1=ALU.mult)
                        ins.then_inc(S("act_made") if halves_ else h_ready, 1)
                    if i and halves_:
                        two = slice(2 * i - 2, 2 * i)
                        cut_act(dst[:, two, :], *(v[:, two, :] for v in halves_)).then_inc(h_ready, 1)

            def x_event():
                dve.drain().then_inc(x_ready_s, 1)

            def ffn(which, l):
                for f in range(FSTEPS):
                    cut_ahead(cutter, (which, l, "gate", f))
                    cut_ahead(cutter, (which, l, "up", f))
                    b = m2(d_ready(dve, (which, l, "up", f)))
                    DB.was_read(dve, (which, l, "gate", f))
                    dread(tt_(fa[:, f % 2, :, :], b, sg[:, f % 2, :, :], ALU.mult))
                    if f > 1:
                        dve.wait_ge(slots_done, SN[((which, l, "down", f - 2), f - 2)] + 1)
                    cut_act(fa[:, f % 2, :, :], fa_hi[:, f % 2, :, :], fa_lo[:, f % 2, :, :]).then_inc(S("fa_cut"), 1)
                for i in range(4):
                    b = m2(x_ready(dve, which, l, i))
                    read(dve.scalar_tensor_tensor(out=x[:, 2 * i:2 * i + 2, :], in0=b, scalar=0.5,
                                                  in1=x[:, 2 * i:2 * i + 2, :], op0=ALU.mult, op1=ALU.add))
                x_event()

            dve.wait_ge(S("par_in"), 16)
            dve.wait_ge(S("con_in"), 16)
            lam = par[:, PCOL["lru_lambda"]:PCOL["lru_lambda"] + 16]
            t0, t1, t2, t3 = (tiny[:, i:i + 16] for i in (0, 16, 32, 48))
            dve.tensor_scalar(t0, lam, -1.0, None, ALU.mult)
            dve.drain()
            tt_(t0, t0, lam, ALU.max)
            dve.drain().then_inc(S("lam_abs"), 1)
            norm("g_mix", before_cut=lambda: prime(cutter, ("a_x", 0)))
            dve.wait_ge(S("lam_exp"), 1)
            dve.tensor_scalar(t2, t1, 2.0, None, ALU.add)
            dve.drain()
            dve.reciprocal(t2, t2)
            dve.drain()
            tt_(t1, t1, t2, ALU.mult)
            dve.drain()
            tt_(t2, t1, t1, ALU.mult)
            dve.memset(t3, 1.0 / 21)
            for n in range(19, 0, -2):
                dve.drain()
                tt_(t3, t3, t2, ALU.mult)
                dve.drain()
                dve.tensor_scalar(t3, t3, 1.0 / n, None, ALU.add)
            dve.drain()
            tt_(t3, t3, t1, ALU.mult)
            dve.tensor_scalar(t0, lam, -1.0, 0.0, ALU.mult, ALU.max)
            dve.drain()
            dve.scalar_tensor_tensor(out=t3, in0=t3, scalar=2.0, in1=t0, op0=ALU.mult, op1=ALU.add)
            dve.drain()
            dve.tensor_scalar(t2, t3, -8.0, None, ALU.mult)
            dve.tensor_scalar(t3, t3, -16.0, None, ALU.mult)
            dve.drain().then_inc(S("lru_c"), 1)

            def conv(b, dst, taps, centre, w, bias):
                b = m2(b)
                order = [centre] + [j for j in range(taps) if j != centre]
                for j in order:
                    o = j - centre
                    for m in range(2):
                        if o == 0:
                            ins = dve.tensor_scalar(dst[m], b[:, m, :], w(j, m), bias(m), ALU.mult, ALU.add)
                        else:
                            a0, a1 = max(0, -o), T - max(0, o)
                            ins = dve.scalar_tensor_tensor(out=dst[m][:, a0:a1], in0=b[:, m, a0 + o:a1 + o],
                                                           scalar=w(j, m), in1=dst[m][:, a0:a1],
                                                           op0=ALU.mult, op1=ALU.add)
                    if j != order[-1]:
                        dve.drain()
                dread(ins)

            for i in range(4):
                cut_ahead(cutter, ("a_x", i))
                conv(d_ready(dve, ("a_x", i)), [xa[:, 2 * i + m, :] for m in range(2)], 4, 2,
                     lambda j, m: pc("conv_a_w", 8 * j + 2 * i + m), lambda m: pc("conv_a_b", 2 * i + m))
            tr = []
            for part, base in (("v", 0), ("x1", 8), ("x2", 16)):
                for i in range(4):
                    cut_ahead(cutter, ("hy_" + part, i))
                    b = d_ready(dve, ("hy_" + part, i))
                    if part == "x2":
                        dst = [x2[:, 2 * i + m, :] for m in range(2)]
                    else:
                        dst = [sq[:, 2 * (i % 2) + m, :] for m in range(2)]
                        if len(tr) > 1:
                            x_ready(dve, "hy_tr", *tr[-2])
                        tr.append((part, i))
                    conv(b, dst, 3, 1, lambda j, m: pc("conv_b_w", 24 * j + base + 2 * i + m),
                         lambda m: pc("conv_b_b", base + 2 * i + m))

            def lru(d, *cuts):
                cut_ahead(cutter, cuts[0])
                dve.wait_ge(S("lru_exp"), d + 1)
                dve.tensor_scalar(le[:, :, :], le[:, :, :], 1.0, -1.0, ALU.min, ALU.mult)
                tt_(li[:, :, :], li[:, :, :], xa, ALU.mult)
                dve.drain()
                first = 0 if d == 0 else T - 1
                dve.memset(le[:, :, first:first + 1], 0.0)
                dve.drain().then_inc(S("lru_neg"), 1)
                cut_ahead(cutter, cuts[1])
                dve.wait_ge(S("lru_mult"), d + 1)
                tt_(li[:, :, :], li[:, :, :], le[:, :, :], ALU.mult)
                dve.drain()
                for c in range(KD):
                    if c == KD // 2:
                        cut_ahead(cutter, cuts[2])
                    if d == 0:
                        dve.tensor_tensor_scan(lh[:, c, :], lr[:, c, :], li[:, c, :], 0.0, ALU.mult, ALU.add)
                    else:
                        dve.tensor_tensor_scan(le[:, c, ::-1], lr[:, c, ::-1], li[:, c, ::-1], 0.0,
                                               ALU.mult, ALU.add)
                dve.drain().then_inc(S("lru_scan"), 1)

            lru(0, ("a_gate", 1), ("a_gate", 2), ("a_gate", 3))
            cut_ahead(cutter, ("gates", 1))
            lru(1, ("gates", 2), ("gates", 3), ("gates", 4))
            cut_ahead(cutter, ("gates", 5))
            tt_(le[:, :, :], lh[:, :, :], le[:, :, :], ALU.add)
            dve.drain()
            DB.was_read(dve, ("a_gate", 3))
            tt_(le[:, :, :], le[:, :, :], ga, ALU.mult)
            cut_acts(le, "lru_out")
            cut_ahead(cutter, ("gates", 7))

            def gate_a(i):
                cut_ahead(cutter, ("w_a_out", i))
                b = m2(d_ready(dve, ("w_a_out", i)))
                dread(tt_(gated[:, 2 * i:2 * i + 2, :], b, gs[:, 2 * i:2 * i + 2, :], ALU.mult))

            DB.was_read(dve, ("gates", 7))
            for i in range(2):
                gate_a(2 * i)
                b = x_ready(dve, "filt", i)[0:64, 0:T]
                v, k = sq[0:64, 1 + i, :], sq[0:64, 3, :]
                read(dve.tensor_scalar(v, b, pc(f"filt_b{i + 1}", 0, 0, 64), pc("filt_freq", i, 0, 64),
                                       ALU.add, ALU.mult))
                dve.drain()
                dve.tensor_scalar(k, v, 1 / (2 * math.pi), L2, ALU.mult, ALU.add)
                dve.drain()
                dve.tensor_scalar(k, k, L2, None, ALU.subtract)
                dve.drain()
                for part in (TWO_PI_HI, TWO_PI_LO):
                    dve.scalar_tensor_tensor(out=v, in0=k, scalar=-part, in1=v, op0=ALU.mult, op1=ALU.add)
                    dve.drain()
                dve.tensor_scalar(v, v, 3.1415925, -3.1415925, ALU.min, ALU.max)
                dve.drain().then_inc(S("filt_red"), 1)
                gate_a(2 * i + 1)
            dve.wait_ge(S("decay"), 1)
            bias_row = at(8, 2, D, parts=1)
            f0, f1 = (sq[:, i:i + 2, :].rearrange("p a t -> p (a t)") for i in (4, 6))
            dve.wait_ge(S("bias_in"), 16)
            for n in range(2):
                for tt in range(TT):
                    for half in range(2):
                        cs = slice(half * 512, (half + 1) * 512)
                        for d, dst in ((0, f0), (1, f1)):
                            b = x_ready(dve, "taps", n, tt, half, d)
                            read(tt_(dst, b[:, :], decay[:, tt, cs], ALU.mult))
                        dve.drain()
                        if tt == 0:
                            dve.memset(f1[0:1, :], 0.0)
                            tt_(f0[0:1, :], f0[0:1, :], bias_row[:, n, cs], ALU.add)
                            dve.drain()
                        tt_(taps_s[:, tt, cs], f0, f1, ALU.add)
                        tt_(taps_d[:, tt, cs], f0, f1, ALU.subtract)
                        dve.drain()
                dve.drain().then_inc(S("taps_ready"), 1)
                XB.was_read(dve, ("spec_k", n, 3, 1))
                for half in range(2):
                    cs = slice(half * 512, (half + 1) * 512)
                    for f in range(2):
                        kr, ki = spec_k[:, f, cs], spec_k[:, 2 + f, cs]
                        yr, yi = spec_y[:, f, cs], spec_y[:, 2 + f, cs]
                        ur = x_ready(dve, "spec_u", n, half, f, 0)
                        tt_(yr, ur[:, :], kr, ALU.mult)
                        read(tt_(yi, ur[:, :], ki, ALU.mult))
                        ui = x_ready(dve, "spec_u", n, half, f, 1)
                        tt_(f0, ui[:, :], ki, ALU.mult)
                        read(tt_(f1, ui[:, :], kr, ALU.mult))
                        dve.drain()
                        tt_(yr, yr, f0, ALU.subtract)
                        tt_(yi, yi, f1, ALU.add)
                        dve.drain().then_inc(S("spec_y"), 1)
                for i in range(4):
                    b = x_ready(dve, "inv", n, i)
                    if n == 0:
                        tt, cs = i // 2, slice((i % 2) * 512, (i % 2 + 1) * 512)
                        read(tt_(v_tok[:, tt, cs], b[:, :], x1_tok[:, tt, cs], ALU.mult))
                    else:
                        read(tt_(x2[:, 2 * i:2 * i + 2, :], m2(b), x2[:, 2 * i:2 * i + 2, :], ALU.mult))
                if n == 0:
                    dve.drain().then_inc(S("z_tok"), 4)
            cut_acts(x2, "z_cut")
            for i in range(4):
                cut_ahead(cutter, ("w_b_out", i))
                b = m2(d_ready(dve, ("w_b_out", i)))
                two = slice(2 * i, 2 * i + 2)
                dread(tt_(sq[:, two, :], b, gs[:, KD + 2 * i:KD + 2 * i + 2, :], ALU.mult))
            dve.drain()
            tt_(gated[:, :, :], gated[:, :, :], sq[:, :, :], ALU.add)
            cut_acts(gated, "merged")
            for i in range(4):
                cut_ahead(cutter, ("w_o", i))
                b = m2(d_ready(dve, ("w_o", i)))
                two = slice(2 * i, 2 * i + 2)
                dread(tt_(x[:, two, :], b, x[:, two, :], ALU.add))
            x_event()
            barrier(dve, "conv")

            norm("g_ffn", halves_=None)
            b = x_ready(dve, "router")[:, 0:32].rearrange("p (t e) -> p t e", t=TT)
            dve.tensor_reduce(tiny[:, 4:6], b, AXX, ALU.max)
            dve.drain()
            read(tt_(lg, b, tiny[:, 4:6].unsqueeze(2).broadcast_to([P, TT, 16]), ALU.subtract))
            dve.drain().then_inc(S("lg_shift"), 1)
            dve.wait_ge(S("aff_exp"), 1)
            dve.reciprocal(tiny[:, 2:4], tiny[:, 0:2])
            dve.drain()
            tt_(aff, aff, tiny[:, 2:4].unsqueeze(2).broadcast_to([P, TT, 16]), ALU.mult)
            dve.drain().then_inc(S("aff"), 1)
            b = x_ready(dve, "affT")
            dve.memset(ones16, 1.0)
            read(dve.tensor_copy(wk, b[0:16, 0:T]))
            for _ in range(CAP // 8):
                dve.drain()
                dve.max(top8, wk)
                dve.drain()
                dve.match_replace(wk, top8, wk, -1.0)
            dve.drain()
            dve.tensor_scalar(msk, wk, 0.0, None, ALU.is_lt)
            dve.drain()
            dve.tensor_tensor_scan(slotT, ones16, msk, 0.0, ALU.mult, ALU.add)
            dve.drain()
            tt_(slotT, slotT, msk, ALU.mult)
            dve.drain().then_inc(S("slotT"), 1)
            b = x_ready(dve, "slot_tr")[:, 0:32].rearrange("p (t e) -> p t e", t=TT)
            read(dve.tensor_copy(slots, b))
            dve.drain()
            for tt in range(TT):
                tt_(onehot[:, tt, :, :], cst("iota", CAP).unsqueeze(1).broadcast_to([P, EXPERTS, CAP]),
                    slots[:, tt, :].unsqueeze(2).broadcast_to([P, EXPERTS, CAP]), ALU.is_equal)
            dve.drain()
            for tt in range(TT):
                for j in range(4):
                    tt_(weighted[:, tt, :, j * CAP:(j + 1) * CAP], onehot[:, tt, :, :],
                        aff[:, tt, :].unsqueeze(2).broadcast_to([P, EXPERTS, CAP]), ALU.mult)
            dve.drain().then_inc(S("weighted"), 1)
            for i in range(8):
                b = x_ready(dve, "xe", i)
                read(dve.tensor_copy(xe[:, i, :], b[:, :]))
            dve.drain()
            with dve.Fori(0, EXPERTS) as e:
                dve.wait_ge(slots_done, 24 * e + (MOE - 8))
                dve.tensor_copy(xs, xe[:, :, bass.ds(e * CAP, CAP)]).then_inc(S("xs_ready"), 1)
                dve.wait_ge(slots_done, 24 * e + MOE + 16)
                dve.wait_ge(S("sg_e"), e + 1)
                tt_(act_e, psd[1][:, :], sg_e, ALU.mult).then_inc(S("act_e"), 1)
                dve.wait_ge(slots_done, 24 * e + MOE + 24)
                dve.tensor_copy(ye[:, 1, :], psd[3][:, :]).then_inc(S("ye_ready"), 1)
            for i in range(4):
                b = m2(x_ready(dve, "moe_acc", i))
                read(dve.tensor_copy(x[:, 2 * i:2 * i + 2, :], b))
            x_event()
            barrier(dve, "merge")
            prime(cutter, ("ffn1", 0, "gate", 0))
            norm("g_final", x, halves_=None)
            x_event()

            for l in range(LAYERS):
                norm(f"norm_ffn1{l}")
                ffn("ffn1", l)
                prime(cutter, (("mix_in", l), 0))
                barrier(dve, f"ffn1{l}")
                norm(f"norm_mix{l}")
                cut_ahead(cutter, (("mix_in", l), 10))

                XB.was_read(dve, ("qk_norm", l, 2))
                dve.reciprocal(rs6, rs6)
                dve.drain()
                for j in range(6):
                    g = pc(f"b_{'q' if j < 3 else 'k'}_gain{l}")
                    dve.scalar_tensor_tensor(out=pb[:, 10 + j, :], in0=pb[:, 10 + j, :], scalar=g, in1=rs6[:, j, :],
                                             op0=ALU.mult, op1=ALU.mult)
                dve.drain().then_inc(S("qk_ready"), 1)
                dve.memset(up[:, :, 0:16], 0.0)
                dve.tensor_copy(up[:, :, 16:16 + T], pb[:, 19:21, :])
                dve.drain()
                src, start = up, 0
                for step, dst in ((1, wa), (2, wb), (4, wa), (8, wb)):
                    start += step
                    tt_(dst[:, :, start:], src[:, :, start:], src[:, :, start - step:16 + T - step], ALU.add)
                    dve.drain()
                    tile, half = ((0, 0), (0, 1), (1, 0), (1, 1))[int(math.log2(step))]
                    r = slice(64 * half, 64 * half + 64)
                    inv_n = con[r, CCOL["invcnt"] + tile * T:CCOL["invcnt"] + (tile + 1) * T]
                    tt_(sq[r, 6 + tile, :], dst[r, tile, 16:16 + T], inv_n, ALU.mult)
                    src = dst
                dve.drain()
                tt_(up[:, :, 16:16 + T], sq[:, 6:8, :], up[:, :, 16:16 + T], ALU.subtract)
                dve.drain().then_inc(S("pooled"), 1)
                dve.wait_ge(S(f"att_in{l}"), 32)
                for hd in range(6):
                    for it, (lo_, hi_) in enumerate(((0, P), (P, AW))):
                        b = x_ready(dve, "score", l, hd, it)
                        pr = prob[:, hd, lo_:hi_]
                        read(dve.scalar_tensor_tensor(out=pr, in0=b[:, 0:hi_ - lo_], scalar=64 ** -0.5,
                                                      in1=rbias[:, hd, lo_:hi_], op0=ALU.mult, op1=ALU.add))
                        dve.drain()
                        dve.tensor_reduce(tiny[:, 24 + 2 * hd + it:25 + 2 * hd + it], pr, AXX, ALU.max)
                    dve.drain()
                    dve.tensor_scalar(tiny[:, 2 * hd:2 * hd + 2], tiny[:, 24 + 2 * hd:26 + 2 * hd], -1.0, None, ALU.mult)
                    dve.drain().then_inc(S("score_max"), 1)
                for hd in range(6):
                    dve.wait_ge(S("score_exp"), 6 * l + hd + 1)
                    dve.reciprocal(tiny[:, 40 + 2 * hd:42 + 2 * hd], tiny[:, 12 + 2 * hd:14 + 2 * hd])
                    dve.drain()
                    for it, (lo_, hi_) in enumerate(((0, P), (P, AW))):
                        j = 40 + 2 * hd + it
                        dve.tensor_scalar(prob[:, hd, lo_:hi_], prob[:, hd, lo_:hi_], tiny[:, j:j + 1], None, ALU.mult)
                    dve.drain().then_inc(S("prob"), 1)
                barrier(dve, f"att{l}")

                mu = par[:, PCOL[f"a_mu{l}"]:PCOL[f"a_mu{l}"] + 10]
                dve.tensor_scalar(tiny[:, 0:10], mu, -1.0, 1.0, ALU.mult, ALU.add)
                dve.memset(MT, 0.0)
                dve.drain()
                for j in range(10):
                    dve.tensor_scalar(ts[:, j, :], pb[:, j, :], tiny[:, j:j + 1], None, ALU.mult)
                dve.drain()
                for j in range(10):
                    dve.scalar_tensor_tensor(out=ts[:, j, 1:T], in0=pb[:, j, 0:T - 1], scalar=mu[:, j:j + 1],
                                             in1=ts[:, j, 1:T], op0=ALU.mult, op1=ALU.add)
                dve.drain().then_inc(S("shifted"), 1)
                r_, k_, v_ = ts[:, 0:3, :], ts[:, 3:6, :], ts[:, 6:9, :]
                for j in range(HP):
                    dve.tensor_scalar(kk[:, j, :], k_[:, j, :], pc(f"a_k_k{l}", j), None, ALU.mult)
                dve.drain().then_inc(S("kk_raw"), 1)
                XB.was_read(dve, ("lora", l, 0, 1))
                dve.tensor_scalar(rt[:, :, :], rt[:, :, :], -math.exp(-0.5), None, ALU.mult)
                dve.drain()
                for j in range(HP):
                    dve.tensor_tensor_scan(kt[:, j, :], cst("reset", T), rt[:, j, :], 0.0, ALU.mult, ALU.add)
                if l:
                    XB.was_read(dve, ("vup", l, 1))
                    tt_(v_first[:, :, :], v_first[:, :, :], v_, ALU.subtract)
                    dve.drain()
                    tt_(v_first[:, :, :], v_first[:, :, :], be[:, :, :], ALU.mult)
                    dve.drain()
                    tt_(v_, v_, v_first[:, :, :], ALU.add)
                else:
                    dve.tensor_copy(v_first[:, :, :], v_)
                dve.drain()
                tt_(be[:, :, :], kt[:, :, :], rt[:, :, :], ALU.subtract)
                dve.drain().then_inc(S("decays"), 1)
                XB.was_read(dve, ("lora", l, 2, 1))
                XB.was_read(dve, ("kk_norm", l, 1))
                dve.tensor_scalar(al[:, :, :], al[:, :, :], 1e-12, None, ALU.max)
                for j in range(HP):
                    dve.tensor_scalar(rt[:, j, :], aa[:, j, :], -1.0, pc(f"a_k_a{l}", j), ALU.add, ALU.mult)
                dve.drain()
                dve.reciprocal(al[:, :, :], al[:, :, :])
                dve.scalar_tensor_tensor(out=k_, in0=rt[:, :, :], scalar=1.0, in1=k_, op0=ALU.add, op1=ALU.mult)
                dve.drain()
                tt_(kk, kk, al[:, :, :], ALU.mult)
                dve.wait_ge(S("decay_exp"), l + 1)
                dve.drain()
                dve.scalar_tensor_tensor(out=al[:, :, :], in0=kk, scalar=-1.0, in1=e3, op0=ALU.mult, op1=ALU.mult)
                tt_(be[:, :, :], kk, aa, ALU.mult)
                tt_(rt[:, :, :], r_, e1, ALU.mult)
                tt_(kt[:, :, :], k_, e2, ALU.mult)
                dve.drain()
                tt_(be[:, :, :], be[:, :, :], e2, ALU.mult)
                dve.drain().then_inc(S("rw_scaled"), 1)

                rows = [slice(64 * p, 64 * p + 64) for p in range(2)]
                for tt in range(TT):
                    tok = slice(tt * P, (tt + 1) * P)
                    b = tri(x_ready(dve, "rw_tr", l, tt, "b"))
                    for c in range(4):
                        ins = dve.tensor_scalar(bm[:, :, c, :], b, con[:, CCOL["chunk"] + c:CCOL["chunk"] + c + 1],
                                                None, ALU.mult)
                    read(ins)

                    def mask(name):
                        return cst(name, P).unsqueeze(1).broadcast_to([P, HP, P])

                    for name, kinds in (("A", (("Aoff", "off32"), ("A", "low16"))), ("AT", (("AT", "up16"),)),
                                        ("BT", (("BT", "up32"),)), ("CT", (("CT", "upi32"),)),
                                        ("DT", (("DT", "upi32"),))):
                        for p in range(2):
                            b = tri(x_ready(dve, name, l, tt, p))
                            if name == "BT" and p == 0:
                                dve.drain()
                                for pp in range(2):
                                    tt_(MATS["Q"][pp], MATS["AT"][pp], mask("ident"), ALU.add)
                            for dst, mk in kinds:
                                ins = tt_(MATS[dst][p], b, mask(mk), ALU.mult)
                            read(ins)
                    for name in ("Q2", "Q4", "Q8", "Q32"):
                        dve.drain()
                        for p in range(2):
                            b = tri(x_ready(dve, name, l, tt, p))
                            read(tt_(MATS["Q"][p], b, MATS["Q"][p], ALU.add))
                    for q in range(HP):
                        b = x_ready(dve, "M", l, tt, q)
                        for p in range(2):
                            ins = tt_(MT[rows[p], :, q, rows[p]],
                                      b[rows[p], 0:T].rearrange("p (c n) -> p c n", c=4),
                                      ident[rows[p], rows[p]].unsqueeze(1).broadcast_to([64, 4, 64]), ALU.add)
                        read(ins)
                        ends = e1[:, q, tt * P + CH - 1:(tt + 1) * P:CH]
                        b = x_ready(dve, "N", l, tt, q)
                        read(tt_(Np[:, :, q, :], b[:, 0:T].rearrange("p (c n) -> p c n", c=4),
                                 ends.unsqueeze(2).broadcast_to([P, 4, 64]), ALU.mult))
                        b = x_ready(dve, "RY", l, tt, q)
                        tt_(RT[:, q, :], b[:, 0:P], rt[:, q, tok], ALU.add)
                        read(dve.tensor_copy(y0T[:, q, :], b[:, P:T]))
                    if tt == 0:
                        dve.memset(Xs[:, 0, :, :], 0.0)
                    else:
                        dve.tensor_copy(Xs[:, 0, :, :], Xs[:, 4, :, :])
                    dve.drain().then_inc(S("state0"), 1)
                    for c in range(4):
                        b = tri(x_ready(dve, "S", l, tt, c), 64)
                        for q in range(HP):
                            end = tt * P + (c + 1) * CH - 1
                            ins = dve.scalar_tensor_tensor(out=Xs[:, c + 1, q, :], in0=b[:, q, :],
                                                           scalar=e1[:, q, end:end + 1], in1=Np[:, c, q, :],
                                                           op0=ALU.mult, op1=ALU.add)
                        read(ins)
                    for p in range(2):
                        b = tri(x_ready(dve, "y", l, tt, p))
                        read(tt_(yy[rows[p], :, tok], b[rows[p], :, :], y0T[rows[p], :, :], ALU.add))
                    dve.drain()
                dve.drain().then_inc(S("y_ready"), 1)
                for i in range(2):
                    b, m = m2(x_ready(dve, "mean", l, i)), 2 - i
                    yv = yy[:, 2 * i:2 * i + m, :]
                    read(dve.scalar_tensor_tensor(out=yv, in0=b[:, 0:m, :], scalar=-1.0 / 64, in1=yv,
                                                  op0=ALU.mult, op1=ALU.add))
                dve.drain().then_inc(S("y_mean"), 1)
                for j in range(HP):
                    dve.scalar_tensor_tensor(out=e1[:, j, :], in0=r_[:, j, :], scalar=pc(f"a_r_k{l}", j),
                                             in1=k_[:, j, :], op0=ALU.mult, op1=ALU.mult)
                dve.drain().then_inc(S("rk_ready"), 1)
                XB.was_read(dve, ("var", l, 1))
                dve.reciprocal(al[:, :, :], al[:, :, :])
                dve.drain()
                tt_(yy, yy, al[:, :, :], ALU.mult)
                dve.drain()
                for j in range(HP):
                    dve.tensor_scalar(yy[:, j, :], yy[:, j, :], pc(f"a_gn_g{l}", j), pc(f"a_gn_b{l}", j),
                                      ALU.mult, ALU.add)
                for i in range(2):
                    b, m = m2(x_ready(dve, "bonus", l, i)), 2 - i
                    two = slice(2 * i, 2 * i + m)
                    read(tt_(e2[:, two, :], b[:, 0:m, :], v_[:, two, :], ALU.mult))
                dve.drain()
                tt_(yy, yy, e2, ALU.add)
                dve.drain()
                tt_(ycat[:, 0:3, :], yy, gg, ALU.mult)
                cut_acts(ycat, "mix_cat")
                for i in range(4):
                    cut_ahead(cutter, (("mix_out", l), i))
                    b = m2(d_ready(dve, (("mix_out", l), i)))
                    two = slice(2 * i, 2 * i + 2)
                    dread(tt_(x[:, two, :], b, x[:, two, :], ALU.add))
                x_event()
                barrier(dve, f"rwkv{l}")

                norm(f"norm_mem{l}", src=memT, halves_=(mn_hi, mn_lo))
                cut_ahead(cutter, (("x_v", l), 3))
                norm(f"norm_cross{l}")
                cut_ahead(cutter, (("x_q", l), 3))
                for j, (name, v) in enumerate((("k", xk), ("q", xq))):
                    XB.was_read(dve, ("xnorm", l, name, 1))
                    rs4 = memT[:, 4 * j:4 * j + 4, :]
                    dve.reciprocal(rs4, rs4)
                    dve.drain()
                    for c in range(KD):
                        dve.scalar_tensor_tensor(out=v[:, c, :], in0=v[:, c, :], scalar=pc(f"x_{name}_gain{l}", c % 2),
                                                 in1=rs4[:, c // 2, :], op0=ALU.mult, op1=ALU.mult)
                dve.drain().then_inc(S("xqk_ready"), 1)
                for hd in range(4):
                    for it in range(TT):
                        j = 2 * hd + it
                        b = x_ready(dve, "xscore", l, hd, it)
                        read(dve.tensor_scalar(xprob[:, j, :], b[:, 0:T], 1.0 / 16, None, ALU.mult))
                        dve.drain()
                        dve.tensor_reduce(tiny[:, 24 + j:25 + j], xprob[:, j, :], AXX, ALU.max)
                    dve.drain()
                    dve.tensor_scalar(tiny[:, 2 * hd:2 * hd + 2], tiny[:, 24 + 2 * hd:26 + 2 * hd], -1.0, None, ALU.mult)
                    dve.drain().then_inc(S("xscore_max"), 1)
                for hd in range(4):
                    dve.wait_ge(S("xscore_exp"), 4 * l + hd + 1)
                    dve.reciprocal(tiny[:, 40 + 2 * hd:42 + 2 * hd], tiny[:, 12 + 2 * hd:14 + 2 * hd])
                    dve.drain()
                    for it in range(TT):
                        j = 2 * hd + it
                        dve.tensor_scalar(xprob[:, j, :], xprob[:, j, :], tiny[:, 40 + j:41 + j], None, ALU.mult)
                    dve.drain().then_inc(S("xprob"), 1)
                for hd in range(4):
                    b = x_ready(dve, "xatt", l, hd)
                    read(dve.tensor_copy(xo[:, 2 * hd:2 * hd + 2, :], m2(b)))
                cut_acts(xo, "xo_cut")
                for i in range(4):
                    cut_ahead(cutter, (("x_o", l), i))
                    b = m2(d_ready(dve, (("x_o", l), i)))
                    two = slice(2 * i, 2 * i + 2)
                    dread(tt_(x[:, two, :], b, x[:, two, :], ALU.add))
                x_event()
                barrier(dve, f"cross{l}")
                norm(f"norm_ffn2{l}")
                ffn("ffn2", l)
                if l < LAYERS - 1:
                    prime(cutter, ("ffn1", l + 1, "gate", 0))
                barrier(dve, f"ffn2{l}")

        @block.gpsimd
        def _(pool):
            def load(dst, src, flag):
                pool.dma_start(dst, src).then_inc(S(flag), 16)

            d_ready(pool, ("a_x", 0))
            load(bd[:, :, :, :], A["lru_bd"].rearrange("p (s c n) -> p s c n", s=4, c=KD), "bd_in")
            pool.wait_ge(S("lru_scan"), 2)
            load(zT, A["zT"], "filt_in")
            load(filt_w[0:33, 0:64], A["filt_w1"], "filt_in")
            load(filt_w[0:64, 64:128], A["filt_w2"], "filt_in")
            load(decay[:, 1, :], A["deltas"].broadcast_to([P, D]), "filt_in")
            load(at(0, 8 * T), A["dft"], "dft_in")
            pool.wait_ge(S("lru_out"), 1)
            load(at(8, 2 * D, parts=1), A["filt_bias"], "bias_in")
            w3 = A["filt_w3"].rearrange("i (n d h c) -> n i d h c", n=2, d=2, h=2)
            load(w3h[:, :, :, :], w3[0], "w3_in0")
            x_ready(pool, "taps", 0, 1, 1, 1)
            load(w3h[:, :, :, :], w3[1], "w3_in1")
            barrier(pool, "conv")
            load(wr[:, :, :], A["w_router"].rearrange("(k p) e -> p k e", p=P), "wr_in")
            barrier(pool, "merge")
            for l in range(LAYERS):
                barrier(pool, f"ffn1{l}")
                load(rbias[:, :, :], A["rel_bias"][l].rearrange("p (h n) -> p h n", h=6), f"att_in{l}")
                load(poolw[:, :, :], A["pool_w"][l].rearrange("p (m n) -> p m n", m=2), f"att_in{l}")
                barrier(pool, f"att{l}")
                load(lora_up, A["lora_up"][l], f"lora_in{l}")
                if l:
                    load(vdn[:, :, :], A["a_v_down"].rearrange("(q p) n -> p q n", p=P), f"lora_in{l}")
                    load(vup, A["a_v_up"], f"lora_in{l}")
                barrier(pool, f"rwkv{l}")
                load(memT[:, :, :], A["memT"].rearrange("(k p) t -> p k t", p=P), "mem_in")
                barrier(pool, f"cross{l}")
                barrier(pool, f"ffn2{l}")

        @block.sync
        def _(sp):
            def slot(n, src, words=SLOT):
                if n >= RING:
                    sp.wait_ge(lo_cut, n - RING + 1)
                sp.dma_start(ring[n % RING][:, 0:words], src).then_inc(land[n % RING], 16)

            sp.dma_start(x[:, :, :], A["xT"].rearrange("(k p) t -> p k t", p=P)).then_inc(S("x_in"), 16)
            sp.dma_start(con[:, :], A["consts"]).then_inc(S("con_in"), 16)
            sp.dma_start(par[:, :], A["params"]).then_inc(S("par_in"), 16)
            for n, (_, _, name, i) in enumerate(plan):
                slot(n, A[name][i])
            with sp.Fori(0, EXPERTS) as e:
                for s in range(24):
                    n = MOE + s
                    sp.wait_ge(slots_done, 24 * e + (n - RING + 1))
                    if s < 16:
                        src = A["w_gate" if s < 8 else "w_up"][bass.ds(8 * e + s % 8, 1), :, :]
                        src = src.rearrange("a p c -> (a p) c")
                        dst = ring[n % RING][:, :]
                    else:
                        src = A["w_down"][bass.ds(8 * e + s - 16, 1), :, :, :].rearrange("a i p c -> p (a i) c")
                        dst = ring[n % RING][:, :].rearrange("p (i c) -> p i c", i=2)
                    sp.dma_start(dst, src).then_inc(land[n % RING], 16)
            for m, (_, _, name, (l, i)) in enumerate(after):
                n = AFTER + m
                if m < RING:
                    sp.wait_ge(slots_done, n - RING + 1)
                else:
                    sp.wait_ge(lo_cut, dense_at[n - RING] + 1)
                src, words = A[name][l, i], SLOT
                dst = ring[n % RING][:, :]
                if name.endswith("_wo") and name.startswith("ffn"):
                    src = src.rearrange("i p c -> p i c")
                    dst = dst.rearrange("p (i c) -> p i c", i=2)
                elif name == "mix_in" and i == 10:
                    src, dst = src[:, 0:KD * P], dst[:, 0:KD * P]
                sp.dma_start(dst, src).then_inc(land[n % RING], 16)
            sp.wait_ge(x_ready_s, len(XEV))
            sp.dma_start(out.rearrange("(k p) t -> p k t", p=P), x[:, :, :]).then_inc(S("out_stored"), 16)
            sp.wait_ge(S("out_stored"), 16)


def kernel(**inputs):
    import concourse.bacc as bacc
    from concourse.bass_utils import run_bass_kernel_spmd

    a = {k: np.asarray(v) for k, v in inputs.items()}

    def tiles(w):
        f = w.shape[1] // 256
        return np.ascontiguousarray(w.reshape(KD, P, f, 256).transpose(2, 1, 0, 3)).reshape(f, P, SLOT)

    def columns(v, n):
        v = v.reshape(-1)
        v = np.concatenate([v.reshape(-1, 64)] * 2, axis=1).reshape(-1, P) if v.size in (64, 128) and n * P > v.size \
            else v.reshape(-1, P)
        assert v.shape[0] == n
        return v.T

    PCOL, npc = param_columns()
    params = np.zeros((P, npc), np.float32)
    order = sorted(PCOL, key=PCOL.get)
    for name, nxt in zip(order, order[1:] + [None]):
        n = (PCOL[nxt] if nxt else npc) - PCOL[name]
        if name in a:
            v = a[name]
        elif name == "a_v0":
            v = a["a_v0_2"]
        else:
            v = a[name[:-1] + "_2"][int(name[-1])]
        params[:, PCOL[name]:PCOL[name] + n] = columns(v, n)

    bd = np.zeros((2, 64, 2, 2, KD, 2, 64), np.float32)
    pw = np.zeros((LAYERS, 2, 64, 2, 2, 64), np.float32)
    for half in range(2):
        for kind, name in enumerate(("lru_w_r", "lru_w_i")):
            w = a[name][0].reshape(2, KD, 2, 64, 64)[:, :, half]
            bd[half, :, :, kind, :, half, :] = w.transpose(2, 0, 1, 3)
        pw[:, half, :, :, half, :] = a["c_pool_w_2"].reshape(LAYERS, 2, 2, 64, 64)[:, :, half].transpose(0, 2, 1, 3)

    i, j = np.arange(T)[:, None], np.arange(T)[None, :]
    rel = a["b_rel_bias_2"][:, :, np.clip(i - j, -63, 256) + 63]
    rel = np.where((i // 64 >= j // 64)[None, None], rel, np.float32(-1e30))
    rel = np.concatenate([rel[:, :, 0:P, 0:P], rel[:, :, P:T, :]], axis=3).transpose(0, 2, 1, 3)

    feed = {
        "xT": a["x"][0].T, "memT": a["mem_2"][0].T, "params": params,
        "w_in": tiles(a["w_in"][0]), "w_a_out": tiles(a["w_a_out"][0]), "w_b_out": tiles(a["w_b_out"][0]),
        "w_o": tiles(a["w_o"][0]),
        "lru_bd": bd.reshape(P, -1), "filt_w1": a["filt_w1"][0], "filt_w2": a["filt_w2"][0],
        "filt_w3": a["filt_w3"][0], "filt_bias": a["filt_bias"].reshape(1, 2 * D),
        "w_router": a["w_router"][0],
        "w_gate": a["w_gate"].reshape(EXPERTS * KD, P, FE), "w_up": a["w_up"].reshape(EXPERTS * KD, P, FE),
        "w_down": a["w_down"].reshape(EXPERTS * 8, 2, P, D),
        "mix_in": np.stack([np.concatenate(
            [tiles(w[:, 0:2560]), np.pad(w[:, 2560:].reshape(KD, P, P).transpose(1, 0, 2).reshape(1, P, KD * P),
                                         ((0, 0), (0, 0), (0, SLOT - KD * P)))]) for w in a["w_in_2"]]),
        "mix_out": np.stack([tiles(w) for w in a["w_out_2"]]),
        "x_wkv": np.stack([tiles(w) for w in a["x_wkv_2"]]),
        "x_wq": np.stack([tiles(w) for w in a["x_wq_2"]]),
        "x_wo": np.stack([tiles(w) for w in a["x_wo_2"]]),
        "rel_bias": rel.reshape(LAYERS, P, 6 * 384), "pool_w": pw.reshape(LAYERS, P, 2 * P),
        "lora_up": np.concatenate([a["a_w_up_2"], a["a_a_up_2"], a["a_g_up_2"]], axis=1),
        "a_v_down": a["a_v_down_2"][0], "a_v_up": a["a_v_up_2"][0],
    }
    for which in ("ffn1", "ffn2"):
        feed[f"{which}_wi"] = np.stack([tiles(w) for w in a[f"{which}_wi_2"]])
        feed[f"{which}_wo"] = a[f"{which}_wo_2"].reshape(LAYERS, FSTEPS, 2, P, D)
    feed.update(constants())

    nc = bacc.Bacc("TRN2", target_bir_lowering=False, num_devices=1)
    A, arrays = {}, {}
    for name, v in feed.items():
        arrays[f"in_{name}"] = np.ascontiguousarray(v)
        A[name] = nc.dram_tensor(f"in_{name}", v.shape, F32, kind="ExternalInput").ap()
    out = nc.dram_tensor("out_x", (D, T), F32, kind="ExternalOutput").ap()
    program(nc, A, out)
    r = run_bass_kernel_spmd(nc, [arrays], core_ids=[0])
    return np.ascontiguousarray(r.results[0]["out_x"].T)[None]
```

```python
import math
from contextlib import ExitStack

import numpy as np

import concourse.bass as bass
from concourse import mybir

F32 = mybir.dt.float32
F32R = mybir.dt.float32r
ALU = mybir.AluOpType
ACT = mybir.ActivationFunctionType
AXX = mybir.AxisListType.X

P = 128
T = 256
TT = T // P
D = 1024
KD = D // P
SLOT = 2048
RING = 4
ERING = 12
ESLOTS = 24
EXPERTS, CAP, FE = 16, 32, 2048
EPS = 1e-6
LAYERS = 2
FF = 2816
FSTEPS = FF // 256
AW = 384
HP = AW // P
NPB = 21
CH = 32
SUB = 16
GN_EPS = 64e-5
L2 = 1.5 * 2.0 ** 23
TWO_PI_HI, TWO_PI_LO = 6.28125, 2 * math.pi - 6.28125


def param_columns():
    cols, at = {}, 0
    sizes = [("g_mix", 8), ("conv_a_w", 32), ("conv_a_b", 8), ("lru_b_r", 16), ("lru_b_i", 16),
             ("lru_lambda", 16), ("conv_b_w", 72), ("conv_b_b", 24), ("filt_b1", 1), ("filt_b2", 1),
             ("filt_freq", 2), ("g_ffn", 8), ("g_final", 8)]
    for l in range(LAYERS):
        sizes += [(f"{n}{l}", c) for n, c in (
            ("norm_ffn1", 8), ("norm_mix", 8), ("a_mu", 10), ("a_w0", 3), ("a_a0", 3), ("a_k_k", 3),
            ("a_k_a", 3), ("a_r_k", 3), ("a_gn_g", 3), ("a_gn_b", 3), ("b_q_gain", 1), ("b_k_gain", 1),
            ("c_pool_scale", 2), ("norm_cross", 8), ("norm_mem", 8), ("x_q_gain", 2), ("x_k_gain", 2),
            ("norm_ffn2", 8))]
    sizes += [("a_v0", 3)]
    for n, c in sizes:
        cols[n] = at
        at += c
    return cols, at


def constant_columns():
    cols, at = {}, 0
    for n, c in (("ident", 128), ("ones", 128), ("bones", 128), ("low16", 128), ("up16", 128),
                 ("off32", 128), ("up32", 128), ("upi32", 128), ("iota", 32), ("chunk", 4),
                 ("reset", 256), ("invcnt", 512), ("eps", 1), ("gneps", 1), ("negt", 2)):
        cols[n] = at
        at += c
    return cols, at


def constants():
    cols, n = constant_columns()
    c = np.zeros((P, n), np.float32)
    i = np.arange(P)[:, None]
    j = np.arange(P)[None, :]

    def put(name, a):
        c[:, cols[name]:cols[name] + a.shape[1]] = a

    put("ident", np.eye(P))
    put("ones", np.ones((P, P)))
    put("bones", (i // 64 == j // 64) * 1.0)
    put("low16", ((i // SUB == j // SUB) & (j < i)) * 1.0)
    put("up16", ((i // SUB == j // SUB) & (j > i)) * 1.0)
    put("off32", ((i // CH == j // CH) & (i // SUB > j // SUB)) * 1.0)
    put("up32", ((i // CH == j // CH) & (j > i)) * 1.0)
    put("upi32", ((i // CH == j // CH) & (j >= i)) * 1.0)
    put("iota", np.ones((P, 1)) * np.arange(1, CAP + 1)[None, :])
    put("chunk", (i // CH == np.arange(4)[None, :]) * 1.0)
    t = np.arange(T)[None, :]
    put("reset", np.ones((P, 1)) * (t % CH != 0))
    wins = np.array([[2, 8], [4, 16]])
    inv = np.zeros((P, 2, T))
    for half in range(2):
        for tile in range(2):
            inv[64 * half:64 * half + 64, tile] = 1.0 / np.minimum(t + 1, wins[half, tile])
    put("invcnt", inv.reshape(P, 512))
    put("eps", np.full((P, 1), EPS))
    put("gneps", np.full((P, 1), GN_EPS))
    put("negt", -(i + P * np.arange(2)[None, :]) / (T - 1.0))
    m = np.arange(T, dtype=np.float64)
    th = np.pi * (2 * m + 1) / (2 * T)
    ang = np.arange(T)[:, None] * th[None, :]
    fwd = np.concatenate([np.cos(ang), -np.sin(ang)], axis=1)
    inv = np.concatenate([np.cos(ang).T, -np.sin(ang).T], axis=0) / T
    dft = np.concatenate([fwd.reshape(2, P, 2 * T).transpose(1, 0, 2).reshape(P, 4 * T),
                          inv.reshape(4, P, T).transpose(1, 0, 2).reshape(P, 4 * T)], axis=1)
    f4 = np.float32
    tt = np.linspace(0.0, 1.0, T, dtype=f4)[:, None]
    w = f4(2.0 * math.pi / T) * np.arange(T, dtype=f4)[:, None]
    f = np.linspace(1e-4, 15, 16, dtype=f4)[None, :]
    z = np.concatenate([tt, np.cos(w * f), -np.sin(w * f)], axis=-1)
    lo, hi = math.log(1e-2) / 1.5, math.log(1e-2) / 0.3
    deltas = np.abs(np.linspace(lo, hi, D, dtype=f4))[None, :]
    return {"consts": c, "dft": dft.astype(f4), "zT": np.ascontiguousarray(z.T.astype(f4)), "deltas": deltas.astype(f4)}


def stream_plan():
    plan = []
    for part, first, count in (("a_x", 0, 4), ("hy_v", 8, 4), ("hy_x1", 12, 4), ("hy_x2", 16, 4),
                               ("a_gate", 4, 4), ("gates", 20, 8)):
        plan += [(part, i, "w_in", first + i) for i in range(count)]
    for part in ("w_a_out", "w_b_out", "w_o"):
        plan += [(part, i, part, i) for i in range(4)]
    moe = len(plan)
    after = []

    def ffn(l, which):
        for f in range(FSTEPS + 1):
            if f < FSTEPS:
                after.append(((which, l, "gate", f), f, f"{which}_wi", (l, f)))
                after.append(((which, l, "up", f), f, f"{which}_wi", (l, FSTEPS + f)))
            if f:
                after.append(((which, l, "down", f - 1), f - 1, f"{which}_wo", (l, f - 1)))

    for l in range(LAYERS):
        ffn(l, "ffn1")
        after += [(("mix_in", l), i, "mix_in", (l, i)) for i in range(11)]
        after += [(("mix_out", l), i, "mix_out", (l, i)) for i in range(4)]
        after += [(("x_k", l), i, "x_wkv", (l, i)) for i in range(4)]
        after += [(("x_v", l), i, "x_wkv", (l, 4 + i)) for i in range(4)]
        after += [(("x_q", l), i, "x_wq", (l, i)) for i in range(4)]
        after += [(("x_o", l), i, "x_wo", (l, i)) for i in range(4)]
        ffn(l, "ffn2")
    return plan, moe, after


class Banks:

    def __init__(self, plan, banks, sems):
        self.banks, self.sems, self.reader, self.count, self.at = banks, sems, [], [], {}
        seen = {"act": 0, "dve": 0, None: 0}
        for g, (key, reader) in enumerate(plan):
            seen[reader] += 1
            self.at[key] = g
            self.reader.append(reader)
            self.count.append(seen[reader])
        self.next = 0

    def bank(self, key):
        return self.banks[self.at[key] % 4]

    def was_read(self, eng, key):
        g = self.at[key]
        eng.wait_ge(self.sems[self.reader[g]], self.count[g])

    def claim(self, pe, key):
        g = self.at[key]
        assert g == self.next, (key, g, self.next)
        self.next += 1
        if g >= 4 and self.reader[g - 4]:
            pe.wait_ge(self.sems[self.reader[g - 4]], self.count[g - 4])
        return self.banks[g % 4]


def dense_plan():
    plan = []
    for part, count, reader in (("a_x", 4, "dve"), ("hy_v", 4, "dve"), ("hy_x1", 4, "dve"), ("hy_x2", 4, "dve"),
                                ("a_gate", 4, "act"), ("gates", 8, "act"),
                                ("w_a_out", 4, "dve"), ("w_b_out", 4, "dve"), ("w_o", 4, "dve")):
        plan += [((part, i), reader) for i in range(count)]
    plan += [(("moe", i), None) for i in range(4)]

    def ffn(l, which):
        for f in range(FSTEPS):
            plan.append(((which, l, "gate", f), "dve"))
            plan.append(((which, l, "up", f), "dve"))

    for l in range(LAYERS):
        ffn(l, "ffn1")
        for part, count, reader in (("mix_in", 11, "dve"), ("mix_out", 4, "dve"), ("x_k", 4, "act"),
                                    ("x_v", 4, "act"), ("x_q", 4, "act"), ("x_o", 4, "dve")):
            plan += [(((part, l), i), reader) for i in range(count)]
        ffn(l, "ffn2")
    return plan


def small_plan():
    plan = []

    def add(reader, *key):
        plan.append((key, reader))

    add("act", "norm", "g_mix")
    for part in ("v", "x1"):
        for i in range(4):
            add("act", "hy_tr", part, i)
    for d in range(2):
        for kind in range(2):
            for i in range(4):
                add("act", "lru", d, kind, i)
    add("dve", "filt", 0)
    add("dve", "filt", 1)
    for n in range(2):
        for tt in range(TT):
            for half in range(2):
                for d in range(2):
                    add("dve", "taps", n, tt, half, d)
        for m in range(4):
            for half in range(2):
                add("act", "spec_k", n, m, half)
        for half in range(2):
            for f in range(2):
                for im in range(2):
                    add("dve", "spec_u", n, half, f, im)
        for i in range(4):
            add("dve", "inv", n, i)
    add("act", "norm", "g_ffn")
    add("dve", "router")
    for tt in range(TT):
        for i in range(2):
            add("act", "h_tok", tt, i)
    add("dve", "affT")
    add("dve", "slot_tr")
    for i in range(8):
        add("act", "PT", i)
    for i in range(8):
        add("dve", "xe", i)
    for i in range(4):
        add("dve", "moe_acc", i)
    add("act", "norm", "g_final")
    for l in range(LAYERS):
        add("act", "norm", f"norm_ffn1{l}")
        for i in range(4):
            add("dve", "ffn1", l, i)
        add("act", "norm", f"norm_mix{l}")
        for i in range(3):
            add("act", "qk_norm", l, i)
        add("act", "av_tr", l, 0)
        add("act", "av_tr", l, 1)
        for h in range(6):
            for it in range(2):
                add("dve", "score", l, h, it)
        for h in range(6):
            add("act", "prob_tr", l, h)
        for q in range(HP):
            add("act", "att", l, q)
        add("act", "pool", l)
        for i in range(2):
            add("act", "kk_norm", l, i)
        for kind in range(3):
            for i in range(2):
                add("act", "lora", l, kind, i)
        if l:
            add("act", "vdown", l)
            for i in range(2):
                add("act", "vup", l, i)
        for tt in range(TT):
            for x in "abkv":
                add("dve" if x == "b" else "act", "rw_tr", l, tt, x)
            for x, r in (("A", "dve"), ("AT", "dve"), ("BT", "dve"), ("CT", "dve"), ("DT", "dve"),
                         ("P2", "act"), ("P2T", "act"), ("Q2", "dve"), ("P4", "act"), ("P4T", "act"), ("Q4", "dve"),
                         ("P8", "act"), ("Q8", "dve"), ("TR", "act"), ("X1", "act"), ("Q32", "dve"),
                         ("BV", "act"), ("WU", "act")):
                for p in range(2):
                    add(r, x, l, tt, p)
            for q in range(HP):
                add("dve", "M", l, tt, q)
                add("dve", "N", l, tt, q)
                add("dve", "RY", l, tt, q)
            for c in range(4):
                add("dve", "S", l, tt, c)
            for p in range(2):
                add("dve", "y", l, tt, p)
        for x, r in (("mean", "dve"), ("var", "act"), ("bonus", "dve")):
            for i in range(2):
                add(r, x, l, i)
        add("act", "norm", f"norm_mem{l}")
        add("act", "norm", f"norm_cross{l}")
        for i in range(2):
            add("act", "xnorm", l, "k", i)
        add("act", "xnorm", l, "q", 0)
        for h in range(4):
            for it in range(2):
                add("dve", "xscore", l, h, it)
        for h in range(4):
            add("act", "xprob_tr", l, h)
        for h in range(4):
            add("dve", "xatt", l, h)
        add("act", "norm", f"norm_ffn2{l}")
        for i in range(4):
            add("dve", "ffn2", l, i)
    return plan


def program(nc, A, out):
    ctx = ExitStack()
    with ctx:
        def sb(name, shape, dt=F32):
            return ctx.enter_context(nc.sbuf_tensor(name, shape, dt))

        def shared(name, words, parts):
            with nc.sbuf_tensor(name, [P, words], F32) as whole:
                pass
            return [whole] + [sb(n, shape, F32R) for n, shape in parts]

        sems = {}

        def S(name):
            if name not in sems:
                sems[name] = ctx.enter_context(nc.semaphore(name))
            return sems[name]

        PCOL, npc = param_columns()
        CCOL, ncc = constant_columns()
        par = sb("par", [P, npc])
        con = sb("con", [P, ncc])
        ring = [sb(f"ring{i}", [P, SLOT]) for i in range(RING)]
        x = sb("x", [P, KD, T])
        sq = sb("sq", [P, KD, T])
        rstd = sb("rstd", [P, T])
        tiny = sb("tiny", [P, 64])
        v_first = sb("v_first", [P, HP, T])
        (e_hi0, hi0), (e_hi1, hi1), (e_lo0, lo0), (e_lo1, lo1) = (
            shared(f"e_{n}", SLOT, [(n, [P, SLOT])]) for n in ("w_hi0", "w_hi1", "w_lo0", "w_lo1"))
        w_hi, w_lo = (hi0, hi1), (lo0, lo1)
        hx, h_hi, h_lo = shared("hx", 2 * KD * T, [("h_hi", [P, KD, T]), ("h_lo", [P, KD, T])])
        h = sq
        SCR = 96 * 256
        scr, halves = shared("scr", SCR, [("halves", [P, 2 * KD * T])])
        ctx.enter_context(nc.sbuf_tensor("scr_rest", [P, SCR - 2 * KD * T], F32))
        psd = [ctx.enter_context(nc.psum_tensor(f"psd{i}", [P, 512], F32)) for i in range(4)]
        psx = [ctx.enter_context(nc.psum_tensor(f"psx{i}", [P, 512], F32)) for i in range(4)]

        def at(kib, *shape, parts=P):
            n = math.prod(shape)
            v = scr[0:parts, int(kib * 256):int(kib * 256) + n]
            assert kib * 256 + n <= SCR
            names = " ".join("abcd"[:len(shape)])
            return v if len(shape) == 1 else v.rearrange(
                f"p ({names}) -> p {names}", **{k: s for k, s in zip("abcd", shape)})

        def pc(name, i=0, lo=0, hi=P):
            return par[lo:hi, PCOL[name] + i:PCOL[name] + i + 1]

        def cst(name, n):
            return con[:, CCOL[name]:CCOL[name] + n]

        ident, ones, bones = cst("ident", P), cst("ones", P), cst("bones", P)
        eps_col = con[:, CCOL["eps"]:CCOL["eps"] + 1]
        gneps_col = con[:, CCOL["gneps"]:CCOL["gneps"] + 1]

        plan, MOE, after = stream_plan()
        AFTER = MOE + EXPERTS * ESLOTS
        SN = {(k, i): n for n, (k, i, _, _) in enumerate(plan)}
        SN.update({(k, i): AFTER + n for n, (k, i, _, _) in enumerate(after)})
        dense_slots = [n for n in range(AFTER + len(after)) if not MOE <= n < AFTER]
        dense_at = {n: j for j, n in enumerate(dense_slots)}
        hi_cut, lo_cut = S("w_hi_cut"), S("w_lo_cut")
        land = [S(f"landed{i}") for i in range(RING)]
        e_ring = [r[:, :] for r in ring] + [r[:, :] for r in (e_hi0, e_lo0, e_hi1, e_lo1)] + [
            hx[:, i * SLOT:(i + 1) * SLOT] for i in range(2)] + [at(80 + 8 * i, SLOT) for i in range(2)]
        assert len(e_ring) == ERING and ESLOTS % ERING == 0 and MOE % RING == 0
        e_land = [S(f"expert_landed{i}") for i in range(ERING)]
        slots_done = S("slots_done")
        x_done = S("small_done")
        d_read = {"act": S("dense_read_act"), "dve": S("dense_read_dve")}
        x_read = {"act": S("small_read_act"), "dve": S("small_read_dve")}
        DB = Banks(dense_plan(), psd, d_read)
        XB = Banks(small_plan(), psx, x_read)

        def slot_of(key):
            return SN[key if key in SN else (key, key[3])]

        def d_ready(eng, key):
            eng.wait_ge(slots_done, slot_of(key) + 1)
            return DB.bank(key)

        def x_ready(eng, *key):
            eng.wait_ge(x_done, XB.at[key] + 1)
            return XB.bank(key)

        half_slot = {SN[(("mix_in", l), 10)] for l in range(LAYERS)}

        class Cutter:

            def __init__(self, eng, cut):
                self.eng, self.cut, self.next = eng, cut, 0

            def upto(self, n):
                while self.next < len(dense_slots) and dense_slots[self.next] <= n:
                    j = self.next
                    if j >= 2 and dense_slots[j] >= AFTER > dense_slots[j - 2]:
                        self.eng.wait_ge(slots_done, AFTER - ERING + 8)
                    elif j >= 2:
                        self.eng.wait_ge(slots_done, dense_slots[j - 2] + 1)
                    self.cut(j, dense_slots[j])
                    self.next += 1

        def cut_ahead(cutter, key):
            n = slot_of(key)
            last = max(s for s in dense_slots if (s < MOE) == (n < MOE))
            cutter.upto(min(dense_slots[min(dense_at[n] + 2, len(dense_slots) - 1)], last))

        def prime(cutter, key):
            cutter.upto(dense_slots[dense_at[slot_of(key)] + 1])

        def m2(bank):
            return bank[:, :].rearrange("p (m t) -> p m t", m=2)

        def tri(bank, n=P):
            return bank[:, 0:HP * n].rearrange("p (q n) -> p q n", q=HP)

        NORMS = ["g_mix", "g_ffn", "g_final"]
        for l in range(LAYERS):
            NORMS += [f"norm_ffn1{l}", f"norm_mix{l}", f"norm_mem{l}", f"norm_cross{l}", f"norm_ffn2{l}"]
        sq_ready, h_ready = S("sq_ready"), S("h_ready")

        def x_made(eng, part, l, i):
            if part == "g_final":
                eng.wait_ge(h_ready, 4 * NORMS.index(part) + i + 1)
            elif part in ("moe_acc", "ffn1", "ffn2"):
                XB.was_read(eng, (part, i) if l is None else (part, l, i))
            else:
                DB.was_read(eng, (part if l is None else (part, l), i))

        def hx_at(kib, *shape):
            n = math.prod(shape)
            names = " ".join("abcd"[:len(shape)])
            return hx[:, int(kib * 256):int(kib * 256) + n].rearrange(
                f"p ({names}) -> p {names}", **{k: s for k, s in zip("abcd", shape)})

        xa, ga, gs = at(0, 8, T), at(8, 8, T), at(16, 16, T)
        v_tok, x1_tok, x2 = at(32, TT, D), at(40, TT, D), at(48, 8, T)
        bd, lr, li, le, lh = at(56, 4, 8, P), at(72, 8, T), at(80, 8, T), at(88, 8, T), sq
        w3h, decay, taps_s, taps_d = at(56, 2, 2, 512, parts=64), at(64, TT, D), hx_at(0, TT, D), hx_at(8, TT, D)
        spec_k, spec_y = at(72, 4, D), hx_at(0, 4, D)
        fwd, inv = at(0, TT, 2 * T), at(4, 4, T)
        filt_w, zT = rstd, at(72, T, parts=33)
        gated = at(88, 8, T)

        h_tok, onehot, weighted = at(0, TT, D), at(8, TT, EXPERTS, CAP), at(12, TT, EXPERTS, P)
        PT, xe = at(28, EXPERTS, T), at(44, KD, EXPERTS * CAP)
        wr = at(60, KD, EXPERTS)
        xs, sg_e, act_e = at(61, KD, CAP), at(62, 512), at(64, 512)
        actT, ye = at(66, 4, P), at(68, 2, 512)
        aff, lg, affT, wk, msk, slotT, slots = (at(72, TT, 16), at(72.25, TT, 16), at(73, T, parts=16),
                                                at(74, T, parts=16), at(75, T, parts=16), at(76, T, parts=16),
                                                at(77, TT, 16))
        top8 = at(78, 8, parts=16)
        ones16 = at(79, T, parts=16)

        sg, fa = at(0, 2, 2, T), at(4, 2, 2, T)
        fa_hi, fa_lo = (halves[:, i * 1024:(i + 1) * 1024].rearrange("p (f i t) -> p f i t", f=2, i=2) for i in (2, 3))
        ycat, pb, ts = at(0, 8, T), at(8, NPB, T), at(29, 10, T)
        al, rt, be, kt = at(39, HP, T), at(42, HP, T), at(45, HP, T), at(48, HP, T)
        rs3 = al
        rq = tiny[:, 52:64]
        v_tm, ab, bm, km = hx_at(8, TT, AW), hx_at(11, 6, P), at(51, HP, 4, P), at(57, HP, 4, P)
        MATS = {n: [at(63 + 1.5 * (2 * i + p), HP, P) for p in range(2)] for i, n in enumerate(
            ("A", "AT", "Aoff", "BT", "CT", "DT", "Q", "P2", "P2T", "P4", "P4T"))}
        e1, e2, e3, kk, aa, gg, yy = (pb[:, 0:3, :], pb[:, 3:6, :], pb[:, 6:9, :], pb[:, 9:12, :],
                                      pb[:, 12:15, :], pb[:, 15:18, :], pb[:, 18:21, :])
        MT, y0T, RT = hx_at(0, 4, HP, P), hx_at(6, HP, P), hx_at(14, HP, P)
        sqf = sq[:, :, :].rearrange("p a t -> p (a t)")
        Np = sqf[:, 0:768].rearrange("p (c q n) -> p c q n", c=4, q=HP)
        Xs = sqf[:, 768:768 + 960].rearrange("p (c q n) -> p c q n", c=5, q=HP)
        lora_up = at(91, AW)
        lo = ts[:, 9, :]
        rbias, prob = at(63, 6, 384), at(72, 6, 384)
        probT = at(81, 6, 3, P)
        up, wa, wb = at(45, 2, 16 + T), at(48, 2, 16 + T), at(51, 2, 16 + T)
        poolw = at(90, 2, P)
        mn_hi, mn_lo = (halves[:, i * 2048:(i + 1) * 2048].rearrange("p (k t) -> p k t", k=KD) for i in (0, 1))
        xk, xv, xq = at(16, 8, T), at(24, TT, D), at(32, 8, T)
        xprob, xpT, xo = at(40, 8, T), at(48, 4, 2, T), at(56, 8, T)
        vdn, vup, vtmp = at(92.5, HP, 32), at(93, AW, parts=32), at(94.5, T, parts=32)
        memT, sqk, sqq = at(64, 8, T), at(56, 8, T), at(72, 8, T)
        rs4 = memT[:, 0:4, :]
        late_sq = at(16, 8, T)
        squares_of = {g: late_sq for g in NORMS if g.startswith(("norm_ffn", "norm_mix"))}
        by_token = rstd[:, :].unsqueeze(1).broadcast_to([P, 2, T])

        block = ctx.enter_context(nc.Block())

        @block.tensor
        def _(pe):
            act_halves = (h_hi, h_lo)

            def done(ins):
                ins.then_inc(x_done, 1)

            def cut(n, **kw):
                j = dense_at[n]
                pe.wait_ge(lo_cut, 2 * j + 1)
                name = list(kw)[0]
                return [w[j % 2][:, :].rearrange(f"p ({name} c) -> p {name} c", **kw) for w in (w_hi, w_lo)]

            def rest_cut(n):
                pe.wait_ge(lo_cut, 2 * dense_at[n] + 2)

            def three(o, w, a, start, stop, **kw):
                for i, (u, v) in enumerate(((0, 0), (0, 1), (1, 0))):
                    mm = pe.matmul(o, w[u], a[v], start=start and i == 0, stop=stop and i == 2, **kw)
                return mm

            def norm(g, first=0, last=4):
                q = NORMS.index(g)
                b = XB.bank(("norm", g)) if first else XB.claim(pe, ("norm", g))
                for k in range(2 * first, 2 * last):
                    if k % 2 == 0:
                        pe.wait_ge(sq_ready, 4 * q + k // 2 + 1)
                    mm = pe.matmul(b[:, 0:T], ones, squares_of.get(g, sq)[:, k, :], start=(k == 0), stop=(k == KD - 1),
                                   skip_group_check=True)
                if last == 4:
                    done(mm)

            def then_norm(key, g, ready, rhs=act_halves, last=4):
                for i in range(4):
                    dense((key, i), rhs, ready=None if i else ready)
                    if i > 1:
                        norm(g, i - 2, i - 1)
                if last == 4:
                    norm(g, 2)

            def dense(key, rhs=act_halves, g=None, ready=None, tiles=2):
                b = m2(DB.claim(pe, key))
                w = cut(slot_of(key), k=KD)
                for m in range(tiles):
                    for k in range(KD):
                        if g is not None and m == 0 and k % 2 == 0:
                            pe.wait_ge(h_ready, 4 * NORMS.index(g) + k // 2 + 1)
                        if ready and m == 0 and k % 2 == 0:
                            pe.wait_ge(S(ready[0]), ready[1] + k // 2 + 1)
                        if m == 0 and k == KD // 2:
                            rest_cut(slot_of(key))
                        c = slice(m * P, (m + 1) * P)
                        mm = three(b[:, m, :], [v[:, k, c] for v in w], [v[:, k, :] for v in rhs],
                                   k == 0, k == KD - 1)
                mm.then_inc(slots_done, 1)

            def ffn(which, l, g):
                for f in range(FSTEPS + 1):
                    if f < FSTEPS:
                        dense((which, l, "gate", f), g=f"norm_{which}{l}" if f == 0 else None)
                        if f == 0:
                            norm(f"norm_{which}{l}", 2)
                        dense((which, l, "up", f))
                    e = f - 1
                    if f:
                        if e == 0:
                            acc = [m2(XB.claim(pe, (which, l, i))) for i in range(4)]
                        n = SN[((which, l, "down", e), e)]
                        w = cut(n, i=2)
                        pe.wait_ge(S("fa_cut"), (2 * l + (which == "ffn2")) * FSTEPS + e + 1)

                        def down(i, dt):
                            c = slice(dt * P, (dt + 1) * P)
                            return three(acc[dt // 2][:, dt % 2, :], [v[:, i, c] for v in w],
                                         [v[:, e % 2, i, :] for v in (fa_hi, fa_lo)],
                                         e == 0 and i == 0 and dt % 2 == 0, e == FSTEPS - 1 and i == 1,
                                         skip_group_check=True)
                        if e < FSTEPS - 1:
                            for i in range(2):
                                if i:
                                    rest_cut(n)
                                for dt in range(KD):
                                    mm = down(i, dt)
                            mm.then_inc(slots_done, 1)
                        else:
                            rest_cut(n)
                            for dt in range(KD):
                                for i in range(2):
                                    mm = down(i, dt)
                                if dt % 2:
                                    done(mm)
                                if g and dt in (3, 5):
                                    norm(g, dt // 2 - 1, dt // 2)
                            pe.drain().then_inc(slots_done, 1)

            pe.wait_ge(S("par_in"), 16)
            pe.wait_ge(S("con_in"), 16)
            norm("g_mix")
            for i in range(4):
                dense(("a_x", i), g="g_mix" if i == 0 else None)

            def conv_turn(part, i):
                DB.was_read(pe, ("hy_" + part, i))
                b = XB.claim(pe, ("hy_tr", part, i))
                for tt in range(TT):
                    for m in range(2):
                        mm = pe.transpose(b[:, (2 * tt + m) * P:(2 * tt + m + 1) * P],
                                          sq[:, 2 * (i % 2) + m, tt * P:(tt + 1) * P], ident)
                done(mm)

            turns = [(part, i) for part in ("v", "x1") for i in range(4)]
            for n, (part, i) in enumerate(turns):
                dense(("hy_" + part, i))
                if n:
                    conv_turn(*turns[n - 1])
            dense(("hy_x2", 0))
            conv_turn(*turns[-1])
            for i in range(1, 4):
                dense(("hy_x2", i))

            def lru_gates(d):
                for kind in range(2):
                    for i in range(4):
                        b = m2(XB.claim(pe, ("lru", d, kind, i)))
                        for m in range(2):
                            mm = pe.matmul(b[:, m, :], bd[:, 2 * d + kind, 2 * i + m, :], xa[:, 2 * i + m, :],
                                           start=True, stop=True)
                        done(mm)

            pe.wait_ge(S("bd_in"), 16)
            DB.was_read(pe, ("a_x", 3))
            lru_gates(0)
            for i in range(4):
                dense(("a_gate", i))
            for i in range(2):
                dense(("gates", i))
            lru_gates(1)
            for i in range(2, 8):
                dense(("gates", i))
            dense(("w_a_out", 0), ready=("lru_out", 0))

            b = XB.claim(pe, ("filt", 0))
            pe.wait_ge(S("filt_in"), 64)
            done(pe.matmul(b[0:64, 0:T], filt_w[0:33, 0:64], zT, start=True, stop=True))
            dense(("w_a_out", 1))
            dense(("w_a_out", 2))
            pe.wait_ge(S("filt_sin"), 1)
            b = XB.claim(pe, ("filt", 1))
            done(pe.matmul(b[0:64, 0:T], filt_w[0:64, 64:128], sq[0:64, 1, :], start=True, stop=True))
            dense(("w_a_out", 3))
            pe.wait_ge(S("filt_sin"), 2)
            pe.wait_ge(S("dft_in"), 16)
            for n in range(2):
                pe.wait_ge(S(f"w3_in{n}"), 16)
                for tt in range(TT):
                    for half in range(2):
                        for d in range(2):
                            b = XB.claim(pe, ("taps", n, tt, half, d))
                            done(pe.matmul(b[:, :], sq[0:64, 2, tt * P:(tt + 1) * P], w3h[:, d, half, :],
                                           start=True, stop=True))
                pe.wait_ge(S("taps_ready"), n + 1)
                for m in range(4):
                    src = taps_s if m < 2 else taps_d
                    for half in range(2):
                        b = XB.claim(pe, ("spec_k", n, m, half))
                        for tt in range(TT):
                            mm = pe.matmul(b[:, :], fwd[:, tt, m * P:(m + 1) * P],
                                           src[:, tt, half * 512:(half + 1) * 512], start=(tt == 0), stop=(tt == 1))
                        done(mm)
                if n:
                    pe.wait_ge(S("z_tok"), 4)
                for half in range(2):
                    for f in range(2):
                        for im in range(2):
                            b = XB.claim(pe, ("spec_u", n, half, f, im))
                            m = 2 * im + f
                            for tt in range(TT):
                                mm = pe.matmul(b[:, :], fwd[:, tt, m * P:(m + 1) * P],
                                               v_tok[:, tt, half * 512:(half + 1) * 512],
                                               start=(tt == 0), stop=(tt == 1))
                            done(mm)
                pe.wait_ge(S("spec_y"), 4 * (n + 1))
                for i in range(4):
                    b = XB.claim(pe, ("inv", n, i))
                    if n == 0:
                        tt, half = i // 2, i % 2
                        for m in range(4):
                            mm = pe.matmul(b[:, :], inv[:, m, tt * P:(tt + 1) * P],
                                           spec_y[:, m, half * 512:(half + 1) * 512], start=(m == 0), stop=(m == 3))
                    else:
                        for c in range(2):
                            for m in range(4):
                                mm = pe.matmul(m2(b)[:, c, :], spec_y[:, m, (2 * i + c) * P:(2 * i + c + 1) * P],
                                               inv[:, m, :], start=(m == 0), stop=(m == 3))
                    done(mm)
            pe.wait_ge(S("z_cut"), 1)
            for i in range(4):
                dense(("w_b_out", i))
            then_norm("w_o", "g_ffn", ("merged", 0), (mn_hi, mn_lo))

            b = XB.claim(pe, ("router",))
            pe.wait_ge(S("wr_in"), 16)
            for tt in range(TT):
                for k in range(KD):
                    if tt == 0 and k % 2 == 0:
                        pe.wait_ge(h_ready, 4 * NORMS.index("g_ffn") + k // 2 + 1)
                    mm = pe.matmul(b[:, tt * 16:tt * 16 + 16], h[:, k, tt * P:(tt + 1) * P], wr[:, k, :],
                                   start=(k == 0), stop=(k == KD - 1))
            done(mm)
            for tt in range(TT):
                for i in range(2):
                    b = XB.claim(pe, ("h_tok", tt, i))
                    for c in range(4):
                        mm = pe.transpose(b[:, c * P:(c + 1) * P], h[:, 4 * i + c, tt * P:(tt + 1) * P], ident)
                    done(mm)
            b = XB.claim(pe, ("affT",))
            pe.wait_ge(S("aff"), 1)
            for tt in range(TT):
                mm = pe.transpose(b[0:16, tt * P:(tt + 1) * P], aff[:, tt, :], ident)
            done(mm)
            b = XB.claim(pe, ("slot_tr",))
            pe.wait_ge(S("slotT"), 1)
            for tt in range(TT):
                mm = pe.transpose(b[:, tt * 16:tt * 16 + 16], slotT[:, tt * P:(tt + 1) * P], ident[0:16, 0:16])
            done(mm)
            pe.wait_ge(S("weighted"), 1)
            for i in range(8):
                b = XB.claim(pe, ("PT", i))
                for c in range(2):
                    for tt in range(TT):
                        mm = pe.transpose(b[:, (2 * c + tt) * P:(2 * c + tt + 1) * P], weighted[:, tt, 2 * i + c, :],
                                          ident)
                done(mm)
            XB.was_read(pe, ("h_tok", 1, 1))
            for i in range(8):
                b = XB.claim(pe, ("xe", i))
                for tt in range(TT):
                    mm = pe.matmul(b[:, :], h_tok[:, tt, i * P:(i + 1) * P],
                                   onehot[:, tt, :, :].rearrange("p e c -> p (e c)"), start=(tt == 0), stop=(tt == 1))
                done(mm)
            acc = [m2(XB.claim(pe, ("moe_acc", i))) for i in range(4)]
            for k in range(KD):
                pe.matmul(acc[k // 2][:, k % 2, :], ident, x[:, k, :], start=(k % 2 == 0), stop=False,
                          skip_group_check=True)
            XB.was_read(pe, ("xe", 7))
            XB.was_read(pe, ("PT", 7))

            for i in range(4):
                DB.claim(pe, ("moe", i))
            turn = psd[0][:, :].rearrange("p (b n) -> p b n", b=4)

            def landed(e, s):
                pe.wait_ge(e_land[s % ERING], e * (16 * ESLOTS // ERING) + 16 * (s // ERING + 1))

            def down_rows(s):
                return e_ring[s % ERING].rearrange("p (i c) -> p i c", i=2)

            with pe.Fori(0, EXPERTS) as e:
                pe.wait_ge(S("xs_ready"), e + 1)
                for s in range(16):
                    landed(e, s)
                    for j in range(4):
                        mm = pe.matmul(psd[s // 8][32 * j:32 * j + 32, :], xs[:, s % 8, :],
                                       e_ring[s % ERING][:, j * 512:(j + 1) * 512], start=(s % 8 == 0), stop=(s % 8 == 7),
                                       skip_group_check=True)
                    mm.then_inc(slots_done, 1)
                pe.wait_ge(S("act_e"), e + 1)
                for b4 in range(4):
                    mm = pe.transpose(turn[:, b4, :], act_e[:, b4 * P:(b4 + 1) * P], ident)
                mm.then_inc(S("turned"), 1)
                pe.wait_ge(S("actT"), e + 1)
                for s in range(0, 8, 2):
                    for q in (s, s + 1):
                        landed(e, 16 + q)
                    for half in range(2):
                        for j in range(4):
                            n, kt_ = 16 + s + j // 2, 2 * s + j
                            mm = pe.matmul(psd[2 + half][32 * j:32 * j + 32, :],
                                           actT[:, kt_ % 4, 32 * (kt_ // 4):32 * (kt_ // 4) + 32],
                                           down_rows(n)[:, j % 2, half * 512:(half + 1) * 512], start=(s == 0), stop=(s == 6),
                                           skip_group_check=True)
                            if half == 1 and j >= 2:
                                mm.then_inc(slots_done, 1)
                pe.wait_ge(S("ye_ready"), 2 * e + 2)
                for k in range(KD):
                    pe.matmul(acc[k // 2][:, k % 2, :], ye[:, k // 4, (k % 4) * P:(k % 4 + 1) * P],
                                   PT[:, bass.ds(e, 1), :].rearrange("p a t -> p (a t)"), start=False, stop=False,
                                   skip_group_check=True)
            pe.drain().then_inc(x_done, 4)
            norm("g_final")

            for l in range(LAYERS):
                if l == 0:
                    norm(f"norm_ffn1{l}", 0, 2)
                ffn("ffn1", l, f"norm_mix{l}")
                for i in range(9):
                    dense((("mix_in", l), i), g=f"norm_mix{l}" if i == 0 else None)
                    if i == 0:
                        norm(f"norm_mix{l}", 2)
                pe.wait_ge(S("qk_sq"), 3 * l + 3)
                b = XB.claim(pe, ("qk_norm", l, 0))
                for q in range(HP):
                    for it in range(TT):
                        mm = pe.matmul(b[:, 4 * q + it:4 * q + it + 3:2], sq[:, q, it * P:(it + 1) * P],
                                       bones[:, 0:P:64], start=True, stop=True)
                done(mm)
                for i in range(2):
                    b = m2(XB.claim(pe, ("qk_norm", l, 1 + i)))
                    for m in range(2 - i):
                        mm = pe.matmul(b[:, m, :], bones, sq[:, HP + 2 * i + m, :], start=True, stop=True)
                    done(mm)
                dense((("mix_in", l), 9))
                key = (("mix_in", l), 10)
                b, j = m2(DB.claim(pe, key)), dense_at[slot_of(key)]
                pe.wait_ge(lo_cut, 2 * j + 2)
                for k in range(KD):
                    c = slice(k * P, (k + 1) * P)
                    mm = three(b[:, 0, :], [w_hi[j % 2][:, c], w_lo[j % 2][:, c]],
                               [v[:, k, :] for v in act_halves], k == 0, k == KD - 1)
                mm.then_inc(slots_done, 1)

                DB.was_read(pe, key)
                for tt in range(TT):
                    b = XB.claim(pe, ("av_tr", l, tt))
                    for q in range(HP):
                        mm = pe.transpose(tri(b)[:, q, :], pb[:, 16 + q, tt * P:(tt + 1) * P], ident)
                    done(mm)
                pe.wait_ge(S("qk_ready"), l + 1)
                for hd in range(6):
                    r = 64 * (hd % 2)
                    for it in range(2):
                        b = XB.claim(pe, ("score", l, hd, it))
                        done(pe.matmul(b[:, 0:P * (it + 1)], pb[r:r + 64, 10 + hd // 2, it * P:(it + 1) * P],
                                       pb[r:r + 64, 13 + hd // 2, 0:P * (it + 1)], start=True, stop=True))
                for hd in range(6):
                    pe.wait_ge(S("prob"), 6 * l + hd + 1)
                    b = XB.claim(pe, ("prob_tr", l, hd))
                    for j in range(3):
                        mm = pe.transpose(tri(b)[:, j, :], prob[:, hd, j * P:(j + 1) * P], ident)
                    done(mm)
                for q in range(HP):
                    b = XB.claim(pe, ("att", l, q))
                    XB.was_read(pe, ("prob_tr", l, 2 * q + 1))
                    for p in range(2):
                        hd = 2 * q + p
                        o = b[64 * p:64 * p + 64, :]
                        v = [v_tm[:, tt, hd * 64:hd * 64 + 64] for tt in range(TT)]
                        pe.matmul(o[:, 0:P], v[0], probT[:, hd, 0, :], start=True, stop=True)
                        pe.matmul(o[:, P:T], v[0], probT[:, hd, 1, :], start=True, stop=False)
                        mm = pe.matmul(o[:, P:T], v[1], probT[:, hd, 2, :], start=False, stop=True)
                    done(mm)
                b = m2(XB.claim(pe, ("pool", l)))
                pe.wait_ge(S("pooled"), l + 1)
                pe.wait_ge(S(f"att_in{l}"), 32)
                for m in range(2):
                    mm = pe.matmul(b[:, m, :], poolw[:, m, :], up[:, m, 16:16 + T], start=True, stop=True)
                done(mm)

                pe.wait_ge(S("kk_sq"), l + 1)
                for i in range(2):
                    b = m2(XB.claim(pe, ("kk_norm", l, i)))
                    for m in range(2 if i == 0 else 1):
                        mm = pe.matmul(b[:, m, :], bones, sq[:, 2 * i + m, :], start=True, stop=True)
                    done(mm)
                pe.wait_ge(S(f"lora_in{l}"), 16 * (3 if l else 1))
                for kind, (r, n) in enumerate(((0, 32), (32, 32), (64, 64))):
                    pe.wait_ge(S("lora_act"), 2 * l + 1 + (kind == 2))
                    for i in range(2):
                        b = m2(XB.claim(pe, ("lora", l, kind, i)))
                        for m in range(2 if i == 0 else 1):
                            c = (2 * i + m) * P
                            mm = pe.matmul(b[:, m, :], lora_up[r:r + n, c:c + P], lo[r:r + n, :], start=True, stop=True)
                        done(mm)
                if l:
                    b = XB.claim(pe, ("vdown", l))
                    for q in range(HP):
                        mm = pe.matmul(b[0:32, 0:T], vdn[:, q, :], ts[:, 6 + q, :], start=(q == 0), stop=(q == 2))
                    done(mm)
                    XB.was_read(pe, ("vdown", l))
                    for i in range(2):
                        b = m2(XB.claim(pe, ("vup", l, i)))
                        for m in range(2 if i == 0 else 1):
                            c = (2 * i + m) * P
                            mm = pe.matmul(b[:, m, :], vup[:, c:c + P], vtmp, start=True, stop=True)
                        done(mm)
                for tt in range(TT):
                    tok = slice(tt * P, (tt + 1) * P)
                    for xk_, src in (("a", al), ("b", be), ("k", kt), ("v", ts[:, 6:9, :])):
                        if tt == 0:
                            if xk_ == "v":
                                pe.wait_ge(S("v_made"), l + 1)
                            else:
                                pe.wait_ge(S("rw_scaled"), 4 * l + "abk".index(xk_) + 1)
                        b = XB.claim(pe, ("rw_tr", l, tt, xk_))
                        for q in range(HP):
                            mm = pe.transpose(tri(b)[:, q, :], src[:, q, tok], ident)
                        done(mm)

                    def mats(name, body, n=P, wait=()):
                        for p in range(2):
                            for w in wait:
                                w(p)
                            b = XB.claim(pe, (name, l, tt, p))
                            for q in range(HP):
                                mm = body(tri(b, n)[:, q, :], p, q)
                            done(mm)

                    def pair(lhs, rhs):
                        def body(o, p, q):
                            r = slice(64 * p, 64 * p + 64)
                            return pe.matmul(o, lhs[r, q, tok], rhs[r, q, tok], start=True, stop=True)
                        return body

                    def prod(lhs, rhs):
                        def body(o, p, q):
                            return pe.matmul(o, MATS[lhs][p][:, q, :], MATS[rhs][p][:, q, :], start=True, stop=True)
                        return body

                    def after(*names):
                        return [lambda p, x=x_: XB.was_read(pe, (x, l, tt, p)) for x_ in names]

                    mats("A", pair(al, be))
                    mats("AT", pair(be, al))
                    mats("BT", pair(kt, al))
                    pe.wait_ge(S("rw_scaled"), 4 * l + 4)
                    mats("CT", pair(be, rt))
                    mats("DT", pair(kt, rt))
                    mats("P2", prod("AT", "A"), wait=after("A", "AT"))
                    mats("P2T", prod("A", "AT"))
                    mats("Q2", prod("P2", "Q"), wait=after("P2"))
                    mats("P4", prod("P2T", "P2"), wait=after("P2T"))
                    mats("P4T", prod("P2", "P2T"))
                    mats("Q4", prod("P4", "Q"), wait=after("P4", "Q2"))
                    mats("P8", prod("P4T", "P4"), wait=after("P4T"))
                    mats("Q8", prod("P2", "Q"), wait=after("P8", "Q4"))
                    mats("TR", lambda o, p, q: pe.transpose(o, MATS["Q"][p][:, q, :], ident), wait=after("Q8"))
                    mats("X1", prod("Aoff", "Q"))
                    mats("Q32", prod("P2T", "P4"), wait=after("TR", "X1"))
                    XB.was_read(pe, ("rw_tr", l, tt, "v"))
                    mats("BV", lambda o, p, q: pe.matmul(
                        o, MATS["BT"][p][:, q, :], v_tm[:, tt, (2 * q + p) * 64:(2 * q + p) * 64 + 64],
                        start=True, stop=True), n=64)
                    mats("WU", lambda o, p, q: pe.matmul(o, MATS["Q"][p][:, q, :], ab[:, 2 * q + p, :],
                                                         start=True, stop=True), wait=after("Q32", "BV"))
                    for w in after("WU"):
                        w(0)
                        w(1)
                    XB.was_read(pe, ("rw_tr", l, tt, "b"))
                    XB.was_read(pe, ("rw_tr", l, tt, "k"))
                    for q in range(HP):
                        wu = [MATS["P4T"][p][:, q, :] for p in range(2)]
                        rows = [slice(64 * p, 64 * p + 64) for p in range(2)]
                        b = XB.claim(pe, ("M", l, tt, q))
                        for p in range(2):
                            mm = pe.matmul(b[rows[p], 0:T], wu[p][:, 0:64], bm[:, q, :, rows[p]],
                                           start=True, stop=True)
                        done(mm)
                        b = XB.claim(pe, ("N", l, tt, q))
                        for p in range(2):
                            hd = 2 * q + p
                            for c in range(4):
                                o = b[rows[p], c * 64:c * 64 + 64]
                                pe.matmul(o, bm[:, q, c, rows[p]], wu[p][:, 64:128], start=True, stop=False)
                                mm = pe.matmul(o, km[:, q, c, rows[p]], v_tm[:, tt, hd * 64:hd * 64 + 64],
                                               start=False, stop=True)
                        done(mm)
                        b = XB.claim(pe, ("RY", l, tt, q))
                        for p in range(2):
                            hd = 2 * q + p
                            pe.matmul(b[rows[p], 0:P], wu[p][:, 0:64], MATS["CT"][p][:, q, :], start=True, stop=True)
                            pe.matmul(b[rows[p], P:T], wu[p][:, 64:128], MATS["CT"][p][:, q, :],
                                      start=True, stop=False)
                            mm = pe.matmul(b[rows[p], P:T], v_tm[:, tt, hd * 64:hd * 64 + 64],
                                           MATS["DT"][p][:, q, :], start=False, stop=True)
                        done(mm)
                    for c in range(4):
                        if c == 0:
                            pe.wait_ge(S("state0"), 2 * l + tt + 1)
                            XB.was_read(pe, ("RY", l, tt, HP - 1))
                        else:
                            XB.was_read(pe, ("S", l, tt, c - 1))
                        b = XB.claim(pe, ("S", l, tt, c))
                        for q in range(HP):
                            mm = pe.matmul(tri(b, 64)[:, q, :], MT[:, c, q, :], Xs[:, c, q, :], start=True, stop=True)
                        done(mm)
                    for p in range(2):
                        b = XB.claim(pe, ("y", l, tt, p))
                        r = slice(64 * p, 64 * p + 64)
                        for q in range(HP):
                            for c in range(4):
                                mm = pe.matmul(tri(b)[r, q, c * CH:(c + 1) * CH], Xs[r, c, q, :],
                                               RT[r, q, c * CH:(c + 1) * CH], start=True, stop=True)
                        done(mm)
                for name, src, flag in (("mean", yy, "y_ready"), ("var", sq[:, 0:3, :], "yc_sq"),
                                        ("bonus", e1, "rk_ready")):
                    pe.wait_ge(S(flag), l + 1)
                    for i in range(2):
                        b = m2(XB.claim(pe, (name, l, i)))
                        for m in range(2 if i == 0 else 1):
                            mm = pe.matmul(b[:, m, :], bones, src[:, 2 * i + m, :], start=True, stop=True)
                        done(mm)
                norm(f"norm_mem{l}")
                pe.wait_ge(S("mix_cat"), l + 1)
                for i in range(4):
                    dense((("mix_out", l), i))

                for i in range(4):
                    dense((("x_k", l), i), (mn_hi, mn_lo), f"norm_mem{l}" if i == 0 else None)
                    if i == 1:
                        norm(f"norm_cross{l}")
                for i in range(4):
                    if i == 1:
                        for n in range(2):
                            b = m2(XB.claim(pe, ("xnorm", l, "k", n)))
                            pe.wait_ge(S("x_sq"), 8 * l + 2 * n + 2)
                            for m in range(2):
                                for c in range(2):
                                    mm = pe.matmul(b[:, m, :], ones, sqk[:, 4 * n + 2 * m + c, :],
                                                   start=(c == 0), stop=(c == 1))
                            done(mm)
                    key = (("x_v", l), i)
                    b = m2(DB.claim(pe, key))
                    w = cut(slot_of(key), k=KD)
                    for tt in range(TT):
                        for k in range(KD):
                            if tt == 0 and k == KD // 2:
                                rest_cut(slot_of(key))
                            mm = three(b[:, tt, :], [v[:, k, tt * P:(tt + 1) * P] for v in (mn_hi, mn_lo)],
                                       [v[:, k, :] for v in w], k == 0, k == KD - 1)
                    mm.then_inc(slots_done, 1)
                for i in range(4):
                    dense((("x_q", l), i), g=f"norm_cross{l}" if i == 0 else None)
                b = XB.claim(pe, ("xnorm", l, "q", 0))
                for hd in range(4):
                    pe.wait_ge(S("x_sq"), 8 * l + 4 + hd + 1)
                    for it in range(TT):
                        j = 2 * hd + it
                        for c in range(2):
                            mm = pe.matmul(b[:, j:j + 1], sqq[:, 2 * hd + c, it * P:(it + 1) * P], ones[:, 0:1],
                                           start=(c == 0), stop=(c == 1))
                done(mm)
                pe.wait_ge(S("xk_ready"), l + 1)
                DB.was_read(pe, (("x_q", l), 3))
                for hd in range(4):
                    for it in range(TT):
                        b = XB.claim(pe, ("xscore", l, hd, it))
                        for c in range(2):
                            mm = pe.matmul(b[:, 0:T], xq[:, 2 * hd + c, it * P:(it + 1) * P], xk[:, 2 * hd + c, :],
                                           start=(c == 0), stop=(c == 1))
                        done(mm)
                for hd in range(4):
                    pe.wait_ge(S("xprob"), 4 * l + hd + 1)
                    b = XB.claim(pe, ("xprob_tr", l, hd))
                    for mt in range(2):
                        for it in range(TT):
                            mm = pe.transpose(m2(b)[:, mt, it * P:(it + 1) * P],
                                              xprob[:, 2 * hd + it, mt * P:(mt + 1) * P], ident)
                    done(mm)
                for hd in range(4):
                    b = m2(XB.claim(pe, ("xatt", l, hd)))
                    XB.was_read(pe, ("xprob_tr", l, hd))
                    for c in range(2):
                        for mt in range(2):
                            mm = pe.matmul(b[:, c, :], xv[:, mt, (2 * hd + c) * P:(2 * hd + c + 1) * P],
                                           xpT[:, hd, mt, :], start=(mt == 0), stop=(mt == 1))
                    done(mm)
                then_norm(("x_o", l), f"norm_ffn2{l}", ("xo_cut", 4 * l), last=2)
                ffn("ffn2", l, f"norm_ffn1{l + 1}" if l < LAYERS - 1 else None)

        @block.scalar
        def _(act):
            def read(ins):
                ins.then_inc(x_read["act"], 1)

            def copy(o, i):
                return act.activation(o, i, ACT.Copy)

            def cut_weights(j, n):
                act.wait_ge(land[n % RING], 16 * (j // RING + 1))
                words = KD * P if n in half_slot else SLOT
                for half in range(2):
                    c = slice(half * words // 2, (half + 1) * words // 2)
                    act.activation(w_hi[j % 2][:, c], ring[n % RING][:, c], ACT.Copy).then_inc(hi_cut, 1)

            cutter = Cutter(act, cut_weights)
            pieces = [0]

            def cut_act(src, hi, ready=None):
                pieces[0] += 1
                if ready:
                    ready()
                else:
                    act.wait_ge(S("act_made"), pieces[0] - ffn_pieces[0])
                copy(hi, src).then_inc(S("act_hi_cut"), 1)

            ffn_pieces = [0]

            def cut_acts(src, hi, pieces_=range(4), mid=None):
                for i in pieces_:
                    two = slice(2 * i, 2 * i + 2)
                    cut_act(src[:, two, :], hi[:, two, :])
                if mid:
                    mid()

            def norm(g, part=None, l=None, src=None, hi=h_hi, each=None, between=None, before_cut=None, mid=None):
                q = NORMS.index(g)
                src = x if src is None else src
                if q and part != "g_final":
                    act.wait_ge(h_ready, 4 * q)
                for i in range(4):
                    if each:
                        each(i)
                    if part:
                        x_made(act, part, l, i)
                    act.activation(sq[:, 2 * i:2 * i + 2, :], src[:, 2 * i:2 * i + 2, :],
                                   ACT.Square).then_inc(sq_ready, 1)
                if between:
                    between()
                b = x_ready(act, "norm", g)
                read(act.activation(rstd[:, :], b[:, 0:T], ACT.Sqrt, bias=eps_col, scale=1.0 / D))
                if before_cut:
                    before_cut()
                if hi is not None:
                    cut_acts(h, hi, mid=mid)

            def late_norm(g, part, l, first, early, each=None):
                for i in range(4):
                    if each:
                        each(i)
                    x_made(act, part, l, i)
                    two = slice(2 * i, 2 * i + 2)
                    act.activation(late_sq[:, two, :], x[:, two, :], ACT.Square).then_inc(sq_ready, 1)
                    if early:
                        cut_acts(h, h_hi, (i,))
                if not early:
                    cut_acts(h, h_hi)
                prime(cutter, first)
                b = x_ready(act, "norm", g)
                read(act.activation(rstd[:, :], b[:, 0:T], ACT.Sqrt, bias=eps_col, scale=1.0 / D))

            def ffn(which, l):
                for f in range(FSTEPS):
                    cut_ahead(cutter, (which, l, "gate", f))
                    DB.was_read(act, (which, l, "gate", f))
                    act.activation(sg[:, f % 2, :, :], sg[:, f % 2, :, :], ACT.Silu).then_inc(S("silu"), 1)
                    cut_ahead(cutter, (which, l, "up", f))
                    if f > 1:
                        act.wait_ge(slots_done, SN[((which, l, "down", f - 2), f - 2)] + 1)
                    ffn_pieces[0] += 1
                    cut_act(fa[:, f % 2, :, :], fa_hi[:, f % 2, :, :],
                            lambda: act.wait_ge(S("fa_made"), (2 * l + (which == "ffn2")) * FSTEPS + f + 1))

            act.wait_ge(S("x_in"), 16)
            act.wait_ge(S("con_in"), 16)
            norm("g_mix", before_cut=lambda: cutter.upto(0), mid=lambda: prime(cutter, ("a_x", 0)))
            act.wait_ge(S("lam_abs"), 1)
            act.activation(tiny[:, 16:32], tiny[:, 0:16], ACT.Exp, scale=-1.0).then_inc(S("lam_exp"), 1)
            cut_ahead(cutter, ("a_x", 3))
            for part, dst in (("v", v_tok), ("x1", x1_tok)):
                for i in range(4):
                    cut_ahead(cutter, ("hy_" + part, i))
                    b = x_ready(act, "hy_tr", part, i)
                    read(copy(dst[:, :, i * 256:(i + 1) * 256], b[:, :].rearrange("p (t c) -> p t c", t=TT)))
            cut_ahead(cutter, ("hy_x2", 3))
            act.wait_ge(S("lru_c"), 1)
            act.wait_ge(S("par_in"), 16)

            def lru(d, first, second):
                if d:
                    act.wait_ge(S("lru_scan"), 1)
                for kind, (dst, bias) in enumerate(((lr, "lru_b_r"), (li, "lru_b_i"))):
                    for i in range(4):
                        b = m2(x_ready(act, "lru", d, kind, i))
                        for m in range(2):
                            c = 2 * i + m
                            ins = act.activation(dst[:, c, :], b[:, m, :], ACT.Sigmoid, bias=pc(bias, 8 * d + c))
                        read(ins)
                act.drain()
                for c in range(KD):
                    act.activation(le[:, c, :], lr[:, c, :], ACT.Exp, scale=tiny[:, 48 + 8 * d + c:49 + 8 * d + c])
                cut_ahead(cutter, first)
                act.drain()
                for c in range(KD):
                    act.activation(lr[:, c, :], lr[:, c, :], ACT.Exp, scale=tiny[:, 32 + 8 * d + c:33 + 8 * d + c])
                act.drain().then_inc(S("lru_exp"), 1)
                cut_ahead(cutter, second)
                act.wait_ge(S("lru_neg"), d + 1)
                act.activation(le[:, :, :], le[:, :, :], ACT.Sqrt, bias=1.0).then_inc(S("lru_mult"), 1)

            def gates(i):
                if i < 7:
                    cut_ahead(cutter, ("gates", i))
                b = d_ready(act, ("gates", i))
                act.activation(gs[:, 2 * i:2 * i + 2, :], m2(b), ACT.Sigmoid).then_inc(d_read["act"], 1)

            lru(0, ("a_gate", 0), ("a_gate", 1))
            for i in range(4):
                cut_ahead(cutter, ("a_gate", i))
                b = d_ready(act, ("a_gate", i))
                act.activation(ga[:, 2 * i:2 * i + 2, :], m2(b), ACT.Gelu_apprx_tanh).then_inc(d_read["act"], 1)
            for i in range(2):
                gates(i)
            lru(1, ("gates", 2), ("gates", 3))
            for i in range(2, 8):
                gates(i)
            cut_acts(le, h_hi)
            cut_ahead(cutter, ("gates", 7))

            for i in range(2):
                cut_ahead(cutter, ("w_a_out", 2 * i))
                act.wait_ge(S("filt_red"), i + 1)
                act.activation(sq[0:64, 1 + i, :], sq[0:64, 1 + i, :], ACT.Sin).then_inc(S("filt_sin"), 1)
            cut_ahead(cutter, ("w_a_out", 3))
            for tt in (0, 1):
                act.activation(decay[:, tt, :], decay[:, 1, :], ACT.Exp,
                               scale=con[:, CCOL["negt"] + tt:CCOL["negt"] + tt + 1])
                act.drain()
            act.drain().then_inc(S("decay"), 1)
            for n in range(2):
                for m in range(4):
                    for half in range(2):
                        b = x_ready(act, "spec_k", n, m, half)
                        read(copy(spec_k[:, m, half * 512:(half + 1) * 512], b[:, :]))
            cut_acts(x2, h_hi)
            for i in range(4):
                cut_ahead(cutter, ("w_b_out", i))
                cut_acts(gated, mn_hi, (i,))

            norm("g_ffn", "w_o", hi=None, each=lambda i: cut_ahead(cutter, ("w_o", i)))
            act.wait_ge(S("lg_shift"), 1)
            for tt in range(TT):
                act.activation(aff[:, tt, :], lg[:, tt, :], ACT.Exp, accum_out=tiny[:, tt:tt + 1])
            act.drain().then_inc(S("aff_exp"), 1)
            for tt in range(TT):
                for i in range(2):
                    b = x_ready(act, "h_tok", tt, i)
                    read(copy(h_tok[:, tt, i * 512:(i + 1) * 512], b[:, :]))
            for i in range(8):
                b = x_ready(act, "PT", i)
                read(copy(PT[:, 2 * i:2 * i + 2, :], m2(b)))
            with act.Fori(0, EXPERTS) as e:
                act.wait_ge(slots_done, ESLOTS * e + MOE + 8)
                act.activation(sg_e, psd[0][:, :], ACT.Silu).then_inc(S("sg_e"), 1)
                act.wait_ge(S("turned"), e + 1)
                copy(actT[:, :, :], psd[0][:, :].rearrange("p (b n) -> p b n", b=4)).then_inc(S("actT"), 1)
                act.wait_ge(slots_done, ESLOTS * e + MOE + ESLOTS)
                copy(ye[:, 0, :], psd[2][:, :]).then_inc(S("ye_ready"), 1)
            norm("g_final", "moe_acc", hi=None)

            for l in range(LAYERS):
                first = ("ffn1", l, "gate", 0)
                cutter.upto(slot_of(first))
                late_norm(f"norm_ffn1{l}", "ffn2" if l else "g_final", l - 1 if l else None, first, True)
                ffn("ffn1", l)
                first = (("mix_in", l), 0)
                cutter.upto(slot_of(first))
                late_norm(f"norm_mix{l}", "ffn1", l, first, True)
                for i in range(11):
                    cut_ahead(cutter, (("mix_in", l), i))
                    if 5 <= i < 8:
                        DB.was_read(act, (("mix_in", l), i))
                        act.activation(sq[:, 2 * i - 10:2 * i - 8, :], pb[:, 2 * i:2 * i + 2, :],
                                       ACT.Square).then_inc(S("qk_sq"), 1)
                    if i == 8:
                        b = x_ready(act, "qk_norm", l, 0)
                        read(act.activation(rq, b[:, 0:12], ACT.Sqrt, bias=eps_col, scale=1.0 / 64))
                        for n in range(2):
                            b = m2(x_ready(act, "qk_norm", l, 1 + n))
                            read(act.activation(rs3[:, 2 * n:2 + n, :], b[:, 0:2 - n, :], ACT.Sqrt, bias=eps_col,
                                                scale=1.0 / 64))
                for tt in range(TT):
                    b = x_ready(act, "av_tr", l, tt)
                    read(copy(v_tm[:, tt, :], b[:, 0:AW]))
                for hd in range(6):
                    act.wait_ge(S("score_max"), 6 * l + hd + 1)
                    for it, (lo_, hi_) in enumerate(((0, P), (P, AW))):
                        act.activation(prob[:, hd, lo_:hi_], prob[:, hd, lo_:hi_], ACT.Exp,
                                       bias=tiny[:, 2 * hd + it:2 * hd + it + 1],
                                       accum_out=tiny[:, 12 + 2 * hd + it:13 + 2 * hd + it])
                    act.drain().then_inc(S("score_exp"), 1)
                for hd in range(6):
                    b = x_ready(act, "prob_tr", l, hd)
                    read(copy(probT[:, hd, :, :], tri(b)))
                for q in range(HP):
                    b = x_ready(act, "att", l, q)
                    read(copy(ycat[:, 3 + q, :], b[:, 0:T]))
                b = m2(x_ready(act, "pool", l))
                for m in range(2):
                    ins = act.activation(ycat[:, 6 + m, :], b[:, m, :], ACT.Copy, scale=pc(f"c_pool_scale{l}", m))
                read(ins)

                act.wait_ge(S("kk_raw"), l + 1)
                act.activation(sq[:, 0:3, :], kk, ACT.Square).then_inc(S("kk_sq"), 1)
                act.activation(lo[0:32, :], lo[0:32, :], ACT.Tanh).then_inc(S("lora_act"), 1)
                for i in range(2):
                    b, m = m2(x_ready(act, "kk_norm", l, i)), 2 - i
                    read(act.activation(al[:, 2 * i:2 * i + m, :], b[:, 0:m, :], ACT.Sqrt))
                act.activation(lo[64:128, :], lo[64:128, :], ACT.Sigmoid).then_inc(S("lora_act"), 1)
                for kind, (dst, bias) in enumerate(((rt, "a_w0"), (aa, "a_a0"), (gg, None))):
                    for i in range(2):
                        b = m2(x_ready(act, "lora", l, kind, i))
                        for m in range(2 if i == 0 else 1):
                            j = 2 * i + m
                            ins = copy(dst[:, j, :], b[:, m, :]) if bias is None else act.activation(
                                dst[:, j, :], b[:, m, :], ACT.Sigmoid, bias=pc(f"{bias}{l}", j))
                        read(ins)
                if l:
                    b = x_ready(act, "vdown", l)
                    read(copy(vtmp, b[0:32, 0:T]))
                    for i in range(2):
                        b = m2(x_ready(act, "vup", l, i))
                        for m in range(2 if i == 0 else 1):
                            j = 2 * i + m
                            ins = act.activation(yy[:, j, :], b[:, m, :], ACT.Sigmoid, bias=pc("a_v0", j))
                        read(ins)
                act.wait_ge(S("decays"), l + 1)
                rate = math.exp(-0.5)
                act.activation(e3, be[:, :, :], ACT.Exp, scale=-rate).then_inc(S("decay_exp"), 1)
                act.activation(e2, kt[:, :, :], ACT.Exp, scale=rate).then_inc(S("decay_exp"), 1)
                act.activation(e1, kt[:, :, :], ACT.Exp, scale=-rate).then_inc(S("decay_exp"), 1)
                for tt in range(TT):
                    b = tri(x_ready(act, "rw_tr", l, tt, "a"))
                    read(copy(ab[:, :, 0:64], b.rearrange("p q (h n) -> p (q h) n", h=2)))
                    b = tri(x_ready(act, "rw_tr", l, tt, "k"))
                    for c in range(4):
                        ins = act.activation(km[:, :, c, :], b, ACT.Copy,
                                             scale=con[:, CCOL["chunk"] + c:CCOL["chunk"] + c + 1])
                    read(ins)
                    b = x_ready(act, "rw_tr", l, tt, "v")
                    read(copy(v_tm[:, tt, :], b[:, 0:AW]))
                    for name, dst in (("P2", "P2"), ("P2T", "P2T"), ("P4", "P4"), ("P4T", "P4T"), ("P8", "P2"),
                                      ("TR", "P2T"), ("X1", "P4"), ("BV", None), ("WU", "P4T")):
                        for p in range(2):
                            b = x_ready(act, name, l, tt, p)
                            if name == "BV":
                                ab_p = ab[:, :, :].rearrange("p (q h) n -> p q h n", h=2)
                                read(copy(ab_p[:, :, p, 64:128], tri(b, 64)))
                            else:
                                read(copy(MATS[dst][p][:, :, :], tri(b)))
                act.wait_ge(S("y_mean"), l + 1)
                act.activation(sq[:, 0:3, :], yy, ACT.Square).then_inc(S("yc_sq"), 1)
                cut_acts(ycat, h_hi, (2, 3))
                for i in range(2):
                    b, m = m2(x_ready(act, "var", l, i)), 2 - i
                    read(act.activation(al[:, 2 * i:2 * i + m, :], b[:, 0:m, :], ACT.Sqrt, bias=gneps_col,
                                        scale=1.0 / 64))
                act.wait_ge(S("mem_in"), 16 * (l + 1))
                norm(f"norm_mem{l}", src=memT, hi=None)
                cut_acts(ycat, h_hi, (0, 1))
                cut_acts(h, mn_hi, mid=lambda: cut_ahead(cutter, (("mix_out", l), 0)))

                def evict(part, i, dst, squares):
                    cut_ahead(cutter, ((part, l), i))
                    b = m2(d_ready(act, ((part, l), i)))
                    if squares is not None:
                        act.activation(squares[:, 2 * i:2 * i + 2, :], b, ACT.Square).then_inc(S("x_sq"), 1)
                    copy(dst, b).then_inc(d_read["act"], 1)

                def keys(first, last):
                    for i in range(first, last):
                        evict("x_k", i, xk[:, 2 * i:2 * i + 2, :], sqk)

                norm(f"norm_cross{l}", "mix_out", l, each=lambda i: cut_ahead(cutter, (("mix_out", l), i)),
                     between=lambda: keys(0, 2), mid=lambda: cut_ahead(cutter, (("x_k", l), 2)))
                keys(2, 4)
                for i in range(4):
                    evict("x_v", i, xv[:, :, i * 256:(i + 1) * 256], None)
                    if i == 0:
                        for n in range(2):
                            b = x_ready(act, "xnorm", l, "k", n)
                            read(act.activation(rs4[:, 2 * n:2 * n + 2, :], m2(b), ACT.Sqrt, bias=eps_col,
                                                scale=1.0 / 256))
                for i in range(4):
                    evict("x_q", i, xq[:, 2 * i:2 * i + 2, :], sqq)
                b = x_ready(act, "xnorm", l, "q", 0)
                read(act.activation(rq[:, 0:8], b[:, 0:8], ACT.Sqrt, bias=eps_col, scale=1.0 / 256))
                for hd in range(4):
                    act.wait_ge(S("xscore_max"), 4 * l + hd + 1)
                    for it in range(TT):
                        j = 2 * hd + it
                        act.activation(xprob[:, j, :], xprob[:, j, :], ACT.Exp, bias=tiny[:, j:j + 1],
                                       accum_out=tiny[:, 12 + j:13 + j])
                    act.drain().then_inc(S("xscore_exp"), 1)
                for hd in range(4):
                    b = x_ready(act, "xprob_tr", l, hd)
                    read(copy(xpT[:, hd, :, :], m2(b)))
                cut_acts(xo, h_hi)
                late_norm(f"norm_ffn2{l}", "x_o", l, ("ffn2", l, "gate", 0), False,
                          each=lambda i: cut_ahead(cutter, (("x_o", l), i)))
                ffn("ffn2", l)

        @block.vector
        def _(dve):
            def read(ins):
                ins.then_inc(x_read["dve"], 1)

            def dread(ins):
                ins.then_inc(d_read["dve"], 1)

            def tt_(o, a, b, op):
                return dve.tensor_tensor(o, a, b, op)

            def cut_weights(j, n):
                words = KD * P if n in half_slot else SLOT
                for half in range(2):
                    dve.wait_ge(hi_cut, 2 * j + half + 1)
                    c = slice(half * words // 2, (half + 1) * words // 2)
                    tt_(w_lo[j % 2][:, c], ring[n % RING][:, c], w_hi[j % 2][:, c].bitcast(F32),
                        ALU.subtract).then_inc(lo_cut, 1)

            cutter = Cutter(dve, cut_weights)
            pieces = [0]

            def cut_act(src, hi, lo):
                pieces[0] += 1
                dve.wait_ge(S("act_hi_cut"), pieces[0])
                return tt_(lo, src, hi.bitcast(F32), ALU.subtract)

            def low(src, hi, lo, i, flag):
                two = slice(2 * i, 2 * i + 2)
                cut_act(src[:, two, :], hi[:, two, :], lo[:, two, :]).then_inc(S(flag), 1)

            def cut_acts(src, flag=None, pieces_=range(4)):
                dve.drain().then_inc(S("act_made"), len(pieces_))
                for i in pieces_:
                    two = slice(2 * i, 2 * i + 2)
                    cut_act(src[:, two, :], h_hi[:, two, :], h_lo[:, two, :])
                if flag:
                    dve.drain().then_inc(S(flag), 1)

            def norm(g, dst=None, src=None, halves_=(h_hi, h_lo), before_cut=None, mid=None):
                src = x if src is None else src
                XB.was_read(dve, ("norm", g))
                dve.reciprocal(rstd[:, :], rstd[:, :])
                dve.drain()
                dst = h if dst is None else dst
                if before_cut:
                    before_cut()
                for i in range(5):
                    if i < 4:
                        for k in (2 * i, 2 * i + 1):
                            ins = dve.scalar_tensor_tensor(out=dst[:, k, :], in0=src[:, k, :], scalar=pc(g, k),
                                                           in1=rstd[:, :], op0=ALU.mult, op1=ALU.mult)
                        ins.then_inc(S("act_made") if halves_ else h_ready, 1)
                    if i and halves_:
                        two = slice(2 * i - 2, 2 * i)
                        cut_act(dst[:, two, :], *(v[:, two, :] for v in halves_)).then_inc(h_ready, 1)
                if mid:
                    mid()

            def late_norm(g, evict, first, early):
                for i in range(4):
                    evict(i)
                    dve.drain()
                    for k in (2 * i, 2 * i + 1):
                        ins = dve.tensor_scalar(h[:, k, :], x[:, k, :], pc(g, k), None, ALU.mult)
                    ins.then_inc(S("act_made"), 1)
                    if early and i:
                        low(h, h_hi, h_lo, i - 1, "h_ready")
                for i in range(3 if early else 0, 4):
                    low(h, h_hi, h_lo, i, "h_ready")
                prime(cutter, first)
                XB.was_read(dve, ("norm", g))
                dve.reciprocal(rstd[:, :], rstd[:, :])
                dve.drain()

            def ffn(which, l, g=None, first=None):
                for f in range(FSTEPS):
                    step = (2 * l + (which == "ffn2")) * FSTEPS + f + 1
                    cut_ahead(cutter, (which, l, "gate", f))
                    b = m2(d_ready(dve, (which, l, "gate", f)))
                    dread(tt_(sg[:, f % 2, :, :], b, by_token, ALU.mult))
                    cut_ahead(cutter, (which, l, "up", f))
                    b = m2(d_ready(dve, (which, l, "up", f)))
                    dread(tt_(fa[:, f % 2, :, :], b, by_token, ALU.mult))
                    dve.drain()
                    dve.wait_ge(S("silu"), step)
                    tt_(fa[:, f % 2, :, :], fa[:, f % 2, :, :], sg[:, f % 2, :, :], ALU.mult).then_inc(S("fa_made"), 1)
                    if f > 1:
                        dve.wait_ge(slots_done, SN[((which, l, "down", f - 2), f - 2)] + 1)
                    cut_act(fa[:, f % 2, :, :], fa_hi[:, f % 2, :, :], fa_lo[:, f % 2, :, :]).then_inc(S("fa_cut"), 1)

                def evict(i):
                    b = m2(x_ready(dve, which, l, i))
                    read(dve.scalar_tensor_tensor(out=x[:, 2 * i:2 * i + 2, :], in0=b, scalar=0.5,
                                                  in1=x[:, 2 * i:2 * i + 2, :], op0=ALU.mult, op1=ALU.add))

                if g:
                    cutter.upto(slot_of(first))
                    late_norm(g, evict, first, True)
                else:
                    for i in range(4):
                        evict(i)

            dve.wait_ge(S("par_in"), 16)
            dve.wait_ge(S("con_in"), 16)
            lam = par[:, PCOL["lru_lambda"]:PCOL["lru_lambda"] + 16]
            t0, t1, t2, t3 = (tiny[:, i:i + 16] for i in (0, 16, 32, 48))
            dve.tensor_scalar(t0, lam, -1.0, None, ALU.mult)
            dve.drain()
            tt_(t0, t0, lam, ALU.max)
            dve.drain().then_inc(S("lam_abs"), 1)
            norm("g_mix", before_cut=lambda: cutter.upto(0), mid=lambda: prime(cutter, ("a_x", 0)))
            dve.wait_ge(S("lam_exp"), 1)
            dve.tensor_scalar(t2, t1, 2.0, None, ALU.add)
            dve.drain()
            dve.reciprocal(t2, t2)
            dve.drain()
            tt_(t1, t1, t2, ALU.mult)
            dve.drain()
            tt_(t2, t1, t1, ALU.mult)
            dve.memset(t3, 1.0 / 21)
            for n in range(19, 0, -2):
                dve.drain()
                tt_(t3, t3, t2, ALU.mult)
                dve.drain()
                dve.tensor_scalar(t3, t3, 1.0 / n, None, ALU.add)
            dve.drain()
            tt_(t3, t3, t1, ALU.mult)
            dve.tensor_scalar(t0, lam, -1.0, 0.0, ALU.mult, ALU.max)
            dve.drain()
            dve.scalar_tensor_tensor(out=t3, in0=t3, scalar=2.0, in1=t0, op0=ALU.mult, op1=ALU.add)
            dve.drain()
            dve.tensor_scalar(t2, t3, -8.0, None, ALU.mult)
            dve.tensor_scalar(t3, t3, -16.0, None, ALU.mult)
            dve.drain().then_inc(S("lru_c"), 1)

            def conv(b, dst, taps, centre, w, bias):
                b = m2(b)
                order = [centre] + [j for j in range(taps) if j != centre]
                for j in order:
                    o = j - centre
                    for m in range(2):
                        if o == 0:
                            ins = dve.tensor_scalar(dst[m], b[:, m, :], w(j, m), bias(m), ALU.mult, ALU.add)
                        else:
                            a0, a1 = max(0, -o), T - max(0, o)
                            ins = dve.scalar_tensor_tensor(out=dst[m][:, a0:a1], in0=b[:, m, a0 + o:a1 + o],
                                                           scalar=w(j, m), in1=dst[m][:, a0:a1],
                                                           op0=ALU.mult, op1=ALU.add)
                    if j != order[-1]:
                        dve.drain()
                dread(ins)

            for i in range(4):
                cut_ahead(cutter, ("a_x", i))
                conv(d_ready(dve, ("a_x", i)), [xa[:, 2 * i + m, :] for m in range(2)], 4, 2,
                     lambda j, m: pc("conv_a_w", 8 * j + 2 * i + m), lambda m: pc("conv_a_b", 2 * i + m))
            tr = []
            for part, base in (("v", 0), ("x1", 8), ("x2", 16)):
                for i in range(4):
                    cut_ahead(cutter, ("hy_" + part, i))
                    b = d_ready(dve, ("hy_" + part, i))
                    if part == "x2":
                        dst = [x2[:, 2 * i + m, :] for m in range(2)]
                    else:
                        dst = [sq[:, 2 * (i % 2) + m, :] for m in range(2)]
                        if len(tr) > 1:
                            x_ready(dve, "hy_tr", *tr[-2])
                        tr.append((part, i))
                    conv(b, dst, 3, 1, lambda j, m: pc("conv_b_w", 24 * j + base + 2 * i + m),
                         lambda m: pc("conv_b_b", base + 2 * i + m))

            def lru(d, *cuts):
                cut_ahead(cutter, cuts[0])
                dve.wait_ge(S("lru_exp"), d + 1)
                dve.tensor_scalar(le[:, :, :], le[:, :, :], 1.0, -1.0, ALU.min, ALU.mult)
                tt_(li[:, :, :], li[:, :, :], xa, ALU.mult)
                dve.drain()
                first = 0 if d == 0 else T - 1
                dve.memset(le[:, :, first:first + 1], 0.0)
                dve.drain().then_inc(S("lru_neg"), 1)
                cut_ahead(cutter, cuts[1])
                dve.wait_ge(S("lru_mult"), d + 1)
                tt_(li[:, :, :], li[:, :, :], le[:, :, :], ALU.mult)
                dve.drain()
                for c in range(KD):
                    if c == KD // 2:
                        cut_ahead(cutter, cuts[2])
                    if d == 0:
                        dve.tensor_tensor_scan(lh[:, c, :], lr[:, c, :], li[:, c, :], 0.0, ALU.mult, ALU.add)
                    else:
                        dve.tensor_tensor_scan(le[:, c, ::-1], lr[:, c, ::-1], li[:, c, ::-1], 0.0,
                                               ALU.mult, ALU.add)
                dve.drain().then_inc(S("lru_scan"), 1)

            lru(0, ("a_gate", 1), ("a_gate", 2), ("a_gate", 3))
            cut_ahead(cutter, ("gates", 1))
            lru(1, ("gates", 2), ("gates", 3), ("gates", 4))
            cut_ahead(cutter, ("gates", 5))
            DB.was_read(dve, ("a_gate", 3))
            tt_(le[:, :, :], lh[:, :, :], le[:, :, :], ALU.add)
            dve.drain()
            for i in range(4):
                two = slice(2 * i, 2 * i + 2)
                tt_(le[:, two, :], le[:, two, :], ga[:, two, :], ALU.mult).then_inc(S("act_made"), 1)
            cut_ahead(cutter, ("gates", 6))
            for i in range(4):
                low(le, h_hi, h_lo, i, "lru_out")
            cut_ahead(cutter, ("gates", 7))

            def gate_a(i):
                cut_ahead(cutter, ("w_a_out", i))
                b = m2(d_ready(dve, ("w_a_out", i)))
                dread(tt_(gated[:, 2 * i:2 * i + 2, :], b, gs[:, 2 * i:2 * i + 2, :], ALU.mult))

            DB.was_read(dve, ("gates", 7))
            for i in range(2):
                gate_a(2 * i)
                b = x_ready(dve, "filt", i)[0:64, 0:T]
                v, k = sq[0:64, 1 + i, :], sq[0:64, 3, :]
                read(dve.tensor_scalar(v, b, pc(f"filt_b{i + 1}", 0, 0, 64), pc("filt_freq", i, 0, 64),
                                       ALU.add, ALU.mult))
                dve.drain()
                dve.tensor_scalar(k, v, 1 / (2 * math.pi), L2, ALU.mult, ALU.add)
                dve.drain()
                dve.tensor_scalar(k, k, L2, None, ALU.subtract)
                dve.drain()
                for part in (TWO_PI_HI, TWO_PI_LO):
                    dve.scalar_tensor_tensor(out=v, in0=k, scalar=-part, in1=v, op0=ALU.mult, op1=ALU.add)
                    dve.drain()
                dve.tensor_scalar(v, v, 3.1415925, -3.1415925, ALU.min, ALU.max)
                dve.drain().then_inc(S("filt_red"), 1)
                gate_a(2 * i + 1)
            dve.wait_ge(S("decay"), 1)
            bias_row = at(8, 2, D, parts=1)
            f0, f1 = (sq[:, i:i + 2, :].rearrange("p a t -> p (a t)") for i in (4, 6))
            dve.wait_ge(S("bias_in"), 16)
            for n in range(2):
                for tt in range(TT):
                    for half in range(2):
                        cs = slice(half * 512, (half + 1) * 512)
                        for d, dst in ((0, f0), (1, f1)):
                            b = x_ready(dve, "taps", n, tt, half, d)
                            read(tt_(dst, b[:, :], decay[:, tt, cs], ALU.mult))
                        dve.drain()
                        if tt == 0:
                            dve.memset(f1[0:1, :], 0.0)
                            tt_(f0[0:1, :], f0[0:1, :], bias_row[:, n, cs], ALU.add)
                            dve.drain()
                        tt_(taps_s[:, tt, cs], f0, f1, ALU.add)
                        tt_(taps_d[:, tt, cs], f0, f1, ALU.subtract)
                        dve.drain()
                dve.drain().then_inc(S("taps_ready"), 1)
                XB.was_read(dve, ("spec_k", n, 3, 1))
                for half in range(2):
                    cs = slice(half * 512, (half + 1) * 512)
                    for f in range(2):
                        kr, ki = spec_k[:, f, cs], spec_k[:, 2 + f, cs]
                        yr, yi = spec_y[:, f, cs], spec_y[:, 2 + f, cs]
                        ur = x_ready(dve, "spec_u", n, half, f, 0)
                        tt_(yr, ur[:, :], kr, ALU.mult)
                        read(tt_(yi, ur[:, :], ki, ALU.mult))
                        ui = x_ready(dve, "spec_u", n, half, f, 1)
                        tt_(f0, ui[:, :], ki, ALU.mult)
                        read(tt_(f1, ui[:, :], kr, ALU.mult))
                        dve.drain()
                        tt_(yr, yr, f0, ALU.subtract)
                        tt_(yi, yi, f1, ALU.add)
                        dve.drain().then_inc(S("spec_y"), 1)
                for i in range(4):
                    b = x_ready(dve, "inv", n, i)
                    if n == 0:
                        tt, cs = i // 2, slice((i % 2) * 512, (i % 2 + 1) * 512)
                        read(tt_(v_tok[:, tt, cs], b[:, :], x1_tok[:, tt, cs], ALU.mult))
                    else:
                        read(tt_(x2[:, 2 * i:2 * i + 2, :], m2(b), x2[:, 2 * i:2 * i + 2, :], ALU.mult))
                if n == 0:
                    dve.drain().then_inc(S("z_tok"), 4)
            cut_acts(x2, "z_cut")
            for i in range(4):
                cut_ahead(cutter, ("w_b_out", i))
                b = m2(d_ready(dve, ("w_b_out", i)))
                two = slice(2 * i, 2 * i + 2)
                dread(tt_(sq[:, two, :], b, gs[:, KD + 2 * i:KD + 2 * i + 2, :], ALU.mult))
                dve.drain()
                tt_(gated[:, two, :], gated[:, two, :], sq[:, two, :], ALU.add).then_inc(S("act_made"), 1)
                low(gated, mn_hi, mn_lo, i, "merged")
            for i in range(4):
                cut_ahead(cutter, ("w_o", i))
                b = m2(d_ready(dve, ("w_o", i)))
                two = slice(2 * i, 2 * i + 2)
                dread(tt_(x[:, two, :], b, x[:, two, :], ALU.add))

            norm("g_ffn", halves_=None)
            b = x_ready(dve, "router")[:, 0:32].rearrange("p (t e) -> p t e", t=TT)
            dve.tensor_reduce(tiny[:, 4:6], b, AXX, ALU.max)
            dve.drain()
            read(tt_(lg, b, tiny[:, 4:6].unsqueeze(2).broadcast_to([P, TT, 16]), ALU.subtract))
            dve.drain().then_inc(S("lg_shift"), 1)
            dve.wait_ge(S("aff_exp"), 1)
            dve.reciprocal(tiny[:, 2:4], tiny[:, 0:2])
            dve.drain()
            tt_(aff, aff, tiny[:, 2:4].unsqueeze(2).broadcast_to([P, TT, 16]), ALU.mult)
            dve.drain().then_inc(S("aff"), 1)
            b = x_ready(dve, "affT")
            dve.memset(ones16, 1.0)
            read(dve.tensor_copy(wk, b[0:16, 0:T]))
            for _ in range(CAP // 8):
                dve.drain()
                dve.max(top8, wk)
                dve.drain()
                dve.match_replace(wk, top8, wk, -1.0)
            dve.drain()
            dve.tensor_scalar(msk, wk, 0.0, None, ALU.is_lt)
            dve.drain()
            dve.tensor_tensor_scan(slotT, ones16, msk, 0.0, ALU.mult, ALU.add)
            dve.drain()
            tt_(slotT, slotT, msk, ALU.mult)
            dve.drain().then_inc(S("slotT"), 1)
            b = x_ready(dve, "slot_tr")[:, 0:32].rearrange("p (t e) -> p t e", t=TT)
            read(dve.tensor_copy(slots, b))
            dve.drain()
            for tt in range(TT):
                tt_(onehot[:, tt, :, :], cst("iota", CAP).unsqueeze(1).broadcast_to([P, EXPERTS, CAP]),
                    slots[:, tt, :].unsqueeze(2).broadcast_to([P, EXPERTS, CAP]), ALU.is_equal)
            dve.drain()
            for tt in range(TT):
                for j in range(4):
                    tt_(weighted[:, tt, :, j * CAP:(j + 1) * CAP], onehot[:, tt, :, :],
                        aff[:, tt, :].unsqueeze(2).broadcast_to([P, EXPERTS, CAP]), ALU.mult)
            dve.drain().then_inc(S("weighted"), 1)
            for i in range(8):
                b = x_ready(dve, "xe", i)
                read(dve.tensor_copy(xe[:, i, :], b[:, :]))
            dve.drain()
            with dve.Fori(0, EXPERTS) as e:
                dve.wait_ge(slots_done, ESLOTS * e + (MOE - 8))
                dve.tensor_copy(xs, xe[:, :, bass.ds(e * CAP, CAP)]).then_inc(S("xs_ready"), 1)
                dve.wait_ge(slots_done, ESLOTS * e + MOE + 16)
                dve.wait_ge(S("sg_e"), e + 1)
                tt_(act_e, psd[1][:, :], sg_e, ALU.mult).then_inc(S("act_e"), 1)
                dve.wait_ge(slots_done, ESLOTS * e + MOE + ESLOTS)
                dve.tensor_copy(ye[:, 1, :], psd[3][:, :]).then_inc(S("ye_ready"), 1)
            for i in range(4):
                b = m2(x_ready(dve, "moe_acc", i))
                read(dve.tensor_copy(x[:, 2 * i:2 * i + 2, :], b))
            norm("g_final", x, halves_=None)

            for l in range(LAYERS):
                if l == 0:
                    first = ("ffn1", l, "gate", 0)
                    cutter.upto(slot_of(first))
                    late_norm(f"norm_ffn1{l}", lambda i: None, first, True)
                ffn("ffn1", l, f"norm_mix{l}", (("mix_in", l), 0))

                def project(i):
                    cut_ahead(cutter, (("mix_in", l), i))
                    b, m = m2(d_ready(dve, (("mix_in", l), i))), 2 if i < 10 else 1
                    dread(tt_(pb[:, 2 * i:2 * i + m, :], b[:, 0:m, :], by_token[:, 0:m, :], ALU.mult))

                for i in range(9):
                    project(i)

                gain = tiny[:, 36:37]
                tt_(gain, pc(f"b_q_gain{l}"), pc(f"b_k_gain{l}"), ALU.mult)
                XB.was_read(dve, ("qk_norm", l, 0))
                dve.reciprocal(rq, rq)
                for n in range(2):
                    XB.was_read(dve, ("qk_norm", l, 1 + n))
                    dve.reciprocal(rs3[:, 2 * n:2 + n, :], rs3[:, 2 * n:2 + n, :])
                dve.drain()
                dve.tensor_scalar(rq, rq, 64 ** -0.5, None, ALU.mult)
                for j in range(HP):
                    dve.scalar_tensor_tensor(out=pb[:, 13 + j, :], in0=pb[:, 13 + j, :], scalar=gain,
                                             in1=rs3[:, j, :], op0=ALU.mult, op1=ALU.mult)
                dve.drain().then_inc(S("qk_ready"), 1)
                project(9)
                project(10)
                dve.wait_ge(S(f"att_in{l}"), 32)

                def normalise(hd):
                    dve.wait_ge(S("score_exp"), 6 * l + hd + 1)
                    dve.reciprocal(tiny[:, 40 + 2 * hd:42 + 2 * hd], tiny[:, 12 + 2 * hd:14 + 2 * hd])
                    dve.drain()
                    for it, (lo_, hi_) in enumerate(((0, P), (P, AW))):
                        j = 40 + 2 * hd + it
                        dve.tensor_scalar(prob[:, hd, lo_:hi_], prob[:, hd, lo_:hi_], tiny[:, j:j + 1], None, ALU.mult)
                    dve.drain().then_inc(S("prob"), 1)

                for hd in range(6):
                    for it, (lo_, hi_) in enumerate(((0, P), (P, AW))):
                        b = x_ready(dve, "score", l, hd, it)
                        pr = prob[:, hd, lo_:hi_]
                        read(dve.scalar_tensor_tensor(out=pr, in0=b[:, 0:hi_ - lo_],
                                                      scalar=rq[:, 2 * hd + it:2 * hd + it + 1],
                                                      in1=rbias[:, hd, lo_:hi_], op0=ALU.mult, op1=ALU.add))
                    dve.drain()
                    for it, (lo_, hi_) in enumerate(((0, P), (P, AW))):
                        dve.tensor_reduce(tiny[:, 24 + 2 * hd + it:25 + 2 * hd + it], prob[:, hd, lo_:hi_], AXX, ALU.max)
                    dve.drain()
                    dve.tensor_scalar(tiny[:, 2 * hd:2 * hd + 2], tiny[:, 24 + 2 * hd:26 + 2 * hd], -1.0, None, ALU.mult)
                    dve.drain().then_inc(S("score_max"), 1)
                    if hd > 1:
                        normalise(hd - 2)
                normalise(4)
                normalise(5)

                mu = par[:, PCOL[f"a_mu{l}"]:PCOL[f"a_mu{l}"] + 10]
                dve.tensor_scalar(tiny[:, 0:10], mu, -1.0, 1.0, ALU.mult, ALU.add)
                dve.drain()
                for j in range(10):
                    dve.tensor_scalar(ts[:, j, :], pb[:, j, :], tiny[:, j:j + 1], None, ALU.mult)
                dve.drain()
                for j in range(10):
                    dve.scalar_tensor_tensor(out=ts[:, j, 1:T], in0=pb[:, j, 0:T - 1], scalar=mu[:, j:j + 1],
                                             in1=ts[:, j, 1:T], op0=ALU.mult, op1=ALU.add)
                dve.drain()
                r_, k_, v_ = ts[:, 0:3, :], ts[:, 3:6, :], ts[:, 6:9, :]
                for j in range(HP):
                    dve.tensor_scalar(kk[:, j, :], k_[:, j, :], pc(f"a_k_k{l}", j), None, ALU.mult)
                dve.drain().then_inc(S("kk_raw"), 1)
                XB.was_read(dve, ("kk_norm", l, 1))
                dve.tensor_scalar(al[:, :, :], al[:, :, :], 1e-12, None, ALU.max)
                dve.drain()
                dve.reciprocal(al[:, :, :], al[:, :, :])
                dve.drain()
                tt_(kk, kk, al[:, :, :], ALU.mult)
                XB.was_read(dve, ("lora", l, 0, 1))
                for j in range(HP):
                    dve.tensor_tensor_scan(kt[:, j, :], cst("reset", T), rt[:, j, :], 0.0, ALU.mult, ALU.add)
                dve.drain()
                tt_(be[:, :, :], kt[:, :, :], rt[:, :, :], ALU.subtract)
                dve.drain().then_inc(S("decays"), 1)
                XB.was_read(dve, ("lora", l, 2, 1))
                for j in range(HP):
                    dve.tensor_scalar(rt[:, j, :], aa[:, j, :], -1.0, pc(f"a_k_a{l}", j), ALU.add, ALU.mult)
                dve.drain()
                dve.scalar_tensor_tensor(out=k_, in0=rt[:, :, :], scalar=1.0, in1=k_, op0=ALU.add, op1=ALU.mult)
                tt_(aa, kk, aa, ALU.mult)
                dve.wait_ge(S("decay_exp"), 3 * l + 1)
                dve.scalar_tensor_tensor(out=al[:, :, :], in0=kk, scalar=-1.0, in1=e3, op0=ALU.mult,
                                         op1=ALU.mult).then_inc(S("rw_scaled"), 1)
                dve.drain()
                dve.wait_ge(S("decay_exp"), 3 * l + 3)
                for dst, a_, b_ in ((be, aa, e2), (kt, k_, e2), (rt, r_, e1)):
                    tt_(dst[:, :, :], a_, b_, ALU.mult).then_inc(S("rw_scaled"), 1)

                rows = [slice(64 * p, 64 * p + 64) for p in range(2)]
                for tt in range(TT):
                    tok = slice(tt * P, (tt + 1) * P)
                    b = tri(x_ready(dve, "rw_tr", l, tt, "b"))
                    for c in range(4):
                        ins = dve.tensor_scalar(bm[:, :, c, :], b, con[:, CCOL["chunk"] + c:CCOL["chunk"] + c + 1],
                                                None, ALU.mult)
                    read(ins)

                    def mask(name):
                        return cst(name, P).unsqueeze(1).broadcast_to([P, HP, P])

                    for name, kinds in (("A", (("Aoff", "off32"), ("A", "low16"))), ("AT", (("AT", "up16"),)),
                                        ("BT", (("BT", "up32"),)), ("CT", (("CT", "upi32"),)),
                                        ("DT", (("DT", "upi32"),))):
                        for p in range(2):
                            b = tri(x_ready(dve, name, l, tt, p))
                            if name == "BT" and p == 0:
                                dve.drain()
                                for pp in range(2):
                                    tt_(MATS["Q"][pp], MATS["AT"][pp], mask("ident"), ALU.add)
                            for dst, mk in kinds:
                                ins = tt_(MATS[dst][p], b, mask(mk), ALU.mult)
                            read(ins)
                    for name in ("Q2", "Q4", "Q8", "Q32"):
                        dve.drain()
                        for p in range(2):
                            b = tri(x_ready(dve, name, l, tt, p))
                            read(tt_(MATS["Q"][p], b, MATS["Q"][p], ALU.add))
                    if tt == 0:
                        dve.wait_ge(S("mt_zero"), l + 1)
                    for q in range(HP):
                        b = x_ready(dve, "M", l, tt, q)
                        for p in range(2):
                            ins = tt_(MT[rows[p], :, q, rows[p]],
                                      b[rows[p], 0:T].rearrange("p (c n) -> p c n", c=4),
                                      ident[rows[p], rows[p]].unsqueeze(1).broadcast_to([64, 4, 64]), ALU.add)
                        read(ins)
                        ends = e1[:, q, tt * P + CH - 1:(tt + 1) * P:CH]
                        b = x_ready(dve, "N", l, tt, q)
                        read(tt_(Np[:, :, q, :], b[:, 0:T].rearrange("p (c n) -> p c n", c=4),
                                 ends.unsqueeze(2).broadcast_to([P, 4, 64]), ALU.mult))
                        b = x_ready(dve, "RY", l, tt, q)
                        tt_(RT[:, q, :], b[:, 0:P], rt[:, q, tok], ALU.add)
                        read(dve.tensor_copy(y0T[:, q, :], b[:, P:T]))
                    if tt == 0:
                        dve.memset(Xs[:, 0, :, :], 0.0)
                    else:
                        dve.tensor_copy(Xs[:, 0, :, :], Xs[:, 4, :, :])
                    dve.drain().then_inc(S("state0"), 1)
                    for c in range(4):
                        b = tri(x_ready(dve, "S", l, tt, c), 64)
                        for q in range(HP):
                            end = tt * P + (c + 1) * CH - 1
                            ins = dve.scalar_tensor_tensor(out=Xs[:, c + 1, q, :], in0=b[:, q, :],
                                                           scalar=e1[:, q, end:end + 1], in1=Np[:, c, q, :],
                                                           op0=ALU.mult, op1=ALU.add)
                        read(ins)
                    for p in range(2):
                        b = tri(x_ready(dve, "y", l, tt, p))
                        read(tt_(yy[rows[p], :, tok], b[rows[p], :, :], y0T[rows[p], :, :], ALU.add))
                    dve.drain()
                dve.drain().then_inc(S("y_ready"), 1)
                for i in range(2):
                    b, m = m2(x_ready(dve, "mean", l, i)), 2 - i
                    yv = yy[:, 2 * i:2 * i + m, :]
                    read(dve.scalar_tensor_tensor(out=yv, in0=b[:, 0:m, :], scalar=-1.0 / 64, in1=yv,
                                                  op0=ALU.mult, op1=ALU.add))
                dve.drain().then_inc(S("y_mean"), 1)
                for j in range(HP):
                    dve.scalar_tensor_tensor(out=e1[:, j, :], in0=r_[:, j, :], scalar=pc(f"a_r_k{l}", j),
                                             in1=k_[:, j, :], op0=ALU.mult, op1=ALU.mult)
                dve.drain().then_inc(S("rk_ready"), 1)
                cut_acts(ycat, pieces_=(2, 3))
                for i in range(2):
                    XB.was_read(dve, ("var", l, i))
                    dve.reciprocal(al[:, 2 * i:2 + i, :], al[:, 2 * i:2 + i, :])
                dve.drain()
                for j in range(HP):
                    dve.scalar_tensor_tensor(out=yy[:, j, :], in0=yy[:, j, :], scalar=pc(f"a_gn_g{l}", j),
                                             in1=al[:, j, :], op0=ALU.mult, op1=ALU.mult)
                for i in range(2):
                    b, m = m2(x_ready(dve, "bonus", l, i)), 2 - i
                    two = slice(2 * i, 2 * i + m)
                    read(tt_(e2[:, two, :], b[:, 0:m, :], v_[:, two, :], ALU.mult))
                dve.drain()
                for j in range(HP):
                    dve.scalar_tensor_tensor(out=yy[:, j, :], in0=yy[:, j, :], scalar=pc(f"a_gn_b{l}", j),
                                             in1=e2[:, j, :], op0=ALU.add, op1=ALU.add)
                dve.drain()
                tt_(ycat[:, 0:3, :], yy, gg, ALU.mult)
                cut_acts(ycat, "mix_cat", (0, 1))
                norm(f"norm_mem{l}", src=memT, halves_=(mn_hi, mn_lo),
                     mid=lambda: cut_ahead(cutter, (("mix_out", l), 0)))
                for i in range(4):
                    cut_ahead(cutter, (("mix_out", l), i))
                    b = m2(d_ready(dve, (("mix_out", l), i)))
                    two = slice(2 * i, 2 * i + 2)
                    dread(tt_(x[:, two, :], b, x[:, two, :], ALU.add))

                cut_ahead(cutter, (("x_k", l), 1))
                norm(f"norm_cross{l}", mid=lambda: cut_ahead(cutter, (("x_k", l), 2)))
                gain = tiny[:, 36:38]
                tt_(gain, *(par[:, PCOL[f"x_{n}_gain{l}"]:PCOL[f"x_{n}_gain{l}"] + 2] for n in "qk"), ALU.mult)
                for n in range(2):
                    cut_ahead(cutter, (("x_v", l), n))
                    XB.was_read(dve, ("xnorm", l, "k", n))
                    dve.reciprocal(rs4[:, 2 * n:2 * n + 2, :], rs4[:, 2 * n:2 * n + 2, :])
                    dve.drain()
                    for c in range(4 * n, 4 * n + 4):
                        dve.scalar_tensor_tensor(out=xk[:, c, :], in0=xk[:, c, :], scalar=tiny[:, 36 + c % 2:37 + c % 2],
                                                 in1=rs4[:, c // 2, :], op0=ALU.mult, op1=ALU.mult)
                dve.drain().then_inc(S("xk_ready"), 1)
                cut_ahead(cutter, (("x_q", l), 3))
                XB.was_read(dve, ("xnorm", l, "q", 0))
                dve.reciprocal(rq[:, 0:8], rq[:, 0:8])
                dve.drain()
                for hd in range(4):
                    for it in range(TT):
                        j = 2 * hd + it
                        b = x_ready(dve, "xscore", l, hd, it)
                        read(dve.tensor_scalar(xprob[:, j, :], b[:, 0:T], rq[:, j:j + 1], 1.0 / 16, ALU.mult, ALU.mult))
                        dve.drain()
                        dve.tensor_reduce(tiny[:, 24 + j:25 + j], xprob[:, j, :], AXX, ALU.max)
                    dve.drain()
                    dve.tensor_scalar(tiny[:, 2 * hd:2 * hd + 2], tiny[:, 24 + 2 * hd:26 + 2 * hd], -1.0, None, ALU.mult)
                    dve.drain().then_inc(S("xscore_max"), 1)
                for hd in range(4):
                    dve.wait_ge(S("xscore_exp"), 4 * l + hd + 1)
                    dve.reciprocal(tiny[:, 40 + 2 * hd:42 + 2 * hd], tiny[:, 12 + 2 * hd:14 + 2 * hd])
                    dve.drain()
                    for it in range(TT):
                        j = 2 * hd + it
                        dve.tensor_scalar(xprob[:, j, :], xprob[:, j, :], tiny[:, 40 + j:41 + j], None, ALU.mult)
                    dve.drain().then_inc(S("xprob"), 1)
                for hd in range(4):
                    b = x_ready(dve, "xatt", l, hd)
                    read(dve.tensor_copy(xo[:, 2 * hd:2 * hd + 2, :], m2(b)))
                    dve.drain().then_inc(S("act_made"), 1)
                    if hd:
                        low(xo, h_hi, h_lo, hd - 1, "xo_cut")
                low(xo, h_hi, h_lo, 3, "xo_cut")

                def evict(i):
                    cut_ahead(cutter, (("x_o", l), i))
                    b = m2(d_ready(dve, (("x_o", l), i)))
                    two = slice(2 * i, 2 * i + 2)
                    dread(tt_(x[:, two, :], b, x[:, two, :], ALU.add))

                late_norm(f"norm_ffn2{l}", evict, ("ffn2", l, "gate", 0), False)
                if l < LAYERS - 1:
                    ffn("ffn2", l, f"norm_ffn1{l + 1}", ("ffn1", l + 1, "gate", 0))
                else:
                    ffn("ffn2", l)

        @block.gpsimd
        def _(pool):
            def load(dst, src, flag):
                pool.dma_start(dst, src).then_inc(S(flag), 16)

            d_ready(pool, ("a_x", 0))
            load(bd[:, :, :, :], A["lru_bd"].rearrange("p (s c n) -> p s c n", s=4, c=KD), "bd_in")
            pool.wait_ge(S("lru_scan"), 2)
            load(zT, A["zT"], "filt_in")
            load(filt_w[0:33, 0:64], A["filt_w1"], "filt_in")
            load(filt_w[0:64, 64:128], A["filt_w2"], "filt_in")
            load(decay[:, 1, :], A["deltas"].broadcast_to([P, D]), "filt_in")
            load(at(0, 8 * T), A["dft"], "dft_in")
            pool.wait_ge(S("lru_out"), 4)
            load(at(8, 2 * D, parts=1), A["filt_bias"], "bias_in")
            w3 = A["filt_w3"].rearrange("i (n d h c) -> n i d h c", n=2, d=2, h=2)
            load(w3h[:, :, :, :], w3[0], "w3_in0")
            x_ready(pool, "taps", 0, 1, 1, 1)
            load(w3h[:, :, :, :], w3[1], "w3_in1")
            x_ready(pool, "taps", 1, 1, 1, 1)
            load(wr[:, :, :], A["w_router"].rearrange("(k p) e -> p k e", p=P), "wr_in")
            for l in range(LAYERS):
                DB.was_read(pool, ("ffn1", l, "gate", 0))
                load(rbias[:, :, :], A["rel_bias"][l].rearrange("p (h n) -> p h n", h=6), f"att_in{l}")
                load(poolw[:, :, :], A["pool_w"][l].rearrange("p (m n) -> p m n", m=2), f"att_in{l}")
                load(lora_up, A["lora_up"][l], f"lora_in{l}")
                if l:
                    load(vdn[:, :, :], A["a_v_down"].rearrange("(q p) n -> p q n", p=P), f"lora_in{l}")
                    load(vup, A["a_v_up"], f"lora_in{l}")
                DB.was_read(pool, (("mix_in", l), 10))
                pool.memset(up[:, :, 0:16], 0.0)
                pool.tensor_copy(up[:, :, 16:16 + T], pb[:, 19:21, :])
                pool.drain()
                src, start = up, 0
                for step, dst in ((1, wa), (2, wb), (4, wa), (8, wb)):
                    start += step
                    pool.tensor_tensor(dst[:, :, start:], src[:, :, start:], src[:, :, start - step:16 + T - step], ALU.add)
                    pool.drain()
                    tile, half = ((0, 0), (0, 1), (1, 0), (1, 1))[int(math.log2(step))]
                    r = slice(64 * half, 64 * half + 64)
                    inv_n = con[r, CCOL["invcnt"] + tile * T:CCOL["invcnt"] + (tile + 1) * T]
                    pool.tensor_tensor(sq[r, 6 + tile, :], dst[r, tile, 16:16 + T], inv_n, ALU.mult)
                    pool.drain()
                    src = dst
                pool.drain()
                pool.tensor_tensor(up[:, :, 16:16 + T], sq[:, 6:8, :], up[:, :, 16:16 + T], ALU.subtract)
                pool.drain().then_inc(S("pooled"), 1)
                pool.memset(MT, 0.0)
                pool.drain().then_inc(S("mt_zero"), 1)
                v_, vf = ts[:, 6:9, :], v_first[:, :, :]
                pool.wait_ge(S("kk_raw"), l + 1)
                if l:
                    XB.was_read(pool, ("vup", l, 1))
                    pool.tensor_tensor(vf, vf, v_, ALU.subtract)
                    pool.drain()
                    pool.tensor_tensor(vf, vf, yy, ALU.mult)
                    pool.drain()
                    pool.tensor_tensor(v_, v_, vf, ALU.add)
                else:
                    pool.tensor_copy(vf, v_)
                pool.drain().then_inc(S("v_made"), 1)
                XB.was_read(pool, ("RY", l, 1, HP - 1))
                load(memT[:, :, :], A["memT"].rearrange("(k p) t -> p k t", p=P), "mem_in")

        @block.sync
        def _(sp):
            def slot(n, src, words=SLOT):
                if n >= RING:
                    sp.wait_ge(lo_cut, 2 * (n - RING + 1))
                sp.dma_start(ring[n % RING][:, 0:words], src).then_inc(land[n % RING], 16)

            sp.dma_start(x[:, :, :], A["xT"].rearrange("(k p) t -> p k t", p=P)).then_inc(S("x_in"), 16)
            sp.dma_start(con[:, :], A["consts"]).then_inc(S("con_in"), 16)
            sp.dma_start(par[:, :], A["params"]).then_inc(S("par_in"), 16)
            for n, (_, _, name, i) in enumerate(plan):
                slot(n, A[name][i])

            def expert_slot(s, e):
                e8, t = 8 * e + 8 * (s // ESLOTS), s % ESLOTS
                if t < 16:
                    src = A["w_gate" if t < 8 else "w_up"][bass.ds(e8 + t % 8, 1), :, :]
                    src = src.rearrange("a p c -> (a p) c")
                    dst = e_ring[t % ERING]
                else:
                    src = A["w_down"][bass.ds(e8 + t - 16, 1), :, :, :].rearrange("a i p c -> p (a i) c")
                    dst = e_ring[t % ERING].rearrange("p (i c) -> p i c", i=2)
                sp.dma_start(dst, src).then_inc(e_land[t % ERING], 16)

            for s in range(ERING):
                if s < RING:
                    sp.wait_ge(lo_cut, 2 * (MOE - RING + s + 1))
                elif s < 8:
                    sp.wait_ge(slots_done, MOE - 1 if s < 6 else MOE)
                expert_slot(s, 0)
            with sp.Fori(0, EXPERTS - 1) as e:
                for s in range(ERING, ESLOTS + ERING):
                    sp.wait_ge(slots_done, ESLOTS * e + (MOE + s - ERING + 1))
                    expert_slot(s, e)
            for s in range(ERING, ESLOTS):
                sp.wait_ge(slots_done, ESLOTS * (EXPERTS - 1) + MOE + s - ERING + 1)
                expert_slot(s, EXPERTS - 1)
            for m, (_, _, name, (l, i)) in enumerate(after):
                n = AFTER + m
                if m < RING:
                    sp.wait_ge(slots_done, n - ERING + 1)
                else:
                    sp.wait_ge(lo_cut, 2 * (dense_at[n - RING] + 1))
                src, words = A[name][l, i], SLOT
                dst = ring[n % RING][:, :]
                if name.endswith("_wo") and name.startswith("ffn"):
                    src = src.rearrange("i p c -> p i c")
                    dst = dst.rearrange("p (i c) -> p i c", i=2)
                elif name == "mix_in" and i == 10:
                    src, dst = src[:, 0:KD * P], dst[:, 0:KD * P]
                sp.dma_start(dst, src).then_inc(land[n % RING], 16)
            x_made(sp, "ffn2", LAYERS - 1, 3)
            sp.dma_start(out.rearrange("(k p) t -> p k t", p=P), x[:, :, :]).then_inc(S("out_stored"), 16)
            sp.wait_ge(S("out_stored"), 16)


def kernel(**inputs):
    import concourse.bacc as bacc
    from concourse.bass_utils import run_bass_kernel_spmd

    a = {k: np.asarray(v) for k, v in inputs.items()}

    def tiles(w):
        f = w.shape[1] // 256
        return np.ascontiguousarray(w.reshape(KD, P, f, 256).transpose(2, 1, 0, 3)).reshape(f, P, SLOT)

    def columns(v, n):
        v = v.reshape(-1)
        v = np.concatenate([v.reshape(-1, 64)] * 2, axis=1).reshape(-1, P) if v.size in (64, 128) and n * P > v.size \
            else v.reshape(-1, P)
        assert v.shape[0] == n
        return v.T

    PCOL, npc = param_columns()
    params = np.zeros((P, npc), np.float32)
    order = sorted(PCOL, key=PCOL.get)
    for name, nxt in zip(order, order[1:] + [None]):
        n = (PCOL[nxt] if nxt else npc) - PCOL[name]
        if name in a:
            v = a[name]
        elif name == "a_v0":
            v = a["a_v0_2"]
        else:
            v = a[name[:-1] + "_2"][int(name[-1])]
        params[:, PCOL[name]:PCOL[name] + n] = columns(v, n)

    bd = np.zeros((2, 64, 2, 2, KD, 2, 64), np.float32)
    pw = np.zeros((LAYERS, 2, 64, 2, 2, 64), np.float32)
    for half in range(2):
        for kind, name in enumerate(("lru_w_r", "lru_w_i")):
            w = a[name][0].reshape(2, KD, 2, 64, 64)[:, :, half]
            bd[half, :, :, kind, :, half, :] = w.transpose(2, 0, 1, 3)
        pw[:, half, :, :, half, :] = a["c_pool_w_2"].reshape(LAYERS, 2, 2, 64, 64)[:, :, half].transpose(0, 2, 1, 3)

    i, j = np.arange(T)[:, None], np.arange(T)[None, :]
    rel = a["b_rel_bias_2"][:, :, np.clip(i - j, -63, 256) + 63]
    rel = np.where((i // 64 >= j // 64)[None, None], rel, np.float32(-1e30))
    rel = np.concatenate([rel[:, :, 0:P, 0:P], rel[:, :, P:T, :]], axis=3).transpose(0, 2, 1, 3)

    feed = {
        "xT": a["x"][0].T, "memT": a["mem_2"][0].T, "params": params,
        "w_in": tiles(a["w_in"][0]), "w_a_out": tiles(a["w_a_out"][0]), "w_b_out": tiles(a["w_b_out"][0]),
        "w_o": tiles(a["w_o"][0]),
        "lru_bd": bd.reshape(P, -1), "filt_w1": a["filt_w1"][0], "filt_w2": a["filt_w2"][0],
        "filt_w3": a["filt_w3"][0], "filt_bias": a["filt_bias"].reshape(1, 2 * D),
        "w_router": a["w_router"][0],
        "w_gate": a["w_gate"].reshape(EXPERTS * KD, P, FE), "w_up": a["w_up"].reshape(EXPERTS * KD, P, FE),
        "w_down": a["w_down"].reshape(EXPERTS * 8, 2, P, D),
        "mix_in": np.stack([np.concatenate(
            [tiles(w[:, 0:2560]), np.pad(w[:, 2560:].reshape(KD, P, P).transpose(1, 0, 2).reshape(1, P, KD * P),
                                         ((0, 0), (0, 0), (0, SLOT - KD * P)))]) for w in a["w_in_2"]]),
        "mix_out": np.stack([tiles(w) for w in a["w_out_2"]]),
        "x_wkv": np.stack([tiles(w) for w in a["x_wkv_2"]]),
        "x_wq": np.stack([tiles(w) for w in a["x_wq_2"]]),
        "x_wo": np.stack([tiles(w) for w in a["x_wo_2"]]),
        "rel_bias": rel.reshape(LAYERS, P, 6 * 384), "pool_w": pw.reshape(LAYERS, P, 2 * P),
        "lora_up": np.concatenate([a["a_w_up_2"], a["a_a_up_2"], a["a_g_up_2"]], axis=1),
        "a_v_down": a["a_v_down_2"][0], "a_v_up": a["a_v_up_2"][0],
    }
    for which in ("ffn1", "ffn2"):
        feed[f"{which}_wi"] = np.stack([tiles(w) for w in a[f"{which}_wi_2"]])
        feed[f"{which}_wo"] = a[f"{which}_wo_2"].reshape(LAYERS, FSTEPS, 2, P, D)
    feed.update(constants())

    nc = bacc.Bacc("TRN2", target_bir_lowering=False, num_devices=1)
    A, arrays = {}, {}
    for name, v in feed.items():
        arrays[f"in_{name}"] = np.ascontiguousarray(v)
        A[name] = nc.dram_tensor(f"in_{name}", v.shape, F32, kind="ExternalInput").ap()
    out = nc.dram_tensor("out_x", (D, T), F32, kind="ExternalOutput").ap()
    program(nc, A, out)
    r = run_bass_kernel_spmd(nc, [arrays], core_ids=[0])
    return np.ascontiguousarray(r.results[0]["out_x"].T)[None]
```
